# Optimizing a Trainium2 kernel written in Bass

```python
import math
import jax, jax.numpy as jnp
from jax import lax
import numpy as np

D_MODEL = 1024
BATCH = 1
SEQ = 512
DEPTH = 1

BRANCH_WIDTH = D_MODEL // 2
A_DK = 64
A_DV = 2 * A_DK
A_HEADS = BRANCH_WIDTH // A_DV
A_QK = A_HEADS * 2 * A_DK
B_DK = 64
B_DV = 64
B_HEADS = BRANCH_WIDTH // B_DV
B_GROUPS = 2
B_HPG = B_HEADS // B_GROUPS
CMP_LEN = 32
CMP_STRIDE = 16
SLC_LEN = 64
SLC_TOPK = 16
WIN = 512
PHI_HIDDEN = 256
N_NSA_BRANCH = 3
C_WIDTH = BRANCH_WIDTH
C_WINDOWS = (2, 4, 8, 16)
C_GROUPS = len(C_WINDOWS)
C_GDIM = C_WIDTH // C_GROUPS
N_BRANCH = 3

Q_BLOCK = 128
EPS = 1e-6
NEG_INF = -1e30
BIG = 1e30

SPLIT_SIZES = (A_QK, A_QK, BRANCH_WIDTH, BRANCH_WIDTH,
               B_HEADS * B_DK, N_NSA_BRANCH * 2 * B_GROUPS * B_DK,
               B_HEADS * N_NSA_BRANCH, BRANCH_WIDTH,
               C_WIDTH, C_WIDTH,
               N_BRANCH * D_MODEL)
N_IN = sum(SPLIT_SIZES)

kernel_name = 'hybrid_diff_nsa_pool_block'

def rms_norm(x, g):
    xf = x.astype(jnp.float32)
    y = xf * lax.rsqrt(jnp.mean(xf * xf, axis=-1, keepdims=True) + EPS)
    return (y * g.astype(jnp.float32)).astype(x.dtype)

def diff_attention(q, k, v, lam):
    Bn, H, _, S, dk = q.shape
    dv = v.shape[-1]
    scale = dk ** -0.5
    key_pos = jnp.arange(S)

    def block(i):
        q0 = i * Q_BLOCK
        qb = lax.dynamic_slice_in_dim(q, q0, Q_BLOCK, axis=3)
        sc = jnp.einsum('bhmqd,bhmkd->bhmqk', qb, k).astype(jnp.float32) * scale
        qpos = q0 + jnp.arange(Q_BLOCK)
        mask = key_pos[None, :] <= qpos[:, None]
        p = jax.nn.softmax(jnp.where(mask, sc, NEG_INF), axis=-1)
        w = p[:, :, 0] - lam * p[:, :, 1]
        return jnp.einsum('bhqk,bhkd->bhqd', w.astype(v.dtype), v)

    out = lax.map(block, jnp.arange(S // Q_BLOCK))
    return out.transpose(1, 2, 0, 3, 4).reshape(Bn, H, S, dv)

def compress_blocks(kv, pos, w1, w2):
    S, d = kv.shape[2], kv.shape[3]
    nc = (S - CMP_LEN) // CMP_STRIDE + 1
    idx = np.arange(nc)[:, None] * CMP_STRIDE + np.arange(CMP_LEN)[None, :]
    blocks = kv[:, :, idx] + pos
    flat = blocks.reshape(blocks.shape[0], blocks.shape[1], nc, CMP_LEN * d)
    return jax.nn.silu(flat @ w1) @ w2

def overlap_matrix(S):
    nc = (S - CMP_LEN) // CMP_STRIDE + 1
    ns = S // SLC_LEN
    cs = np.arange(nc) * CMP_STRIDE
    ce = cs + CMP_LEN
    ss = np.arange(ns) * SLC_LEN
    se = ss + SLC_LEN
    ov = np.clip(np.minimum(ce[:, None], se[None, :]) - np.maximum(cs[:, None], ss[None, :]), 0, None)
    return jnp.asarray(ov / CMP_LEN, dtype=jnp.float32)

def nsa_attention(q, k_cmp, v_cmp, k_slc, v_slc, k_win_pad, v_win_pad, gates):
    Bn, G, Hg, S, dk = q.shape
    nc = k_cmp.shape[2]
    ns = k_slc.shape[2]
    topk = min(SLC_TOPK, ns)
    scale = dk ** -0.5
    ov = overlap_matrix(S)
    cmp_end = jnp.arange(nc) * CMP_STRIDE + CMP_LEN - 1
    blk = jnp.arange(ns)
    bi = jnp.arange(Bn)[:, None, None, None]
    gi = jnp.arange(G)[None, :, None, None]

    def block(i):
        q0 = i * Q_BLOCK
        qb = lax.dynamic_slice_in_dim(q, q0, Q_BLOCK, axis=3)
        gb = lax.dynamic_slice_in_dim(gates, q0, Q_BLOCK, axis=3)
        qpos = q0 + jnp.arange(Q_BLOCK)
        sc = jnp.einsum('bghqd,bgnd->bghqn', qb, k_cmp).astype(jnp.float32) * scale
        cmask = cmp_end[None, :] <= qpos[:, None]
        has_cmp = jnp.any(cmask, axis=-1)[:, None].astype(jnp.float32)
        p_cmp = jax.nn.softmax(jnp.where(cmask, sc, NEG_INF), axis=-1) * has_cmp
        o_cmp = jnp.einsum('bghqn,bgnd->bghqd', p_cmp.astype(v_cmp.dtype), v_cmp)
        imp = jnp.einsum('bghqn,ns->bgqs', p_cmp, ov)
        cur = (qpos // SLC_LEN)[:, None]
        forced = (blk[None, :] == 0) | (blk[None, :] == cur) | (blk[None, :] == cur - 1)
        imp = jnp.where(forced, BIG, imp)
        imp = jnp.where(blk[None, :] > cur, NEG_INF, imp)
        _, idx = lax.top_k(imp, topk)
        kb = k_slc[bi, gi, idx]
        vb = v_slc[bi, gi, idx]
        tok = idx[..., None] * SLC_LEN + jnp.arange(SLC_LEN)
        smask = (tok <= qpos[:, None, None])[:, :, None]
        ss = jnp.einsum('bghqd,bgqnld->bghqnl', qb, kb).astype(jnp.float32) * scale
        ss = jnp.where(smask, ss, NEG_INF)
        ps = jax.nn.softmax(ss.reshape(ss.shape[:4] + (-1,)), axis=-1).reshape(ss.shape)
        o_slc = jnp.einsum('bghqnl,bgqnld->bghqd', ps.astype(vb.dtype), vb)
        kw = lax.dynamic_slice_in_dim(k_win_pad, q0, Q_BLOCK + WIN, axis=2)
        vw = lax.dynamic_slice_in_dim(v_win_pad, q0, Q_BLOCK + WIN, axis=2)
        kpos = q0 - WIN + jnp.arange(Q_BLOCK + WIN)
        wmask = ((kpos[None, :] <= qpos[:, None]) & (kpos[None, :] > qpos[:, None] - WIN)
                 & (kpos[None, :] >= 0))
        sw = jnp.einsum('bghqd,bgkd->bghqk', qb, kw).astype(jnp.float32) * scale
        pw = jax.nn.softmax(jnp.where(wmask, sw, NEG_INF), axis=-1)
        o_win = jnp.einsum('bghqk,bgkd->bghqd', pw.astype(vw.dtype), vw)
        return gb[..., 0:1] * o_cmp + gb[..., 1:2] * o_slc + gb[..., 2:3] * o_win

    out = lax.map(block, jnp.arange(S // Q_BLOCK))
    return out.transpose(1, 2, 3, 0, 4, 5).reshape(Bn, G, Hg, S, -1)

def pool_mixer(u, w_grp, scale):
    Bn, S, C = u.shape
    ug = u.reshape(Bn, S, C_GROUPS, C_GDIM).astype(jnp.float32)
    cs = jnp.pad(jnp.cumsum(ug, axis=1), ((0, 0), (1, 0), (0, 0), (0, 0)))
    t = jnp.arange(S)
    means = []
    for g, w in enumerate(C_WINDOWS):
        start = jnp.maximum(t + 1 - w, 0)
        cnt = (t + 1 - start).astype(jnp.float32)
        means.append((cs[:, 1:, g] - cs[:, start, g]) / cnt[None, :, None])
    pooled = (jnp.stack(means, axis=2) - ug).astype(u.dtype)
    y = jnp.einsum('bsgc,gcd->bsgd', pooled, w_grp)
    return y.reshape(Bn, S, C) * scale

def setup_inputs(seed: int = 0) -> dict:
    key = jax.random.key(seed)
    ks = jax.random.split(key, 20)
    L, D = DEPTH, D_MODEL
    nrm = lambda k, shape, s: jax.random.normal(k, shape, jnp.float32) * s
    return {
        'x': nrm(ks[0], (BATCH, SEQ, D), 1.0),
        'norm_g': 1.0 + nrm(ks[1], (L, D), 0.1),
        'w_in': nrm(ks[2], (L, D, N_IN), D ** -0.5),
        'a_q_g': 1.0 + nrm(ks[3], (L, A_DK), 0.1),
        'a_k_g': 1.0 + nrm(ks[4], (L, A_DK), 0.1),
        'a_lam': nrm(ks[5], (L, 4, A_DK), 0.1),
        'a_subln_g': 1.0 + nrm(ks[6], (L, A_DV), 0.1),
        'b_q_g': 1.0 + nrm(ks[7], (L, B_DK), 0.1),
        'b_k_g': 1.0 + nrm(ks[8], (L, N_NSA_BRANCH, B_DK), 0.1),
        'b_cmp_pos': nrm(ks[9], (L, 2, CMP_LEN, B_DK), 0.1),
        'b_phi_w1': nrm(ks[10], (L, 2, CMP_LEN * B_DK, PHI_HIDDEN), (CMP_LEN * B_DK) ** -0.5),
        'b_phi_w2': nrm(ks[11], (L, 2, PHI_HIDDEN, B_DK), PHI_HIDDEN ** -0.5),
        'c_w': nrm(ks[12], (L, C_GROUPS, C_GDIM, C_GDIM), C_GDIM ** -0.5),
        'c_scale': 1.0 + nrm(ks[13], (L, C_WIDTH), 0.1),
        'w_branch': nrm(ks[14], (L, N_BRANCH, BRANCH_WIDTH, D), BRANCH_WIDTH ** -0.5),
        'w_out': nrm(ks[15], (L, D, D), D ** -0.5),
    }

def reference(x, norm_g, w_in, a_q_g, a_k_g, a_lam, a_subln_g, b_q_g, b_k_g, b_cmp_pos,
              b_phi_w1, b_phi_w2, c_w, c_scale, w_branch, w_out):
    Bn, S, D = x.shape
    split_at = [int(v) for v in np.cumsum(SPLIT_SIZES)[:-1]]
    for l in range(DEPTH):
        h = rms_norm(x, norm_g[l])
        z = h @ w_in[l]
        aq, ak, av, ag, bq, bkv, bbg, bg, cu, cg, mg = jnp.split(z, split_at, axis=-1)

        qa = rms_norm(aq.reshape(Bn, S, A_HEADS, 2, A_DK), a_q_g[l]).transpose(0, 2, 3, 1, 4)
        ka = rms_norm(ak.reshape(Bn, S, A_HEADS, 2, A_DK), a_k_g[l]).transpose(0, 2, 3, 1, 4)
        va = av.reshape(Bn, S, A_HEADS, A_DV).transpose(0, 2, 1, 3)
        lam_init = 0.8 - 0.6 * math.exp(-0.3 * l)
        lp = a_lam[l].astype(jnp.float32)
        lam = jnp.exp(jnp.sum(lp[0] * lp[1])) - jnp.exp(jnp.sum(lp[2] * lp[3])) + lam_init
        oa = diff_attention(qa, ka, va, lam).transpose(0, 2, 1, 3)
        oa = (rms_norm(oa, a_subln_g[l]) * (1.0 - lam_init)).reshape(Bn, S, BRANCH_WIDTH)
        ya = (oa * jax.nn.silu(ag)) @ w_branch[l, 0]

        qb = rms_norm(bq.reshape(Bn, S, B_GROUPS, B_HPG, B_DK), b_q_g[l]).transpose(0, 2, 3, 1, 4)
        kv = bkv.reshape(Bn, S, N_NSA_BRANCH, 2, B_GROUPS, B_DK).transpose(2, 3, 0, 4, 1, 5)
        gates = jax.nn.sigmoid(bbg.reshape(Bn, S, B_GROUPS, B_HPG, N_NSA_BRANCH)).transpose(0, 2, 3, 1, 4)
        k_cmp = rms_norm(compress_blocks(kv[0, 0], b_cmp_pos[l, 0], b_phi_w1[l, 0], b_phi_w2[l, 0]), b_k_g[l, 0])
        v_cmp = compress_blocks(kv[0, 1], b_cmp_pos[l, 1], b_phi_w1[l, 1], b_phi_w2[l, 1])
        ns = S // SLC_LEN
        k_slc = rms_norm(kv[1, 0], b_k_g[l, 1]).reshape(Bn, B_GROUPS, ns, SLC_LEN, B_DK)
        v_slc = kv[1, 1].reshape(Bn, B_GROUPS, ns, SLC_LEN, B_DV)
        pad = ((0, 0), (0, 0), (WIN, 0), (0, 0))
        k_win = jnp.pad(rms_norm(kv[2, 0], b_k_g[l, 2]), pad)
        v_win = jnp.pad(kv[2, 1], pad)
        ob = nsa_attention(qb, k_cmp, v_cmp, k_slc, v_slc, k_win, v_win, gates)
        ob = ob.transpose(0, 3, 1, 2, 4).reshape(Bn, S, BRANCH_WIDTH)
        yb = (ob * jax.nn.silu(bg)) @ w_branch[l, 1]

        oc = pool_mixer(cu, c_w[l], c_scale[l])
        yc = (oc * jax.nn.silu(cg)) @ w_branch[l, 2]

        g = jax.nn.sigmoid(mg.reshape(Bn, S, N_BRANCH, D))
        merged = g[:, :, 0] * ya + g[:, :, 1] * yb + g[:, :, 2] * yc
        x = x + merged @ w_out[l]
    return x


_drawn_inputs = setup_inputs


def setup_inputs(seed=0):
    import zlib

    import numpy as np

    out = dict(_drawn_inputs(seed))
    spreads = {}
    factors = {'a_lam': 17.954, 'b_q_g': 8.0, 'b_k_g': 8.0, 'b_cmp_pos': 6.185, 'a_k_g': 2.889}
    for name, (base, spread) in spreads.items():
        noise = np.random.default_rng([zlib.crc32(name.encode()), seed]).standard_normal(out[name].shape)
        drawn = base * np.exp(spread * noise) if base else spread * noise
        out[name] = __import__('jax').numpy.asarray(drawn.astype(out[name].dtype))
    for name, factor in factors.items():
        out[name] = (out[name] * factor).astype(out[name].dtype)
    return out
```

```python
import math
from contextlib import ExitStack

import concourse.bass as bass
from concourse import mybir


def hybrid_trunk_kernel(nc: bass.Bass, x, norm_g, w_in, a_q_g, a_k_g, a_lam, a_subln_g, b_q_g, b_k_g,
                        b_cmp_pos, b_phi_w1, b_phi_w2, c_w, c_scale, w_branch, w_out, out):
    F32, F32R, BF16 = mybir.dt.float32, mybir.dt.float32r, mybir.dt.bfloat16
    ALU, ACT, AX = mybir.AluOpType, mybir.ActivationFunctionType, mybir.AxisListType
    P = 128
    _, SEQ, D = x.shape
    EPS, NEG = 1e-6, -1e30
    NT = SEQ // P
    NK = D // P
    BW = w_branch.shape[2]
    NF = BW // P
    DK = a_q_g.shape[1]
    AH = BW // (2 * DK)
    BH = BW // DK
    G = 2
    HPG = BH // G
    CMP_LEN, CMP_STRIDE = b_cmp_pos.shape[2], 16
    NCMP = (SEQ - CMP_LEN) // CMP_STRIDE + 1
    CP = 32
    LP = CMP_LEN // 2
    HID = b_phi_w1.shape[3]
    NH2 = HID // P
    LAM_INIT = 0.8 - 0.6 * math.exp(-0.3 * 0)

    C_AQ, C_AK, C_AV, C_AG = 0, BW, 2 * BW, 3 * BW
    C_BQ = 4 * BW
    C_KV = 5 * BW
    C_CMP, C_SW = C_KV, C_KV + 4 * DK
    C_BBG = C_KV + 12 * DK
    NG = 3 * BH
    C_BG = C_BBG + NG
    C_CU, C_CG = C_BG + BW, C_BG + 2 * BW
    C_MG = C_BG + 3 * BW

    win_k = w_in[0].rearrange("(k p) n -> p k n", p=P)
    wout_k = w_out[0].rearrange("(k p) n -> p k n", p=P)
    wbr_k = [w_branch[0, b].rearrange("(k p) n -> p k n", p=P) for b in range(3)]
    w1_k = [b_phi_w1[0, c].rearrange("(l p) n -> p l n", p=P) for c in range(2)]
    HK = NK // 2
    SLOT = HK * BW
    items = []

    def add(name, view, kt, cols, split=True):
        items.append((name, view, kt, cols, split))

    def add_halves(name, view, c0, cols):
        for half in range(2):
            add(f"{name}{half}", view[:, half * HK:(half + 1) * HK, c0:c0 + cols], HK, cols)

    add_halves("aq", win_k, C_AQ, BW)
    add_halves("ak", win_k, C_AK, BW)
    add_halves("av", win_k, C_AV, BW)
    add("cmp", win_k[:, :, C_CMP:C_CMP + 4 * DK], NK, 4 * DK)
    add_halves("bq", win_k, C_BQ, BW)
    add_halves("sw", win_k, C_SW, 8 * DK)
    for c in range(2):
        for half in range(2):
            add(f"phi{c}{half}", w1_k[c][:, half * (LP // 2):(half + 1) * (LP // 2), :], LP // 2, HID, False)
    add("bbg", win_k[:, :, C_BBG:C_BBG + NG], NK, NG)
    add_halves("cu", win_k, C_CU, BW)
    add_halves("ag", win_k, C_AG, BW)
    add("cw", c_w[0].rearrange("g c d -> c g d"), NF, P, False)
    add_halves("bg", win_k, C_BG, BW)
    add_halves("cg", win_k, C_CG, BW)
    PC = 2 * P
    NP = D // PC
    for pr in range(NP):
        for b in range(3):
            add(f"mg{pr}{b}", win_k[:, :, C_MG + b * D + pr * PC:C_MG + b * D + (pr + 1) * PC], NK, PC)
            add(f"wb{pr}{b}", wbr_k[b][:, :, pr * PC:(pr + 1) * PC], NF, PC)
    for c in range(2):
        add_halves(f"wo{c}", wout_k, c * BW, BW)
    NAMES = [i[0] for i in items]
    SPLIT = [n for n, i in enumerate(items) if i[4]]
    WHOLE = [n for n, i in enumerate(items) if not i[4]]
    NRAW, NSPL = 3, 2

    units = []
    for h in range(AH):
        units += [("A", h, t, m) for t in range(NT) for m in range(2)]
    for h in range(BH):
        units += [("C", h, 0, 0)] + [("B", h, t, m) for m in range(2) for t in range(NT)]
    NU = len(units)
    jobs = [u for u, (kind, _, _, m) in enumerate(units) if kind != "A" or m == 1]
    job_of = {u: j for j, u in enumerate(jobs)}
    NHEAD = AH + BH
    head_of = [h if kind == "A" else AH + h for kind, h, _, _ in units]
    first_u = [head_of.index(i) for i in range(NHEAD)]
    last_u = [NU - 1 - head_of[::-1].index(i) for i in range(NHEAD)]
    LT, LV, LF = 2, 3, 4
    NSTEP = NU + LF + 4

    first_pv = [next(u for u in jobs if head_of[u] == i and units[u][0] != "C") for i in range(NHEAD)]

    def jobs_until(u):
        return sum(1 for j in jobs if j <= u)

    hls, head_hl = [], {}
    for i in range(NHEAD):
        if i < AH:
            mine = [("q", i, 0), ("k", i, 0), ("q", i, 1), ("k", i, 1)]
        else:
            mine = [("q", i, 0)]
            if (i - AH) % HPG == 0:
                mine += [("k", i, 0), ("k", i, 1)]
        head_hl[i] = list(range(len(hls), len(hls) + len(mine)))
        hls += mine
    trs = {s: [] for s in range(-1, NSTEP)}
    trs[-1] += [("kc", 0), ("kc", 1)]

    def prep(i):
        r = []
        for k in head_hl[i]:
            r += [("q", k)] if hls[k][0] == "q" else [("kh", k), ("kl", k)]
        return r
    trs[-1] += prep(0)
    for i in range(1, NHEAD):
        for n, r in enumerate(prep(i)):
            trs[first_u[i - 1] + 1 + n].append(r)
    for u, (kind, h, _, _) in enumerate(units):
        if kind == "C":
            trs[u + LV].append(("oc", u))
    for i in range(NHEAD):
        if i < AH or (i - AH) % 2:
            trs[last_u[i] + LF + 3].append(("fin", i))
    tr_list = [(s, r) for s in trs for r in trs[s]]
    NTR = len(tr_list)

    def tr_no(r):
        return next(n for n, (_, q) in enumerate(tr_list) if q == r)
    hl_last_tr = [tr_no(("q", k)) if hls[k][0] == "q" else tr_no(("kl", k)) for k in range(len(hls))]

    ctx = ExitStack()
    with ctx:
        def sem(name):
            return ctx.enter_context(nc.semaphore(name))

        def sb(name, shape, dt, c=ctx):
            return c.enter_context(nc.sbuf_tensor(name, shape, dt))

        h_hi = sb("h_hi", [P, NK, SEQ], F32R)
        h_lo = sb("h_lo", [P, NK, SEQ], F32R)
        raw = sb("raw", [P, NRAW, SLOT], F32)
        w_hi = sb("w_hi", [P, NSPL, SLOT], F32R)
        w_lo = sb("w_lo", [P, NSPL, SLOT], F32R)
        U = sb("U", [P, 3 * NF, SEQ], F32)
        ident = sb("ident", [P, P], F32)
        identb = sb("identb", [P, P], BF16)
        causal = sb("causal", [P, P], BF16)
        cmask = sb("cmask", [P, NT * CP], BF16)
        gains = sb("gains", [P, 6, DK], F32)
        subln = sb("subln", [P, 2 * DK], F32)
        cols = sb("cols", [P, NF + 2 * LP], F32)
        w2 = sb("w2", [P, 2, NH2, DK], F32)
        Vbd = sb("Vbd", [P, G, NT * DK], F32)
        KC = sb("KC", [P, 2, G * CP], F32R)
        gates = sb("gates", [P, NT, NG], F32)
        st = sb("st", [P, 256], F32)
        half_pow = sb("half_pow", [P, 32], F32)
        inv_cnt = sb("inv_cnt", [P, 16], F32)
        has_cmp = sb("has_cmp", [P, 1], F32)

        early = ExitStack()
        tok = sb("tok", [P, 5 * NT * BW], F32, early)
        QS = sb("QS", [P, 4, SEQ], F32R, early)
        KS = sb("KS", [P, 8, SEQ], F32R, early)
        PTs = sb("PTs", [P, 2, SEQ], F32, early)
        HL = sb("HL", [P, 2, NT, 3, DK], F32R, early)
        OF = sb("OF", [P, 2, NT, P], F32, early)
        TMP = sb("TMP", [P, NT, DK], F32, early)
        TMP2 = sb("TMP2", [P, P], F32, early)
        OC = sb("OC", [P, 2, NT, DK], F32, early)
        mtmp = sb("mtmp", [P, P], F32, early)
        lamv = sb("lamv", [P, 4, DK], F32, early)
        rows = sb("rows", [NF + 2 * LP, P], F32, early)
        kchl = sb("kchl", [P, 3, DK], F32R, early)
        kcn = sb("kcn", [P, DK], F32, early)
        early.close()
        o_hi = sb("o_hi", [P, 3 * NF, SEQ], F32R)
        o_lo = sb("o_lo", [P, 3 * NF, SEQ], F32R)
        M_hi = sb("M_hi", [P, NK, SEQ], F32R)
        M_lo = sb("M_lo", [P, NK, SEQ], F32R)
        PADL = 16
        work = sb("work", [P, 3 * (PADL + SEQ)], F32)
        rowA, rowB, rowC = (work[:, i * (PADL + SEQ):(i + 1) * (PADL + SEQ)] for i in range(3))
        gt = work[:, 0:2 * SEQ].rearrange("p (a s) -> p a s", a=2)
        acc = U[:, 0:2, :].rearrange("p a s -> p (a s)")
        sg = U[:, 2:6, :].rearrange("p (b a) s -> p b (a s)", b=2)
        xres = [U[:, 8:12, :], U[:, 4:8, :]]

        def region(a, n):
            return tok[:, a * NT * BW // 2:(a + n) * NT * BW // 2]
        qA = region(0, 2).rearrange("p (t n) -> p t n", t=NT)
        kA = region(2, 2).rearrange("p (t n) -> p t n", t=NT)
        vA = region(4, 2).rearrange("p (t n) -> p t n", t=NT)
        qB = region(6, 2).rearrange("p (t n) -> p t n", t=NT)
        kB = region(8, 1).rearrange("p (t n) -> p t n", t=NT)
        vB = region(9, 1).rearrange("p (t n) -> p t n", t=NT)
        gB = tok[:, 0:D]
        xt = region(4, 4).rearrange("p (t n) -> p t n", t=NT)
        T2 = U[:, 0:4, :].rearrange("p (c g) s -> p c g s", c=2)
        X = U[:, 4:8, :].rearrange("p c s -> p (c s)").rearrange("p (c l g b) -> p c l g b", c=2, l=LP, g=G)
        Pr = U[:, 8:12, :]
        sq = Pr
        HTk = PTs[:, :, :].rearrange("p a s -> p (a s)")[:, 0:NH2 * P].rearrange("p (n r c) -> p n r c", n=NH2, r=2)
        HTv = PTs[:, :, :].rearrange("p a s -> p (a s)")[:, NH2 * P:3 * NH2 * P]\
            .rearrange("p (n g r b) -> p n g r b", n=NH2, g=G, r=4)
        PS = ctx.enter_context(nc.psum_tensor("PS", [P, 8, 512], F32))
        B_S, B_PT, B_TR, B_O = 0, 3, 5, 6

        ssx, rsx = st[:, 0:4], st[:, 4:8]
        ssn, rsn = st[:, 8:40], st[:, 40:72]
        sskc, rskc = st[:, 72:73], st[:, 73:74]
        lam2, lame, nlam = st[:, 74:76], st[:, 76:78], st[:, 78:79]
        negmax = st[:, 80:88]
        rowsum = st[:, 88:104]
        recip = st[:, 104:120]
        nmc = st[:, 120:124]
        lc = st[:, 124:128]
        fc = st[:, 128:132]
        ssf, rsf = st[:, 132:136], st[:, 136:140]
        fB = st[:, 140:148]
        gtmp = st[:, 148:244].rearrange("p (t n) -> p t n", t=NT)

        raw_in = [sem(f"raw_in{i}") for i in range(NRAW)]
        x_in = [sem(f"x_in{i}") for i in range(NT)]
        gb_in, small_in, rows_in = sem("gb_in"), sem("small_in"), sem("rows_in")
        xres_in = [sem("xres_in0"), sem("xres_in1")]
        stored = sem("stored")
        hi_done, lo_done, split_used, whole_used = (sem(n) for n in ("hi_done", "lo_done", "split_used", "whole_used"))
        consts, maskf, maskb, ssx_done, rsx_done, xn_done = (sem(n) for n in ("consts", "maskf", "maskb", "ssx_done", "rsx_done", "xn_done"))
        xT_done, hhi_done, hlo_done, cols_tr, cols_done = (sem(n) for n in ("xT_done", "hhi_done", "hlo_done", "cols_tr", "cols_done"))
        drained = [sem("drained0"), sem("drained1")]
        sq_done, ssn_part, rsn_done = sem("sq_done"), sem("ssn_part"), sem("rsn_done")
        t2_done, x_done, ht_done, kcs_done, kcr_done, kchl_done = (sem(n) for n in ("t2_done", "x_done", "ht_done", "kcs_done", "kcr_done", "kchl_done"))
        tok_done = sem("tok_done")
        vals_done = sem("vals_done")
        gate_e, gates_done, lam_s, lam_e, lam_done, vbd_zero, xpad = (sem(n) for n in ("gate_e", "gates_done", "lam_s", "lam_e", "lam_done", "vbd_zero", "xpad"))
        hl_made, tr_made, tr_drained = sem("hl_made"), sem("tr_made"), sem("tr_drained")
        scores, maxed, exped, weighted = sem("scores"), sem("maxed"), sem("exped"), sem("weighted")
        csub, ptd, pt_out, pv_done = sem("csub"), sem("ptd"), sem("pt_out"), sem("pv_done")
        ss_f, rs_f, of_done, o_free = sem("ss_f"), sem("rs_f"), sem("of_done"), sem("o_free")
        cu_done, pooled, oc_scaled, silu_done, u_done, u_hi, u_lo = (sem(n) for n in ("cu_done", "pooled", "oc_scaled", "silu_done", "u_done", "u_hi", "u_lo"))
        sg_done, sg_used, acc_done, m_hi, m_lo, res_done = (sem(n) for n in ("sg_done", "sg_used", "acc_done", "m_hi", "m_lo", "res_done"))
        pool_zero = sem("pool_zero")
        dve_link, act_link, pool_link = sem("dve_link"), sem("act_link"), sem("pool_link")

        chunks = ["aq", "ak", "av", "cmp", "bq", "sw", "phi", "misc", "cu", "ag", "cw", "bg", "cg"]
        chunks += [f"m{pr}{b}" for pr in range(NP) for b in range(3)] + ["wo0", "wo1"]
        CH = {c: n for n, c in enumerate(chunks)}
        BEFORE = CH["cu"]

        def bank0(c):
            return 4 * (CH[c] % 2)

        def bcast(v, n):
            return bass.AP(v.tensor, v.offset, [[0, P], [1, n]])

        def item(name):
            return NAMES.index(name)

        def wait_pv(eng, j):
            if units[jobs[j]][0] == "C":
                eng.wait_ge(tr_made, tr_no(("oc", jobs[j])) + 1)
            else:
                eng.wait_ge(pv_done, sum(1 for v in jobs[:j + 1] if units[v][0] != "C"))

        def linker(eng, s):
            n = [0]

            def link(ins):
                n[0] += 1
                ins.then_inc(s, 1)
                eng.wait_ge(s, n[0])
            return link

        def wait_raw(eng, n):
            eng.wait_ge(raw_in[n % NRAW], 16 * (n // NRAW + 1))

        LAST = {"aq": "aq1", "ak": "ak1", "av": "av1", "cmp": "cmp", "bq": "bq1", "sw": "sw1", "phi": "phi11",
                "misc": "bbg", "cu": "cu1", "ag": "ag1", "cw": "cw", "bg": "bg1", "cg": "cg1", "wo0": "wo01", "wo1": "wo11"}
        LAST.update({f"m{pr}{b}": f"wb{pr}{b}" for pr in range(NP) for b in range(3)})

        def splits_through(c):
            done = sum(1 for n in SPLIT if n <= item(LAST[c]))
            beyond = {"sw": 0, "phi": 1}.get(c, NSPL)
            return min(done + beyond, len(SPLIT))

        def wait_item_used(eng, name):
            n = item(name)
            if n in SPLIT:
                eng.wait_ge(split_used, SPLIT.index(n) + 1)
            else:
                eng.wait_ge(whole_used, WHOLE.index(n) + 1)

        block = ctx.enter_context(nc.Block())

        @block.sync
        def _(sp):
            for n, (name, view, kt, ncol, split) in enumerate(items):
                if n >= NRAW:
                    if n - NRAW in SPLIT:
                        sp.wait_ge(lo_done, SPLIT.index(n - NRAW) + 1)
                    else:
                        sp.wait_ge(whole_used, WHOLE.index(n - NRAW) + 1)
                dst = raw[:, n % NRAW, 0:kt * ncol].rearrange("p (k n) -> p k n", k=kt)
                sp.dma_start(dst, view).then_inc(raw_in[n % NRAW], 16)
            for c in range(2):
                if c == 0:
                    sp.wait_ge(u_lo, 3 * NF)
                else:
                    sp.wait_ge(m_lo, NP)
                sp.dma_start(xres[c], x[0, :, c * BW:(c + 1) * BW].rearrange("(t p) n -> p t n", p=P))\
                    .then_inc(xres_in[c], 16)
            for c in range(2):
                for t in range(NT):
                    sp.wait_ge(res_done, c * NT + t + 1)
                    sp.dma_start(out[0, t * P:(t + 1) * P, c * BW:(c + 1) * BW], xres[c][:, t, :]).then_inc(stored, 16)
            sp.wait_ge(stored, 16 * 2 * NT)

        @block.gpsimd
        def _(pool):
            link = linker(pool, pool_link)
            nsplit = [0]

            def low_parts(upto):
                while nsplit[0] < upto:
                    i = nsplit[0]
                    n = SPLIT[i]
                    size = items[n][2] * items[n][3]
                    pool.wait_ge(hi_done, i + 1)
                    pool.tensor_tensor(w_lo[:, i % NSPL, 0:size], raw[:, n % NRAW, 0:size],
                                       w_hi[:, i % NSPL, 0:size].bitcast(F32), ALU.subtract).then_inc(lo_done, 1)
                    nsplit[0] += 1

            def rsqrt(dst, src, scale, add):
                link(pool.tensor_scalar(dst, src, scale, add, ALU.mult, ALU.add))
                return pool.tensor_tensor(dst, dst, half_pow[:, 0:dst.shape[1]], ALU.pow)

            link(pool.memset(ident[:, :], 0.0))
            pool.affine_select(out=ident[:, :], in_=ident[:, :], compare_op=ALU.not_equal, fill=1.0, base=0,
                               pattern=[[-1, P]], channel_multiplier=1).then_inc(consts, 1)
            pool.memset(half_pow[:, :], -0.5).then_inc(consts, 1)
            pool.wait_ge(consts, 2)
            for t in range(NT):
                pool.wait_ge(ssx_done, t + 1)
                rsqrt(rsx[:, t:t + 1], ssx[:, t:t + 1], 1.0 / D, EPS).then_inc(rsx_done, 1)
            link(pool.memset(mtmp[:, :], 0.0))
            pool.affine_select(out=mtmp[:, :], in_=mtmp[:, :], compare_op=ALU.is_ge, fill=NEG, base=0,
                               pattern=[[-1, P]], channel_multiplier=1).then_inc(maskf, 1)
            low_parts(1)
            pool.wait_ge(maskb, 1)
            link(pool.memset(mtmp[:, :], 0.0))
            pool.affine_select(out=mtmp[:, :], in_=mtmp[:, :], compare_op=ALU.is_ge, fill=NEG, base=-(CMP_LEN - 1),
                               pattern=[[P, NT], [-CMP_STRIDE, CP]], channel_multiplier=1).then_inc(maskf, 1)
            low_parts(2)
            link(pool.memset(has_cmp[:, :], 1.0))
            link(pool.affine_select(out=has_cmp[:, :], in_=has_cmp[:, :], compare_op=ALU.is_ge, fill=0.0,
                                    base=-(CMP_LEN - 1), pattern=[[0, 1]], channel_multiplier=1))
            for i in range(16):
                pool.memset(inv_cnt[:, i:i + 1], 1.0 / (i + 1))
            pool.memset(Vbd[:, :, :], 0.0).then_inc(vbd_zero, 1)
            pool.memset(X[:, :, :, :, NCMP:CP], 0.0).then_inc(xpad, 1)
            for c in chunks[:BEFORE]:
                low_parts(min(splits_through(c), sum(1 for n in SPLIT if n < item("cu0")) + NSPL))
                if c in ("aq", "ak", "bq", "sw"):
                    k = ("aq", "ak", "bq", "sw").index(c)
                    nn = {"sw": 4 * NT}.get(c, BH * NT)
                    pool.wait_ge(ssn_part, NT * (k + 1))
                    if c in ("aq", "bq"):
                        ins = rsqrt(rsn[:, 0:nn], ssn[:, 0:nn], 1.0, DK * EPS)
                    else:
                        ins = rsqrt(rsn[:, 0:nn], ssn[:, 0:nn], 1.0 / DK, EPS)
                    ins.then_inc(rsn_done, 1)
                if c == "misc":
                    pool.wait_ge(kcs_done, 1)
                    rsqrt(rskc, sskc, 1.0 / DK, EPS).then_inc(kcr_done, 1)
            pool.wait_ge(tok_done, 4)

            def make_hl(k):
                kind, i, m = hls[k]
                if i < AH:
                    src = (qA if kind == "q" else kA)[:, :, (2 * i + m) * DK:(2 * i + m + 1) * DK]
                elif kind == "q":
                    src = qB[:, :, (i - AH) * DK:(i - AH + 1) * DK]
                else:
                    g = (i - AH) // HPG
                    src = kB[:, :, (m * G + g) * DK:(m * G + g + 1) * DK]
                if k >= 2:
                    pool.wait_ge(tr_made, hl_last_tr[k - 2] + 1)
                link(pool.tensor_copy(HL[:, k % 2, :, 0, :], src))
                if kind == "k":
                    pool.tensor_copy(HL[:, k % 2, :, 2, :], src)
                pool.tensor_tensor(HL[:, k % 2, :, 1, :], src, HL[:, k % 2, :, 0, :].bitcast(F32),
                                   ALU.subtract).then_inc(hl_made, 1)
            for i in range(NHEAD):
                for n, k in enumerate(head_hl[i]):
                    make_hl(k)
                    if n == min(2, len(head_hl[i]) - 1) and 2 <= i < AH + 2:
                        pool.wait_ge(ss_f, i - 1)
                        rsqrt(rsf, ssf, 1.0 / P, EPS).then_inc(rs_f, 1)
            for c in chunks[BEFORE:]:
                low_parts(splits_through(c))

        @block.scalar
        def _(act):
            link = linker(act, act_link)
            nsplit = [0]

            def high_parts(upto):
                while nsplit[0] < upto:
                    i = nsplit[0]
                    n = SPLIT[i]
                    size = items[n][2] * items[n][3]
                    wait_raw(act, n)
                    if i >= NSPL:
                        act.wait_ge(split_used, i - NSPL + 1)
                    act.activation(w_hi[:, i % NSPL, 0:size], raw[:, n % NRAW, 0:size], ACT.Copy).then_inc(hi_done, 1)
                    nsplit[0] += 1

            for t in range(NT):
                act.dma_start(xt[:, t, :], x[0, t * P:(t + 1) * P, :]).then_inc(x_in[t], 16)
                if t == 0:
                    act.dma_start(gB, bcast(norm_g[0], D)).then_inc(gb_in, 16)
            srcs = [a_q_g[0], a_k_g[0], b_q_g[0], b_k_g[0, 0], b_k_g[0, 1], b_k_g[0, 2]]
            for i, s in enumerate(srcs):
                act.dma_start(gains[:, i, :], bcast(s, DK)).then_inc(small_in, 16)
            act.dma_start(subln[:, :], bcast(a_subln_g[0], 2 * DK)).then_inc(small_in, 16)
            act.dma_start(lamv[:, :, :], bass.AP(a_lam.tensor, 0, [[0, P], [DK, 4], [1, DK]])).then_inc(small_in, 16)
            for c in range(2):
                act.dma_start(w2[:, c, :, :], b_phi_w2[0, c].rearrange("(n p) d -> p n d", p=P)).then_inc(small_in, 16)
            act.dma_start(rows[0:NF, :], c_scale[0].rearrange("(g p) -> g p", p=P)).then_inc(rows_in, 16)
            act.dma_start(rows[NF:NF + 2 * LP, :], b_cmp_pos[0].rearrange("c (l two) d -> (c l) (two d)", two=2)).then_inc(rows_in, 16)

            for t in range(NT):
                act.wait_ge(x_in[t], 16)
                if t >= 1:
                    act.wait_ge(ssx_done, t)
                act.activation(sq[:, 0:2, :].rearrange("p a s -> p (a s)"), xt[:, t, :], ACT.Square,
                               accum_out=ssx[:, t:t + 1]).then_inc(ssx_done, 1)
            high_parts(1)
            for n in range(2 * NT):
                t, half = n // 2, n % 2
                act.wait_ge(xT_done, n + 1)
                act.activation(h_hi[:, 4 * half:4 * half + 4, t * P:(t + 1) * P],
                               PS[:, n % 8, :].rearrange("p (k s) -> p k s", k=4), ACT.Copy).then_inc(hhi_done, 1)
                if n == 3:
                    high_parts(2)
            act.wait_ge(cols_tr, 1)
            act.activation(cols[:, :], PS[:, 0, 0:NF + 2 * LP], ACT.Copy).then_inc(cols_done, 1)

            nsq = [0]

            def squares(c, groups):
                for t in range(NT):
                    if nsq[0] >= 2:
                        act.wait_ge(ssn_part, nsq[0] - 1)
                    act.activation(sq[:, nsq[0] % 2, :], PS[:, bank0(c) + t, :], ACT.Square).then_inc(sq_done, 1)
                    nsq[0] += 1

            cap = sum(1 for n in SPLIT if n < item("cu0")) + NSPL
            for c in chunks[:BEFORE]:
                high_parts(min(splits_through(c), cap))
                wait_item_used(act, "mg" + c[1:] if c[0] == "m" and c != "misc" else LAST[c])
                b0 = bank0(c)
                if c in ("aq", "ak", "bq"):
                    squares(c, BH)
                elif c == "sw":
                    squares(c, 4)
                    for t in range(NT):
                        src = PS[:, b0 + t, :].rearrange("p (s two n) -> p s two n", s=2, two=2)[:, :, 1, :]
                        ins = act.activation(vB[:, t, :].rearrange("p (s n) -> p s n", s=2), src, ACT.Copy)
                    ins.then_inc(vals_done, 1)
                elif c == "av":
                    for t in range(NT):
                        ins = act.activation(vA[:, t, :], PS[:, b0 + t, :], ACT.Copy)
                    ins.then_inc(drained[CH[c] % 2], 1)
                elif c == "cmp":
                    for kv in range(2):
                        for g in range(G):
                            src = PS[g * DK:(g + 1) * DK, b0 + kv, :]
                            act.activation(T2[0:DK, kv, g, :], src, ACT.Copy)
                            ins = act.activation(T2[DK:P, kv, g, 0:SEQ - 1], src[:, 1:SEQ], ACT.Copy)
                    ins.then_inc(t2_done, 1)
                elif c == "phi":
                    hid = PS[:, b0, 0:2 * NH2 * G * CP].rearrange("p (c n k) -> p c n k", c=2, n=NH2)
                    act.activation(HTk, hid[:, 0, :, :].unsqueeze(2).broadcast_to([P, NH2, 2, G * CP]), ACT.Silu)
                    for n in range(NH2):
                        src = hid[:, 1, n, :].rearrange("p (g b) -> p g b", g=G).unsqueeze(2).broadcast_to([P, G, 4, CP])
                        ins = act.activation(HTv[:, n], src, ACT.Silu)
                    ins.then_inc(ht_done, 1)
                    act.wait_ge(ht_done, 1)
                    act.sem_inc(drained[CH[c] % 2], 1)
                elif c == "misc":
                    act.activation(gates[:, :, :].rearrange("p t n -> p (t n)"), PS[:, b0, 0:NT * NG], ACT.Sigmoid).then_inc(gates_done, 1)
                    act.activation(kcn[:, :], PS[:, b0 + 1, 0:DK], ACT.Square, accum_out=sskc).then_inc(kcs_done, 1)
            act.wait_ge(lam_s, 1)
            act.activation(lame, lam2, ACT.Exp).then_inc(lam_e, 1)

            def drain_tr(r):
                n = tr_no(r)
                act.wait_ge(tr_made, n + 1)
                src = PS[:, B_TR, :]
                if r[0] == "kc":
                    act.activation(KC[:, r[1], :], src[:, 0:G * CP], ACT.Copy).then_inc(tr_drained, 1)
                elif r[0] == "q":
                    _, i, m = hls[r[1]]
                    act.activation(QS[:, 2 * (i % 2) + m, :], src, ACT.Copy).then_inc(tr_drained, 1)
                elif r[0] in ("kh", "kl"):
                    _, i, m = hls[r[1]]
                    par = i % 2 if i < AH else ((i - AH) // HPG) % 2
                    act.activation(KS[:, 4 * par + 2 * m + (r[0] == "kl"), :], src, ACT.Copy).then_inc(tr_drained, 1)
                elif r[0] == "oc":
                    act.activation(OC[:, units[r[1]][1] % 2, :, :].rearrange("p t d -> p (t d)"), src[:, 0:NT * DK], ACT.Copy).then_inc(tr_drained, 1)
                else:
                    i = r[1]
                    f = i if i < AH else NF + (i - AH) // 2
                    act.activation(U[:, f, :], src, ACT.Copy).then_inc(tr_drained, 1)

            for r in trs[-1]:
                drain_tr(r)
            for s in range(NSTEP):
                if s < NU:
                    kind, h, t, m = units[s]
                    if s >= 4:
                        act.wait_ge(ptd, jobs_until(s - 4) + (1 if units[s - 4][0] == "A" and units[s - 4][3] == 0 else 0))
                    if kind == "C":
                        act.wait_ge(csub, h + 1)
                        act.activation(Pr[:, s % 4, 0:P], Pr[:, s % 4, 0:P], ACT.Exp).then_inc(exped, 1)
                    else:
                        W = (t + 1) * P
                        act.wait_ge(maxed, s + 1)
                        slot = rowsum[:, s % 16:s % 16 + 1] if kind == "A" else rowsum[:, m * NT + t + 8 * (h % 2):m * NT + t + 8 * (h % 2) + 1]
                        act.activation(Pr[:, s % 4, 0:W], PS[:, B_S + s % 3, 0:W], ACT.Exp,
                                       bias=negmax[:, s % 8:s % 8 + 1], accum_out=slot).then_inc(exped, 1)
                for r in trs[s]:
                    drain_tr(r)

            nsilu = [0]
            for c in chunks[BEFORE:]:
                high_parts(splits_through(c))
                wait_item_used(act, "mg" + c[1:] if c[0] == "m" and c != "misc" else LAST[c])
                b0 = bank0(c)
                if c == "cu":
                    for g in range(NF):
                        if g >= 1:
                            act.wait_ge(pooled, g)
                        else:
                            act.wait_ge(pool_zero, 1)
                        ins = act.activation(rowA[:, 16:16 + SEQ], PS[:, b0 + g, :], ACT.Copy)
                        ins.then_inc(cu_done, 1)
                elif c == "cw":
                    act.wait_ge(cols_done, 1)
                    for g in range(NF):
                        act.activation(U[:, 2 * NF + g, :], PS[:, b0 + g, :], ACT.Copy, scale=cols[:, g:g + 1]).then_inc(oc_scaled, 1)
                elif c in ("ag", "bg", "cg"):
                    for f in range(NF):
                        if nsilu[0] >= 2:
                            act.wait_ge(u_lo, nsilu[0] - 1)
                        else:
                            act.wait_ge(pooled, NF)
                        act.activation(gt[:, nsilu[0] % 2, :], PS[:, b0 + f, :], ACT.Silu).then_inc(silu_done, 1)
                        act.wait_ge(u_done, nsilu[0] + 1)
                        b = ("ag", "bg", "cg").index(c)
                        act.activation(o_hi[:, b * NF + f, :], gt[:, nsilu[0] % 2, :], ACT.Copy).then_inc(u_hi, 1)
                        nsilu[0] += 1
                elif c[0] == "m":
                    k = CH[c] - CH["m00"]
                    if k >= 2:
                        act.wait_ge(sg_used, k - 1)
                    act.activation(sg[:, k % 2, :], PS[:, b0:b0 + 2, :].rearrange("p a s -> p (a s)"), ACT.Sigmoid).then_inc(sg_done, 1)
                    if c[2] == "2":
                        pr = int(c[1])
                        act.wait_ge(acc_done, k + 1)
                        act.activation(M_hi[:, 2 * pr:2 * pr + 2, :].rearrange("p a s -> p (a s)"), acc, ACT.Copy).then_inc(m_hi, 1)

        @block.vector
        def _(dve):
            link = linker(dve, dve_link)
            for t in range(NT):
                dve.wait_ge(rsx_done, t + 1)
                if t == 0:
                    dve.wait_ge(gb_in, 16)
                dve.scalar_tensor_tensor(xt[:, t, :], xt[:, t, :], rsx[:, t:t + 1], gB, ALU.mult, ALU.mult).then_inc(xn_done, 1)
            dve.wait_ge(consts, 1)
            dve.tensor_copy(identb[:, :], ident[:, :])
            for n in range(2 * NT):
                t, half = n // 2, n % 2
                dve.wait_ge(hhi_done, n + 1)
                hh = h_hi[:, 4 * half:4 * half + 4, t * P:(t + 1) * P]
                dve.tensor_tensor(h_lo[:, 4 * half:4 * half + 4, t * P:(t + 1) * P],
                                  PS[:, n % 8, :].rearrange("p (k s) -> p k s", k=4), hh.bitcast(F32), ALU.subtract).then_inc(hlo_done, 1)
            dve.wait_ge(maskf, 1)
            dve.tensor_copy(causal[:, :], mtmp[:, :]).then_inc(maskb, 1)
            dve.wait_ge(maskf, 2)
            dve.tensor_copy(cmask[:, :], mtmp[:, :]).then_inc(maskb, 1)
            dve.wait_ge(small_in, 16 * 10)
            lv = lamv[:, :, :].rearrange("p (a two) d -> p a two d", two=2)
            link(dve.tensor_tensor(TMP[:, 0:2, :], lv[:, :, 0, :], lv[:, :, 1, :], ALU.mult))
            dve.reduce_sum(lam2, TMP[:, 0:2, :], AX.X).then_inc(lam_s, 1)
            link(dve.tensor_scalar(subln[:, :], subln[:, :], 1.0 - LAM_INIT, None, ALU.mult))

            nsq = [0]
            for c in chunks[:BEFORE]:
                b0 = bank0(c)
                if c in ("aq", "ak", "bq", "sw"):
                    k = ("aq", "ak", "bq", "sw").index(c)
                    ng = 4 if c == "sw" else BH
                    if k:
                        dve.wait_ge(rsn_done, k)
                    for t in range(NT):
                        dve.wait_ge(sq_done, nsq[0] + 1)
                        s = sq[:, nsq[0] % 2, :]
                        if c == "sw":
                            s = s.rearrange("p (s two g d) -> p s two g d", s=2, two=2, g=G)[:, :, 0, :, :]
                            o = ssn[:, 4 * t:4 * t + 4].rearrange("p (s g) -> p s g", s=2)
                        else:
                            s = s.rearrange("p (h d) -> p h d", d=DK)
                            o = ssn[:, ng * t:ng * (t + 1)]
                        ins = dve.reduce_sum(o, s, AX.X)
                        ins.then_inc(ssn_part, 1)
                        nsq[0] += 1
                    dve.wait_ge(rsn_done, k + 1)
                    if c == "sw":
                        dve.wait_ge(vals_done, 1)
                    dst = {"aq": qA, "ak": kA, "bq": qB, "sw": kB}[c]
                    for t in range(NT):
                        if c == "sw":
                            for s2 in range(2):
                                src = PS[:, b0 + t, s2 * 256:s2 * 256 + 128].rearrange("p (g d) -> p g d", g=G)
                                r = rsn[:, 4 * t + 2 * s2:4 * t + 2 * s2 + 2].unsqueeze(2).broadcast_to([P, G, DK])
                                ins = dve.tensor_tensor(dst[:, t, s2 * P:(s2 + 1) * P].rearrange("p (g d) -> p g d", g=G), src, r, ALU.mult)
                        else:
                            src = PS[:, b0 + t, :].rearrange("p (h d) -> p h d", d=DK)
                            r = rsn[:, ng * t:ng * (t + 1)].unsqueeze(2).broadcast_to([P, ng, DK])
                            ins = dve.tensor_tensor(dst[:, t, :].rearrange("p (h d) -> p h d", d=DK), src, r, ALU.mult)
                    link(ins)
                    dve.sem_inc(drained[CH[c] % 2], 1)
                    if c == "sw":
                        for s2 in range(2):
                            v = dst[:, :, s2 * P:(s2 + 1) * P].rearrange("p t (g d) -> p t g d", g=G)
                            gg = gains[:, 4 + s2, :].unsqueeze(1).unsqueeze(1).broadcast_to([P, NT, G, DK])
                            ins = dve.tensor_tensor(v, v, gg, ALU.mult)
                    else:
                        gi = {"aq": 0, "ak": 1, "bq": 2}[c]
                        v = dst.rearrange("p t (h d) -> p (t h) d", d=DK)
                        ins = dve.tensor_tensor(v, v, gains[:, gi, :].unsqueeze(1).broadcast_to([P, NT * BH, DK]), ALU.mult)
                    ins.then_inc(tok_done, 1)
                elif c == "cmp":
                    dve.wait_ge(t2_done, 1)
                    dve.sem_inc(drained[CH[c] % 2], 1)
                    dve.wait_ge(cols_done, 1)
                    dve.wait_ge(xpad, 1)
                    for kv in range(2):
                        for g in range(G):
                            base = T2[:, kv, g, :]
                            src = bass.AP(base.tensor, base.offset, [list(base.ap[0]), [2, LP], [CMP_STRIDE, NCMP]])
                            ps = cols[:, NF + kv * LP:NF + (kv + 1) * LP].unsqueeze(2).broadcast_to([P, LP, NCMP])
                            ins = dve.tensor_tensor(X[:, kv, :, g, 0:NCMP], src, ps, ALU.add)
                    ins.then_inc(x_done, 1)
                elif c == "misc":
                    dve.wait_ge(kcr_done, 1)
                    link(dve.scalar_tensor_tensor(kcn[:, :], PS[:, b0 + 1, 0:DK], rskc, gains[:, 3, :], ALU.mult, ALU.mult))
                    link(dve.tensor_copy(kchl[:, 0, :], kcn[:, :]))
                    dve.tensor_copy(kchl[:, 2, :], kcn[:, :])
                    dve.tensor_tensor(kchl[:, 1, :], kcn[:, :], kchl[:, 0, :].bitcast(F32), ALU.subtract).then_inc(kchl_done, 1)
                    dve.wait_ge(vbd_zero, 1)
                    for g in range(G):
                        for t in range(NT):
                            ins = dve.tensor_copy(Vbd[t * CP:(t + 1) * CP, g, t * DK:(t + 1) * DK],
                                                  PS[t * CP:(t + 1) * CP, b0 + 1, (1 + g) * DK:(2 + g) * DK])
                    link(ins)
                    dve.wait_ge(gates_done, 1)
                    dve.sem_inc(drained[CH[c] % 2], 1)
            dve.wait_ge(lam_e, 1)
            link(dve.tensor_scalar(nlam, lame[:, 1:2], lame[:, 0:1], -LAM_INIT, ALU.subtract, ALU.add))

            gates_h = gates[:, :, :].rearrange("p t (h j) -> p t h j", j=3)
            nz = [0]
            for s in range(NSTEP):
                if s < NU:
                    kind, h, t, m = units[s]
                    dve.wait_ge(scores, s + 1)
                    if kind == "C":
                        if s >= 4:
                            dve.wait_ge(ptd, jobs_until(s - 4) + (1 if units[s - 4][0] == "A" and units[s - 4][3] == 0 else 0))
                        sc = PS[:, B_S + s % 3, 0:P].rearrange("p (t k) -> p t k", t=NT)
                        ins = dve.tensor_reduce(nmc, sc, AX.X, ALU.max, negate=True)
                        ins.then_inc(maxed, 1)
                        dve.wait_ge(maxed, s + 1)
                        dve.tensor_tensor(Pr[:, s % 4, 0:P].rearrange("p (t k) -> p t k", t=NT), sc,
                                          nmc.unsqueeze(2).broadcast_to([P, NT, CP]), ALU.add).then_inc(csub, 1)
                    else:
                        dve.tensor_reduce(negmax[:, s % 8:s % 8 + 1], PS[:, B_S + s % 3, 0:(t + 1) * P], AX.X, ALU.max,
                                          negate=True).then_inc(maxed, 1)
                u = s - 1
                if 0 <= u < NU:
                    kind, h, t, m = units[u]
                    W = (t + 1) * P
                    if kind == "A" and m == 1:
                        a, b = (u - 1) % 16, u % 16
                        dve.wait_ge(exped, u + 1)
                        link(dve.reciprocal(recip[:, a:b + 1], rowsum[:, a:b + 1]))
                        link(dve.tensor_tensor(recip[:, b:b + 1], recip[:, b:b + 1], nlam, ALU.mult))
                        link(dve.tensor_scalar(Pr[:, u % 4, 0:W], Pr[:, u % 4, 0:W], recip[:, b:b + 1], None, ALU.mult))
                        dve.scalar_tensor_tensor(Pr[:, u % 4, 0:W], Pr[:, (u - 1) % 4, 0:W], recip[:, a:a + 1],
                                                 Pr[:, u % 4, 0:W], ALU.mult, ALU.add).then_inc(weighted, 1)
                    elif kind == "C":
                        pc = Pr[:, u % 4, 0:P].rearrange("p (t k) -> p t k", t=NT)
                        dve.wait_ge(exped, u + 1)
                        link(dve.reduce_sum(lc, pc, AX.X))
                        link(dve.reciprocal(fc, lc))
                        link(dve.tensor_tensor(fc, fc, gates_h[:, :, h, 0], ALU.mult))
                        link(dve.tensor_tensor(fc[:, 0:1], fc[:, 0:1], has_cmp[:, :], ALU.mult))
                        dve.tensor_tensor(pc, pc, fc.unsqueeze(2).broadcast_to([P, NT, CP]), ALU.mult).then_inc(weighted, 1)
                u = s - LT
                if u in job_of:
                    j = job_of[u]
                    kind, h, t, m = units[u]
                    W = P if kind == "C" else (t + 1) * P
                    dve.wait_ge(ptd, j + 1)
                    if j >= 2:
                        wait_pv(dve, j - 2)
                    dve.tensor_copy(PTs[:, j % 2, 0:W], PS[:, B_PT + j % 2, 0:W]).then_inc(pt_out, 1)
                for i in range(NHEAD):
                    ob = PS[:, B_O + i % 2, :]
                    if i < AH:
                        o = OF[:, i % 2, :, :]
                        if s == last_u[i] + LF:
                            wait_pv(dve, job_of[last_u[i]])
                            if i >= 2:
                                dve.wait_ge(tr_made, tr_no(("fin", i - 2)) + 1)
                            link(dve.tensor_copy(o.rearrange("p t n -> p (t n)"), ob))
                            dve.sem_inc(o_free, 1)
                            for t in range(NT):
                                ins = dve.tensor_tensor_reduce(out=TMP2[:, :], in0=o[:, t, :], in1=o[:, t, :], scale=1.0, scalar=0.0,
                                                               op0=ALU.mult, op1=ALU.add, accum_out=ssf[:, t:t + 1])
                                link(ins)
                            dve.sem_inc(ss_f, 1)
                        if s == last_u[i] + LF + 2:
                            dve.wait_ge(rs_f, i + 1)
                            link(dve.tensor_tensor(o, o, rsf.unsqueeze(2).broadcast_to([P, NT, P]), ALU.mult))
                            dve.tensor_tensor(o, o, subln[:, :].unsqueeze(1).broadcast_to([P, NT, P]), ALU.mult).then_inc(of_done, 1)
                    elif s == last_u[i] + LF:
                        h = i - AH
                        pair = h // 2
                        slot = (AH + pair) % 2
                        o = OF[:, slot, :, (h % 2) * DK:(h % 2 + 1) * DK]
                        obr = ob.rearrange("p (m t d) -> p m t d", m=2, t=NT)
                        wait_pv(dve, job_of[last_u[i]])
                        dve.wait_ge(tr_drained, tr_no(("oc", first_u[i])) + 1)
                        if h % 2 == 0 and pair < 2:
                            dve.wait_ge(tr_made, tr_no(("fin", AH - 2 + pair)) + 1)
                        elif h % 2 == 0:
                            dve.wait_ge(tr_made, tr_no(("fin", AH + 2 * (pair - 2) + 1)) + 1)
                        rs = rowsum[:, 8 * (h % 2):8 * (h % 2) + 8]
                        link(dve.reciprocal(fB, rs))
                        for m in range(2):
                            ins = dve.tensor_tensor(fB[:, m * NT:(m + 1) * NT], fB[:, m * NT:(m + 1) * NT], gates_h[:, :, h, 1 + m], ALU.mult)
                        link(ins)
                        dve.tensor_tensor(o, obr[:, 0], fB[:, 0:NT].unsqueeze(2).broadcast_to([P, NT, DK]), ALU.mult)
                        link(dve.tensor_tensor(TMP[:, :, :], obr[:, 1], fB[:, NT:2 * NT].unsqueeze(2).broadcast_to([P, NT, DK]), ALU.mult))
                        dve.sem_inc(o_free, 1)
                        link(dve.tensor_tensor(o, o, TMP[:, :, :], ALU.add))
                        dve.tensor_tensor(o, o, OC[:, h % 2, :, :], ALU.add).then_inc(of_done, 1)

            dve.wait_ge(tr_drained, NTR)
            dve.memset(rowA[:, 0:PADL], 0.0)
            dve.memset(rowB[:, 0:PADL], 0.0)
            link(dve.memset(rowC[:, 0:PADL], 0.0))
            dve.sem_inc(pool_zero, 1)
            nsilu = [0]
            for c in chunks[BEFORE:]:
                b0 = bank0(c)
                if c == "cu":
                    for g in range(NF):
                        win = 2 << g
                        dve.wait_ge(cu_done, g + 1)
                        if g == NF - 1:
                            dve.sem_inc(drained[CH[c] % 2], 1)
                        dst = U[:, 2 * NF + g, :]
                        src, width, turn = rowA, 1, 0
                        bufs = [rowB, rowC]
                        while width < win:
                            nxt = bufs[turn % 2]
                            link(dve.tensor_tensor(nxt[:, 16:16 + SEQ], src[:, 16:16 + SEQ], src[:, 16 - width:16 + SEQ - width], ALU.add))
                            src, width, turn = nxt, 2 * width, turn + 1
                        link(dve.scalar_tensor_tensor(dst, src[:, 16:16 + SEQ], 1.0 / win, rowA[:, 16:16 + SEQ], ALU.mult, ALU.subtract))
                        link(dve.tensor_tensor(dst[:, 0:win - 1], src[:, 16:15 + win], inv_cnt[:, 0:win - 1], ALU.mult))
                        dve.tensor_tensor(dst[:, 0:win - 1], dst[:, 0:win - 1], rowA[:, 16:15 + win], ALU.subtract).then_inc(pooled, 1)
                elif c == "cw":
                    dve.wait_ge(oc_scaled, NF)
                    dve.sem_inc(drained[CH[c] % 2], 1)
                elif c in ("ag", "bg", "cg"):
                    b = ("ag", "bg", "cg").index(c)
                    for f in range(NF):
                        k = nsilu[0]
                        dve.wait_ge(silu_done, k + 1)
                        if f == NF - 1:
                            dve.sem_inc(drained[CH[c] % 2], 1)
                        dve.tensor_tensor(gt[:, k % 2, :], gt[:, k % 2, :], U[:, b * NF + f, :], ALU.mult).then_inc(u_done, 1)
                        dve.wait_ge(u_hi, k + 1)
                        dve.tensor_tensor(o_lo[:, b * NF + f, :], gt[:, k % 2, :], o_hi[:, b * NF + f, :].bitcast(F32), ALU.subtract).then_inc(u_lo, 1)
                        nsilu[0] += 1
                elif c[0] == "m":
                    k = CH[c] - CH["m00"]
                    dve.wait_ge(sg_done, k + 1)
                    wait_item_used(dve, LAST[c])
                    y = PS[:, b0 + 2:b0 + 4, :].rearrange("p a s -> p (a s)")
                    if c[2] == "0":
                        if k:
                            dve.wait_ge(m_lo, int(c[1]))
                        link(dve.tensor_tensor(acc, sg[:, k % 2, :], y, ALU.mult))
                        dve.sem_inc(drained[CH[c] % 2], 1)
                        dve.sem_inc(sg_used, 1)
                        dve.sem_inc(acc_done, 1)
                    else:
                        link(dve.tensor_tensor(sg[:, k % 2, :], sg[:, k % 2, :], y, ALU.mult))
                        dve.sem_inc(drained[CH[c] % 2], 1)
                        link(dve.tensor_tensor(acc, acc, sg[:, k % 2, :], ALU.add))
                        dve.sem_inc(sg_used, 1)
                        dve.sem_inc(acc_done, 1)
                    if c[2] == "2":
                        pr = int(c[1])
                        dve.wait_ge(m_hi, pr + 1)
                        dve.tensor_tensor(M_lo[:, 2 * pr:2 * pr + 2, :].rearrange("p a s -> p (a s)"), acc,
                                          M_hi[:, 2 * pr:2 * pr + 2, :].rearrange("p a s -> p (a s)").bitcast(F32), ALU.subtract).then_inc(m_lo, 1)
                else:
                    cc = int(c[2])
                    wait_item_used(dve, LAST[c])
                    dve.wait_ge(xres_in[cc], 16)
                    for t in range(NT):
                        dve.tensor_tensor(xres[cc][:, t, :], xres[cc][:, t, :], PS[:, b0 + t, :], ALU.add).then_inc(res_done, 1)

        @block.tensor
        def _(pe):
            pe.wait_ge(consts, 1)
            for n in range(2 * NT):
                t, half = n // 2, n % 2
                if half == 0:
                    pe.wait_ge(xn_done, t + 1)
                for k in range(4):
                    ins = pe.transpose(PS[:, n % 8, k * P:(k + 1) * P], xt[:, t, (4 * half + k) * P:(4 * half + k + 1) * P], ident[:, :])
                ins.then_inc(xT_done, 1)
            pe.wait_ge(rows_in, 32)
            pe.wait_ge(hlo_done, 1)
            NR = NF + 2 * LP
            pe.transpose(PS[:, 0, 0:NR], rows[:, :], ident[0:NR, 0:NR]).then_inc(cols_tr, 1)
            pe.wait_ge(hlo_done, 2 * NT)
            pe.wait_ge(cols_done, 1)

            def weights(name):
                n = item(name)
                i = SPLIT.index(n)
                pe.wait_ge(lo_done, i + 1)
                _, _, kt, ncol, _ = items[n]
                return [w[:, i % NSPL, 0:kt * ncol].rearrange("p (k n) -> p k n", k=kt) for w in (w_hi, w_lo)]

            def whole(name):
                n = item(name)
                wait_raw(pe, n)
                _, _, kt, ncol, _ = items[n]
                return raw[:, n % NRAW, 0:kt * ncol].rearrange("p (k n) -> p k n", k=kt)

            def three(out_, s_hi, s_lo, m_hi_, m_lo_, start, stop):
                pe.matmul(out_, s_hi, m_hi_, start=start, stop=False)
                pe.matmul(out_, s_hi, m_lo_, start=False, stop=False)
                return pe.matmul(out_, s_lo, m_hi_, start=False, stop=stop)

            def bank_free(c):
                n = CH[c]
                if n >= 2:
                    pe.wait_ge(drained[n % 2], n // 2)

            def token_major(c, names, ths, tls, nk):
                bank_free(c)
                b0 = bank0(c)
                per = nk // len(names)
                for part, name in enumerate(names):
                    wh, wl = weights(name)
                    for t in range(NT):
                        for k in range(per):
                            kk = part * per + k
                            ins = three(PS[:, b0 + t, 0:wh.shape[2]], ths[:, kk, t * P:(t + 1) * P], tls[:, kk, t * P:(t + 1) * P],
                                        wh[:, k, :], wl[:, k, :], kk == 0, kk == nk - 1)
                    ins.then_inc(split_used, 1)

            def feature_major(c, names, nf, bank, ths, tls, nk):
                per = nk // len(names)
                for part, name in enumerate(names):
                    wh, wl = weights(name)
                    for f in range(nf):
                        for k in range(per):
                            kk = part * per + k
                            ins = three(PS[:, bank + f, :], wh[:, k, f * P:(f + 1) * P], wl[:, k, f * P:(f + 1) * P],
                                        ths[:, kk, :], tls[:, kk, :], kk == 0, kk == nk - 1)
                    ins.then_inc(split_used, 1)

            for c in chunks[:BEFORE]:
                b0 = bank0(c)
                if c in ("aq", "ak", "av", "bq", "sw"):
                    token_major(c, [c + "0", c + "1"], h_hi, h_lo, NK)
                elif c == "cmp":
                    bank_free(c)
                    feature_major(c, ["cmp"], 2, b0, h_hi, h_lo, NK)
                elif c == "phi":
                    bank_free(c)
                    pe.wait_ge(x_done, 1)
                    for kv in range(2):
                        w1 = [None, None]
                        for half in range(2):
                            w1[half] = whole(f"phi{kv}{half}")
                        for n in range(NH2):
                            for l in range(LP):
                                ins = pe.matmul(PS[:, b0, (kv * NH2 + n) * G * CP:(kv * NH2 + n + 1) * G * CP],
                                                w1[l // (LP // 2)][:, l % (LP // 2), n * P:(n + 1) * P],
                                                X[:, kv, l, :, :].rearrange("p g b -> p (g b)"), start=l == 0, stop=l == LP - 1)
                                if n == NH2 - 1 and l >= LP - 2:
                                    ins.then_inc(whole_used, 1)
                else:
                    bank_free(c)
                    wh, wl = weights("bbg")
                    for t in range(NT):
                        for k in range(NK):
                            ins = three(PS[:, b0, t * NG:(t + 1) * NG], h_hi[:, k, t * P:(t + 1) * P], h_lo[:, k, t * P:(t + 1) * P],
                                        wh[:, k, :], wl[:, k, :], k == 0, k == NK - 1)
                    pe.wait_ge(ht_done, 1)
                    pe.wait_ge(small_in, 16 * 10)
                    for n in range(NH2):
                        pe.matmul(PS[:, b0 + 1, 0:DK], HTk[:, n].rearrange("p r c -> p (r c)"), w2[:, 0, n, :], start=n == 0, stop=n == NH2 - 1)
                    for g in range(G):
                        for n in range(NH2):
                            ins = pe.matmul(PS[:, b0 + 1, (1 + g) * DK:(2 + g) * DK], HTv[:, n, g].rearrange("p r b -> p (r b)"),
                                            w2[:, 1, n, :], start=n == 0, stop=n == NH2 - 1)
                    ins.then_inc(split_used, 1)

            for par in range(2):
                pe.wait_ge(drained[par], BEFORE // 2)
            pe.wait_ge(vals_done, 1)
            pe.wait_ge(maskb, 2)

            def transpose_tr(r):
                n = tr_no(r)
                if n:
                    pe.wait_ge(tr_drained, n)
                bank = PS[:, B_TR, :]
                if r[0] == "kc":
                    pe.wait_ge(kchl_done, 1)
                    src = kchl[:, r[1]:r[1] + 2, :].rearrange("p a d -> p (a d)").bitcast(F32)
                    pe.transpose(bank[:, 0:P], src, ident[:, :]).then_inc(tr_made, 1)
                elif r[0] in ("q", "kh", "kl"):
                    pe.wait_ge(hl_made, r[1] + 1)
                    for t in range(NT):
                        j = int(r[0] == "kl")
                        hl = HL[:, r[1] % 2, t, j:j + 2, :].rearrange("p a d -> p (a d)").bitcast(F32)
                        ins = pe.transpose(bank[:, t * P:(t + 1) * P], hl, ident[:, :])
                    ins.then_inc(tr_made, 1)
                elif r[0] == "oc":
                    u = r[1]
                    j = job_of[u]
                    g = units[u][1] // HPG
                    pe.wait_ge(pt_out, j + 1)
                    pe.matmul(bank[:, 0:NT * DK], PTs[:, j % 2, 0:P], Vbd[:, g, :], start=True, stop=True).then_inc(tr_made, 1)
                else:
                    i = r[1]
                    slot = i % 2 if i < AH else (AH + (i - AH) // 2) % 2
                    pe.wait_ge(of_done, i + 1)
                    for t in range(NT):
                        ins = pe.transpose(bank[:, t * P:(t + 1) * P], OF[:, slot, t, :], ident[:, :])
                    ins.then_inc(tr_made, 1)

            for r in trs[-1]:
                transpose_tr(r)
            for s in range(NSTEP):
                if s < NU:
                    kind, h, t, m = units[s]
                    i = head_of[s]
                    if s >= 3:
                        pe.wait_ge(exped, s - 2)
                    if s == first_u[i]:
                        pe.wait_ge(tr_drained, max(tr_no(r) for r in prep(i)) + 1)
                    bank = PS[:, B_S + s % 3, :]
                    if kind == "C":
                        q = QS[:, 2 * (i % 2), :]
                        g = h // HPG
                        for tt in range(NT):
                            o = bank[:, tt * CP:(tt + 1) * CP]
                            for a in range(2):
                                pe.matmul(o, q[:, tt * P:(tt + 1) * P], KC[:, a, g * CP:(g + 1) * CP], start=a == 0, stop=False)
                            ins = pe.matmul(o, identb[:, :], cmask[:, tt * CP:(tt + 1) * CP], start=False, stop=True)
                    else:
                        if kind == "A":
                            q, kpos = QS[:, 2 * (i % 2) + m, :], 4 * (i % 2) + 2 * m
                        else:
                            q, kpos = QS[:, 2 * (i % 2), :], 4 * ((h // HPG) % 2) + 2 * m
                        W = (t + 1) * P
                        for a in range(2):
                            pe.matmul(bank[:, 0:W], q[:, t * P:(t + 1) * P], KS[:, kpos + a, 0:W], start=a == 0, stop=False)
                        ins = pe.matmul(bank[:, t * P:W], identb[:, :], causal[:, :], start=False, stop=True)
                    ins.then_inc(scores, 1)
                u = s - LT
                if u in job_of:
                    j = job_of[u]
                    kind, h, t, m = units[u]
                    if kind == "B":
                        pe.wait_ge(exped, u + 1)
                    else:
                        pe.wait_ge(weighted, sum(1 for v in jobs[:j + 1] if units[v][0] != "B"))
                    if j >= 2:
                        pe.wait_ge(pt_out, j - 1)
                    for kb in range(1 if kind == "C" else t + 1):
                        ins = pe.transpose(PS[:, B_PT + j % 2, kb * P:(kb + 1) * P], Pr[:, u % 4, kb * P:(kb + 1) * P], ident[:, :])
                    ins.then_inc(ptd, 1)
                u = s - LV
                if u in job_of and units[u][0] != "C":
                    j = job_of[u]
                    kind, h, t, m = units[u]
                    i = head_of[u]
                    pe.wait_ge(pt_out, j + 1)
                    if i >= 2 and u == first_pv[i]:
                        pe.wait_ge(o_free, i - 1)
                    for kb in range(t + 1):
                        lhs = PTs[:, j % 2, kb * P:(kb + 1) * P]
                        if kind == "A":
                            ins = pe.matmul(PS[:, B_O + i % 2, t * P:(t + 1) * P], lhs, vA[:, kb, h * P:(h + 1) * P], start=kb == 0, stop=kb == t)
                        else:
                            g = h // HPG
                            o = (m * NT + t) * DK
                            ins = pe.matmul(PS[:, B_O + i % 2, o:o + DK], lhs, vB[:, kb, (m * G + g) * DK:(m * G + g + 1) * DK],
                                            start=kb == 0, stop=kb == t)
                    ins.then_inc(pv_done, 1)
                for r in trs[s]:
                    transpose_tr(r)

            pe.wait_ge(tr_drained, NTR)
            pe.wait_ge(o_free, NHEAD)
            for c in chunks[BEFORE:]:
                b0 = bank0(c)
                bank_free(c)
                if c in ("cu", "ag", "bg", "cg"):
                    feature_major(c, [c + "0", c + "1"], NF, b0, h_hi, h_lo, NK)
                elif c == "cw":
                    pe.wait_ge(pooled, NF)
                    w = whole("cw")
                    for g in range(NF):
                        ins = pe.matmul(PS[:, b0 + g, :], w[:, g, :], U[:, 2 * NF + g, :], start=True, stop=True)
                    ins.then_inc(whole_used, 1)
                elif c[0] == "m":
                    pr, b = int(c[1]), int(c[2])
                    feature_major(c, [f"mg{pr}{b}"], 2, b0, h_hi, h_lo, NK)
                    pe.wait_ge(u_lo, (b + 1) * NF)
                    feature_major(c, [f"wb{pr}{b}"], 2, b0 + 2, o_hi[:, b * NF:(b + 1) * NF, :], o_lo[:, b * NF:(b + 1) * NF, :], NF)
                else:
                    pe.wait_ge(m_lo, NP)
                    token_major(c, [c + "0", c + "1"], M_hi, M_lo, NK)


_INS = ['x', 'norm_g', 'w_in', 'a_q_g', 'a_k_g', 'a_lam', 'a_subln_g', 'b_q_g', 'b_k_g', 'b_cmp_pos',
        'b_phi_w1', 'b_phi_w2', 'c_w', 'c_scale', 'w_branch', 'w_out']


def kernel(**inputs):
    import numpy as _np
    import concourse.bacc as _bacc
    from concourse import mybir as _mybir
    from concourse.bass_utils import run_bass_kernel_spmd as _run

    nc = _bacc.Bacc("TRN2", target_bir_lowering=False, num_devices=1)
    arrays, args = {}, []
    for name in _INS:
        a = _np.ascontiguousarray(inputs[name])
        arrays[f"in_{name}_dram"] = a
        args.append(nc.dram_tensor(f"in_{name}_dram", a.shape, _mybir.dt.from_np(a.dtype), kind="ExternalInput").ap())
    shape = arrays["in_x_dram"].shape
    args.append(nc.dram_tensor("out_0_dram", shape, _mybir.dt.float32, kind="ExternalOutput").ap())
    hybrid_trunk_kernel(nc, *args)
    r = _run(nc, [arrays], core_ids=[0])
    return r.results[0]["out_0_dram"]
```

```python
import math
from contextlib import ExitStack

import concourse.bass as bass
from concourse import mybir


def hybrid_trunk_kernel(nc: bass.Bass, x, norm_g, w_in, a_q_g, a_k_g, a_lam, a_subln_g, b_q_g, b_k_g,
                        b_cmp_pos, b_phi_w1, b_phi_w2, c_w, c_scale, w_branch, w_out, out):
    F32, F32R, BF16 = mybir.dt.float32, mybir.dt.float32r, mybir.dt.bfloat16
    ALU, ACT, AX = mybir.AluOpType, mybir.ActivationFunctionType, mybir.AxisListType
    P = 128
    _, SEQ, D = x.shape
    EPS, NEG = 1e-6, -1e30
    NT = SEQ // P
    NK = D // P
    BW = w_branch.shape[2]
    NF = BW // P
    DK = a_q_g.shape[1]
    AH = BW // (2 * DK)
    BH = BW // DK
    G = 2
    HPG = BH // G
    CMP_LEN, CMP_STRIDE = b_cmp_pos.shape[2], 16
    NCMP = (SEQ - CMP_LEN) // CMP_STRIDE + 1
    CP = 32
    LP = CMP_LEN // 2
    HID = b_phi_w1.shape[3]
    NH2 = HID // P
    LAM_INIT = 0.8 - 0.6 * math.exp(-0.3 * 0)

    C_AQ, C_AK, C_AV, C_AG = 0, BW, 2 * BW, 3 * BW
    C_BQ = 4 * BW
    C_KV = 5 * BW
    C_CMP, C_SW = C_KV, C_KV + 4 * DK
    C_BBG = C_KV + 12 * DK
    NG = 3 * BH
    C_BG = C_BBG + NG
    C_CU, C_CG = C_BG + BW, C_BG + 2 * BW
    C_MG = C_BG + 3 * BW

    win_k = w_in[0].rearrange("(k p) n -> p k n", p=P)
    wout_k = w_out[0].rearrange("(k p) n -> p k n", p=P)
    wbr_k = [w_branch[0, b].rearrange("(k p) n -> p k n", p=P) for b in range(3)]
    w1_k = [b_phi_w1[0, c].rearrange("(l p) n -> p l n", p=P) for c in range(2)]
    HK = NK // 2
    SLOT = HK * BW
    PC = 2 * P
    items = []

    def add(name, view, kt, cols, split=True):
        items.append((name, view, kt, cols, split))

    def add_halves(name, view, c0):
        for half in range(2):
            add(f"{name}{half}", view[:, half * HK:(half + 1) * HK, c0:c0 + BW], HK, BW)

    def add_pairs(name, c0):
        for half in range(2):
            add(f"{name}{half}", win_k[:, :, c0 + half * PC:c0 + (half + 1) * PC], NK, PC)

    add_halves("aq", win_k, C_AQ)
    add_halves("ak", win_k, C_AK)
    add_halves("av", win_k, C_AV)
    add_pairs("bq", C_BQ)
    add_pairs("sw", C_SW)
    add("cmp", win_k[:, :, C_CMP:C_CMP + PC], NK, PC)
    for c in range(2):
        for half in range(2):
            add(f"phi{c}{half}", w1_k[c][:, half * LP // 2:(half + 1) * LP // 2, :], LP // 2, HID, False)
    add("bbg", win_k[:, :, C_BBG:C_BBG + NG], NK, NG)
    add_pairs("ag", C_AG)
    add_pairs("cu", C_CU)
    add_pairs("bg", C_BG)
    add("cw", c_w[0].rearrange("g c d -> c g d"), NF, P, False)
    add_pairs("cg", C_CG)
    NP = D // PC
    for pr in range(NP):
        for b in range(3):
            add(f"mg{pr}{b}", win_k[:, :, C_MG + b * D + pr * PC:C_MG + b * D + (pr + 1) * PC], NK, PC)
            add(f"wb{pr}{b}", wbr_k[b][:, :, pr * PC:(pr + 1) * PC], NF, PC)
    for c in range(2):
        add_halves(f"wo{c}", wout_k, c * BW)
    NAMES = [i[0] for i in items]
    SPLIT = [n for n, i in enumerate(items) if i[4]]
    WHOLE = [n for n, i in enumerate(items) if not i[4]]
    NRAW, NSPL = 3, 2

    def item(name):
        return NAMES.index(name)

    units = []
    for h in range(AH):
        units += [("A", h, t, m) for t in range(NT) for m in range(2)]
    for h in range(BH):
        units += [("B", h, t, m) for m in range(2) for t in range(NT)] + [("C", h, 0, 0)]
    NU = len(units)
    jobs = [u for u, (kind, _, _, m) in enumerate(units) if kind != "A" or m == 1]
    job_of = {u: j for j, u in enumerate(jobs)}
    NHEAD = AH + BH
    head_of = [h if kind == "A" else AH + h for kind, h, _, _ in units]
    first_u = [head_of.index(i) for i in range(NHEAD)]
    last_u = [NU - 1 - head_of[::-1].index(i) for i in range(NHEAD)]
    first_pv = [next(u for u in jobs if head_of[u] == i) for i in range(NHEAD)]
    LT, LV, LF = 2, 3, 4
    S0, NSTEP = -8, NU + LF + 4
    STEPS = range(S0, NSTEP)

    hls, head_hl = [], {}
    for i in range(NHEAD):
        if i < AH:
            mine = [("q", i, 0), ("k", i, 0), ("q", i, 1), ("k", i, 1)]
        else:
            mine = [("q", i, 0)]
            if (i - AH) % HPG == 0:
                mine += [("k", i, 0), ("k", i, 1)]
        head_hl[i] = list(range(len(hls), len(hls) + len(mine)))
        hls += mine

    def prep(i):
        r = []
        for k in head_hl[i]:
            r += [("q", k)] if hls[k][0] == "q" else [("kh", k), ("kl", k)]
        return r

    fills = []
    for name in ("bq", "sw"):
        fills += [("tok", f"{name}{half}", tp) for half in range(2) for tp in range(2)]
    fills += [("cmp", "cmp", kv) for kv in range(2)]
    fills += [("phi", "phi", 0), ("bbg", "bbg", 0), ("phi2", "phi2", 0)]
    NEARLY = len(fills)
    for name in ("ag", "cu", "bg"):
        fills += [(name, f"{name}{half}", f) for half in range(2) for f in range(2)]
    fills += [("cw", "cw", g) for g in range(NF)]
    NFILL = len(fills)
    PIECES = {"tok": 4, "cmp": 4, "phi": 8, "bbg": 2, "phi2": 1, "ag": 4, "cu": 4, "bg": 4, "cw": 1}
    DVE_DRAINS = ("phi", "phi2", "ag", "bg")

    def item_of(kind, name, p):
        return None if kind == "phi2" else item(f"phi{p // 4}{p // 2 % 2}" if kind == "phi" else name)

    def drain_step(k):
        return fill_end[k] + (2 if fills[k][0] in DVE_DRAINS else 1)

    fill_at = {s: [] for s in STEPS}
    fill_end = {}
    used_step = {}
    first_split = sum(1 for n in SPLIT if n <= item("av1")) + NSPL

    def split_step(n):
        i = SPLIT.index(n)
        if i < first_split:
            return S0
        return 1 + max(used_step.get(NAMES[w], S0) for w in [SPLIT[i - NSPL]] + [w for w in WHOLE if w <= n - NRAW])

    def high_step(i):
        return max(split_step(SPLIT[i]), high_step(i - 1) + 2 if i > first_split else S0)
    s, room = S0, 0.0
    RATE_A, RATE_B = 1.5, 0.8
    for k, (kind, name, _) in enumerate(fills):
        for p in range(PIECES[kind]):
            while True:
                ok = room >= 1
                if item_of(kind, name, p) in SPLIT:
                    i = SPLIT.index(item_of(kind, name, p))
                    ok = ok and (i < first_split or s > high_step(i) + 2)
                if p == 0 and k >= 2:
                    ok = ok and s > drain_step(k - 2)
                if kind == "phi" and p == 0:
                    ok = ok and s > fill_end[k - 1] + 2
                if kind == "phi2":
                    ok = ok and s > fill_end[k - 2] + 4
                if kind == "ag" and p == 0:
                    ok = ok and s > last_u[AH - 1] - 1
                if kind == "cw":
                    ok = ok and s > fill_end[k - 2 * NF] + 2 + k - NFILL + NF + 2
                if ok:
                    break
                s += 1
                room = min(room, 2) + (RATE_A if k < NEARLY else RATE_B)
            fill_at[s].append((k, p))
            if kind != "phi2":
                used_step[NAMES[item_of(kind, name, p)]] = s
            room -= 1
        fill_end[k] = s
    gate_fills = [k for k, f in enumerate(fills) if f[0] in ("ag", "bg")]
    FILL = {f: k for k, f in enumerate(fills)}

    trs = {s: [] for s in STEPS}
    for i in range(NHEAD):
        s0 = first_u[i - 1] + 1 if i else S0 + 2
        for n, r in enumerate(prep(i)):
            trs[s0 + n].append(r)
    trs[fill_end[FILL[("phi", "phi", 0)]] + 3].append(("ht", 0))
    KC_STEP = fill_end[FILL[("phi2", "phi2", 0)]] + 4
    trs[KC_STEP].append(("kc", 0))
    trs[KC_STEP + 1].append(("kc", 1))
    for u, (kind, h, _, _) in enumerate(units):
        if kind == "C":
            trs[u + LV].append(("oc", u))
    for i in range(NHEAD):
        if i < AH or (i - AH) % 2:
            trs[last_u[i] + LF + (4 if i < AH else 1)].append(("fin", i))
    tr_list = [(s, r) for s in STEPS for r in trs[s]]
    tr_step = {r: s for s, r in tr_list}
    NTR = len(tr_list)

    def tr_no(r):
        return next(n for n, (_, q) in enumerate(tr_list) if q == r)

    def last_tr(k):
        return tr_no(("q", k)) if hls[k][0] == "q" else tr_no(("kl", k))

    dve_at = {s: [] for s in STEPS}
    act_at = {s: [] for s in STEPS}
    pool_at = {s: [] for s in STEPS}
    for k in range(len(hls)):
        dve_at[tr_step[("q" if hls[k][0] == "q" else "kh", k)] - 1].append(("hl", k))
    norms = [("bq0", 0), ("bq1", 1), ("sw0", 2), ("sw1", 3)]
    for k, (kind, name, w) in enumerate(fills):
        e = fill_end[k]
        act_at[e + 1].append(("drain", k))
        if kind == "tok" and w == 1:
            dve_at[e + 2].append(("norm1", name))
            pool_at[e + 2].append(("norm", name))
            dve_at[e + 4].append(("norm2", name))
        if kind == "cmp":
            dve_at[e + 2].append(("x", w))
        if kind == "phi":
            dve_at[e + 2].append(("silu", k))
        if kind == "bbg":
            dve_at[e + 2].append(("gates", k))
        if kind == "phi2":
            dve_at[e + 2].append(("kc1", k))
            pool_at[e + 2].append(("kc", k))
            dve_at[e + 3].append(("kc2", k))
        if kind in ("ag", "bg"):
            dve_at[e + 2].append(("gate", k))
        if kind == "ag":
            dve_at[e + 3].append(("agate", k))
        if kind == "cu":
            g = 2 * int(name[2]) + w
            for level in range(g + 2):
                dve_at[e + 2 + level].append(("pool", (k, g, level)))
    for i in range(AH):
        pool_at[last_u[i] + LF + 1].append(("fin", i))
    in_steps = sum(1 for n in SPLIT if n <= item("bg1")) + NSPL
    splits_at = {s: max([first_split] + [i + 1 for i in range(in_steps) if high_step(i) + 1 <= s]) for s in STEPS}
    highs_at = {s: [] for s in STEPS}
    for i in range(first_split, in_steps):
        for half in range(2):
            highs_at[high_step(i) + half].append((i, half))

    ctx = ExitStack()
    with ctx:
        def sem(name):
            return ctx.enter_context(nc.semaphore(name))

        def sb(name, shape, dt, c=ctx):
            return c.enter_context(nc.sbuf_tensor(name, shape, dt))

        h_hi = sb("h_hi", [P, NK, SEQ], F32R)
        h_lo = sb("h_lo", [P, NK, SEQ], F32R)
        raw = sb("raw", [P, NRAW, SLOT], F32)
        w_hi = sb("w_hi", [P, NSPL, SLOT], F32R)
        w_lo = sb("w_lo", [P, NSPL, SLOT], F32R)
        U = sb("U", [P, 3 * NF, SEQ], F32)
        gt = sb("gt", [P, 2, SEQ], F32)
        ident = sb("ident", [P, P], F32)
        identb = sb("identb", [P, P], BF16)
        causal = sb("causal", [P, P], BF16)
        cmask = sb("cmask", [P, NT * CP], BF16)
        gains = sb("gains", [P, 6, DK], F32)
        subln = sb("subln", [P, 2 * DK], F32)
        cols = sb("cols", [P, NF + 2 * LP], F32)
        Vbd = sb("Vbd", [P, G, NT * DK], F32)
        KC = sb("KC", [P, 2, G * CP], F32R)
        gates = sb("gates", [P, NT, NG], F32)
        st = sb("st", [P, 156], F32)
        half_pow = sb("half_pow", [P, 32], F32)
        inv_cnt = sb("inv_cnt", [P, 16], F32)
        has_cmp = sb("has_cmp", [P, 1], F32)

        early = ExitStack()
        qkA = sb("qkA", [P, 2, NT, BW], F32, early)
        early.close()
        oA_hi = sb("oA_hi", [P, NF, SEQ], F32R)
        oA_lo = sb("oA_lo", [P, NF, SEQ], F32R)

        early = ExitStack()
        tok = sb("tok", [P, 3 * NT * BW], F32, early)
        QS = sb("QS", [P, 4, SEQ], F32R, early)
        KS = sb("KS", [P, 8, SEQ], F32R, early)
        PTs = sb("PTs", [P, 2, SEQ], F32, early)
        HLq = sb("HLq", [P, NT, 2, DK], F32R, early)
        HLk = sb("HLk", [P, NT, 3, DK], F32R, early)
        OF = sb("OF", [P, NT, P], F32, early)
        Pr = sb("Pr", [P, 3, SEQ], F32, early)
        OC = sb("OC", [P, 2, NT, DK], F32, early)
        kchl = sb("kchl", [P, 3, DK], F32R, early)
        kcn = sb("kcn", [P, DK], F32, early)
        early.close()
        M_hi = sb("M_hi", [P, NK, SEQ], F32R)
        M_lo = sb("M_lo", [P, NK, SEQ], F32R)
        oB_hi = sb("oB_hi", [P, 2 * NF, SEQ], F32R)
        oB_lo = sb("oB_lo", [P, 2 * NF, SEQ], F32R)
        o_hi = [oA_hi[:, f, :] for f in range(NF)] + [oB_hi[:, f, :] for f in range(2 * NF)]
        o_lo = [oA_lo[:, f, :] for f in range(NF)] + [oB_lo[:, f, :] for f in range(2 * NF)]
        acc = U[:, 0:2, :].rearrange("p a s -> p (a s)")
        sg = U[:, 2:6, :].rearrange("p (b a) s -> p b (a s)", b=2)
        xres = [U[:, 8:12, :], U[:, 4:8, :]]

        def region(a, n):
            return tok[:, a * NT * BW // 2:(a + n) * NT * BW // 2]
        qA, kA = qkA[:, 0], qkA[:, 1]
        vA = region(0, 2).rearrange("p (t n) -> p t n", t=NT)
        gB2 = vA
        qB = region(2, 2).rearrange("p (t n) -> p t n", t=NT)
        kB = region(4, 1).rearrange("p (t n) -> p t n", t=NT)
        vB = region(5, 1).rearrange("p (t n) -> p t n", t=NT)
        gB = qkA[:, 0, 0:2, :].rearrange("p t n -> p (t n)")
        xt = region(0, 4).rearrange("p (t n) -> p t n", t=NT)
        lamv = PTs[:, 0, 0:4 * DK].rearrange("p (a d) -> p a d", a=4)
        rows = PTs[0:NF + 2 * LP, 0, 2 * P:3 * P]
        mtmp = PTs[:, 0, 3 * P:4 * P]
        lamt = PTs[:, 1, 0:2 * DK].rearrange("p (a d) -> p a d", a=2)
        w2 = U[:, 3, 0:2 * NH2 * DK].rearrange("p (c n d) -> p c n d", c=2, n=NH2)
        T2 = U[:, 4:8, :].rearrange("p (c g) s -> p c g s", c=2)
        X = U[:, 8:12, :].rearrange("p c s -> p (c s)").rearrange("p (l c g b) -> p l c g b", c=2, l=LP, g=G)
        T2f = U[:, 4:8, :].rearrange("p c s -> p (c s)")
        NH = HID
        hid_e = T2f[:, 0:NH]
        HTk = T2f[:, NH:NH + NH2 * P].rearrange("p (n r c) -> p n r c", n=NH2, r=2)
        HTv = T2f[:, NH + NH2 * P:NH + 3 * NH2 * P].rearrange("p (n g r b) -> p n g r b", n=NH2, g=G, r=4)
        wB = U[:, 2 * NF - 1, :].rearrange("p (m d) -> p m d", d=DK)
        sq2 = gt[:, :, :].rearrange("p a s -> p (a s)")
        PS = ctx.enter_context(nc.psum_tensor("PS", [P, 8, 512], F32))
        B_S, B_PT, B_TR, B_O, B_F = 0, 2, 4, 5, 6

        ssx, rsx = st[:, 0:4], st[:, 4:8]
        ssn, rsn = st[:, 8:40], st[:, 40:72]
        sskc, rskc = st[:, 72:73], st[:, 73:74]
        lam2, lame, nlam = st[:, 74:76], st[:, 76:78], st[:, 78:79]
        negmax = st[:, 80:88]
        rowsum = st[:, 88:104]
        recip = st[:, 104:120]
        nmc, lc, fc = st[:, 120:124], st[:, 124:128], st[:, 128:132]
        ssf, rsf = st[:, 132:136], st[:, 136:140]
        fB = st[:, 140:148]

        raw_in = [sem(f"raw_in{i}") for i in range(NRAW)]
        x_in = [sem(f"x_in{i}") for i in range(NT)]
        gb_in, small_in, rows_in = sem("gb_in"), sem("small_in"), sem("rows_in")
        xres_in = [sem("xres_in0"), sem("xres_in1")]
        stored = sem("stored")
        hi_done, lo_done, lo_dve, split_used, whole_used = (sem(n) for n in (
            "hi_done", "lo_done", "lo_dve", "split_used", "whole_used"))
        consts, maskf, maskb, ssx_done, rsx_done, xn_done = (sem(n) for n in (
            "consts", "maskf", "maskb", "ssx_done", "rsx_done", "xn_done"))
        xT_done, hhi_done, hlo_done, cols_tr, cols_done, vbd_zero, xpad = (sem(n) for n in (
            "xT_done", "hhi_done", "hlo_done", "cols_tr", "cols_done", "vbd_zero", "xpad"))
        lam_s, lam_e = sem("lam_s"), sem("lam_e")
        drained = [sem("drained0"), sem("drained1")]
        sq_done, ssn_part, rsn_done, tok_done = sem("sq_done"), sem("ssn_part"), sem("rsn_done"), sem("tok_done")
        filled, act_free, dve_free = sem("filled"), sem("act_free"), sem("dve_free")
        ssn2_done, rsn2_done, x_done, hid_done, kcs_done, kcr_done, kchl_done = (sem(n) for n in (
            "ssn2_done", "rsn2_done", "x_done", "hid_done", "kcs_done", "kcr_done", "kchl_done"))
        e_done, g_done, pooled = sem("e_done"), sem("g_done"), sem("pooled")
        hl_made, tr_made, tr_drained = sem("hl_made"), sem("tr_made"), sem("tr_drained")
        scores, maxed, exped, weighted = sem("scores"), sem("maxed"), sem("exped"), sem("weighted")
        csub, ptd, pt_out, pv_done = sem("csub"), sem("ptd"), sem("pt_out"), sem("pv_done")
        ss_f, rs_f, of_done, o_free = sem("ss_f"), sem("rs_f"), sem("of_done"), sem("o_free")
        silu_done, u_done, u_hi, u_lo = sem("silu_done"), sem("u_done"), sem("u_hi"), sem("u_lo")
        sg_done, sg_used, acc_done, m_hi, m_lo, res_done = (sem(n) for n in (
            "sg_done", "sg_used", "acc_done", "m_hi", "m_lo", "res_done"))
        dve_link, act_link, pool_link = sem("dve_link"), sem("act_link"), sem("pool_link")

        CHUNKS1 = ["aq", "ak", "av"]
        CHUNKS2 = ["cg"] + [f"m{pr}{b}" for pr in range(NP) for b in range(3)] + ["wo0", "wo1"]
        PARITY = {c: n % 2 for n, c in enumerate(CHUNKS1)}
        PARITY.update({c: n % 2 for n, c in enumerate(CHUNKS2)})
        EARLIER = {c: n // 2 for n, c in enumerate(CHUNKS1)}
        base = [(len(CHUNKS1) + 1) // 2, len(CHUNKS1) // 2]
        EARLIER.update({c: base[n % 2] + n // 2 for n, c in enumerate(CHUNKS2)})
        MI = {c: n - 1 for n, c in enumerate(CHUNKS2)}
        LAST = {"aq": "aq1", "ak": "ak1", "av": "av1", "cg": "cg1", "wo0": "wo01", "wo1": "wo11"}
        LAST.update({f"m{pr}{b}": f"wb{pr}{b}" for pr in range(NP) for b in range(3)})

        def bank0(c):
            return 4 * PARITY[c]

        def bcast(v, n):
            return bass.AP(v.tensor, v.offset, [[0, P], [1, n]])

        def splits_through(c):
            return min(sum(1 for n in SPLIT if n <= item(LAST[c])) + NSPL, len(SPLIT))

        DVE_LO = {n: 1408 for n in SPLIT if NAMES[n][:2] == "mg"}

        def wait_item_used(eng, name):
            n = item(name)
            if n in SPLIT:
                eng.wait_ge(split_used, SPLIT.index(n) + 1)
            else:
                eng.wait_ge(whole_used, WHOLE.index(n) + 1)

        def wait_low(eng, i):
            eng.wait_ge(lo_done, i + 1)
            if SPLIT[i] in DVE_LO:
                eng.wait_ge(lo_dve, sum(1 for n in DVE_LO if n <= SPLIT[i]))

        def wait_pv(eng, j):
            if units[jobs[j]][0] == "C":
                eng.wait_ge(tr_made, tr_no(("oc", jobs[j])) + 1)
            else:
                eng.wait_ge(pv_done, sum(1 for v in jobs[:j + 1] if units[v][0] != "C"))

        def wait_bank_read(eng, k):
            mine = fills[k][0] in DVE_DRAINS
            eng.wait_ge(dve_free if mine else act_free, sum(1 for f in fills[:k + 1] if (f[0] in DVE_DRAINS) == mine))

        def ends_item(k):
            kind, _, w = fills[k]
            return kind == "phi" or kind == "bbg" or (kind == "cw" and w == NF - 1) or \
                (kind in ("tok", "cmp", "ag", "cu", "bg") and w == 1)

        def wait_filled(eng, k):
            kind, name, _ = fills[k]
            if ends_item(k):
                wait_item_used(eng, f"phi1{NH2 - 1}" if kind == "phi" else name)
            else:
                eng.wait_ge(filled, sum(1 for q in range(k + 1) if not ends_item(q)))

        def wait_place(eng, s):
            if s >= 3:
                kind, _, _, m = units[s - 3]
                if kind == "A" and m == 0:
                    eng.wait_ge(weighted, weighted_no(s - 2))
                else:
                    eng.wait_ge(ptd, job_of[s - 3] + 1)

        def weighted_no(u):
            return sum(1 for v in jobs[:job_of[u] + 1] if units[v][0] != "B")

        def linker(eng, s):
            n = [0]

            def link(ins):
                n[0] += 1
                ins.then_inc(s, 1)
                eng.wait_ge(s, n[0])
            return link

        def wait_raw(eng, n):
            eng.wait_ge(raw_in[n % NRAW], 16 * (n // NRAW + 1))

        block = ctx.enter_context(nc.Block())

        @block.sync
        def _(sp):
            for n, (name, view, kt, ncol, split) in enumerate(items):
                if n >= NRAW:
                    if n - NRAW in SPLIT:
                        wait_low(sp, SPLIT.index(n - NRAW))
                    else:
                        sp.wait_ge(whole_used, WHOLE.index(n - NRAW) + 1)
                dst = raw[:, n % NRAW, 0:kt * ncol].rearrange("p (k n) -> p k n", k=kt)
                sp.dma_start(dst, view).then_inc(raw_in[n % NRAW], 16)
            for c in range(2):
                if c == 0:
                    sp.wait_ge(u_lo, 2 * NF)
                else:
                    sp.wait_ge(m_lo, NP)
                sp.dma_start(xres[c], x[0, :, c * BW:(c + 1) * BW].rearrange("(t p) n -> p t n", p=P))\
                    .then_inc(xres_in[c], 16)
            for c in range(2):
                for t in range(NT):
                    sp.wait_ge(res_done, c * NT + t + 1)
                    sp.dma_start(out[0, t * P:(t + 1) * P, c * BW:(c + 1) * BW], xres[c][:, t, :]).then_inc(stored, 16)
            sp.wait_ge(stored, 16 * 2 * NT)

        @block.gpsimd
        def _(pool):
            link = linker(pool, pool_link)
            nsplit = [0]

            def low_parts(upto):
                while nsplit[0] < upto:
                    i = nsplit[0]
                    n = SPLIT[i]
                    size = items[n][2] * items[n][3] - DVE_LO.get(n, 0)
                    pool.wait_ge(hi_done, i + 1)
                    pool.tensor_tensor(w_lo[:, i % NSPL, 0:size], raw[:, n % NRAW, 0:size],
                                       w_hi[:, i % NSPL, 0:size].bitcast(F32), ALU.subtract).then_inc(lo_done, 1)
                    nsplit[0] += 1

            def rsqrt(dst, src, scale, add):
                link(pool.tensor_scalar(dst, src, scale, add, ALU.mult, ALU.add))
                return pool.tensor_tensor(dst, dst, half_pow[:, 0:dst.shape[1]], ALU.pow)

            link(pool.memset(ident[:, :], 0.0))
            pool.affine_select(out=ident[:, :], in_=ident[:, :], compare_op=ALU.not_equal, fill=1.0, base=0,
                               pattern=[[-1, P]], channel_multiplier=1).then_inc(consts, 1)
            pool.memset(half_pow[:, :], -0.5).then_inc(consts, 1)
            pool.wait_ge(consts, 2)
            for t in range(NT):
                pool.wait_ge(ssx_done, t + 1)
                rsqrt(rsx[:, t:t + 1], ssx[:, t:t + 1], 1.0 / D, EPS).then_inc(rsx_done, 1)
            link(pool.memset(mtmp, 0.0))
            pool.affine_select(out=mtmp, in_=mtmp, compare_op=ALU.is_ge, fill=NEG, base=0,
                               pattern=[[-1, P]], channel_multiplier=1).then_inc(maskf, 1)
            low_parts(1)
            pool.wait_ge(maskb, 1)
            link(pool.memset(mtmp, 0.0))
            pool.affine_select(out=mtmp, in_=mtmp, compare_op=ALU.is_ge, fill=NEG, base=-(CMP_LEN - 1),
                               pattern=[[P, NT], [-CMP_STRIDE, CP]], channel_multiplier=1).then_inc(maskf, 1)
            low_parts(2)
            link(pool.memset(has_cmp[:, :], 1.0))
            link(pool.affine_select(out=has_cmp[:, :], in_=has_cmp[:, :], compare_op=ALU.is_ge, fill=0.0,
                                    base=-(CMP_LEN - 1), pattern=[[0, 1]], channel_multiplier=1))
            for i in range(16):
                pool.memset(inv_cnt[:, i:i + 1], 1.0 / (i + 1))
            pool.memset(Vbd[:, :, :], 0.0).then_inc(vbd_zero, 1)
            pool.memset(X.rearrange("p l c g b -> p (l c g) b")[:, :, NCMP:CP], 0.0).then_inc(xpad, 1)
            for k, c in enumerate(CHUNKS1):
                low_parts(splits_through(c))
                if c != "av":
                    pool.wait_ge(ssn_part, NT * (k + 1))
                    scale, add_ = (1.0, DK * EPS) if c == "aq" else (1.0 / DK, EPS)
                    rsqrt(rsn[:, 0:BH * NT], ssn[:, 0:BH * NT], scale, add_).then_inc(rsn_done, 1)
            for s in STEPS:
                for what, a in pool_at[s]:
                    if what == "norm":
                        k = ("bq0", "bq1", "sw0", "sw1").index(a)
                        ng = 16 if k < 2 else 8
                        pool.wait_ge(ssn2_done, k + 1)
                        scale, add_ = (1.0, DK * EPS) if k < 2 else (1.0 / DK, EPS)
                        rsqrt(rsn[:, 0:ng], ssn[:, 0:ng], scale, add_).then_inc(rsn2_done, 1)
                    elif what == "kc":
                        pool.wait_ge(kcs_done, 1)
                        rsqrt(rskc, sskc, 1.0 / DK, EPS).then_inc(kcr_done, 1)
                    elif what == "fin":
                        pool.wait_ge(ss_f, a + 1)
                        rsqrt(rsf, ssf, 1.0 / P, EPS).then_inc(rs_f, 1)
                low_parts(splits_at[s])
            for c in CHUNKS2:
                low_parts(splits_through(c))

        @block.scalar
        def _(act):
            link = linker(act, act_link)
            nsplit = [0]

            def high_parts(upto):
                while nsplit[0] < upto:
                    i = nsplit[0]
                    n = SPLIT[i]
                    size = items[n][2] * items[n][3]
                    wait_raw(act, n)
                    if i >= NSPL:
                        act.wait_ge(split_used, i - NSPL + 1)
                    act.activation(w_hi[:, i % NSPL, 0:size], raw[:, n % NRAW, 0:size], ACT.Copy).then_inc(hi_done, 1)
                    nsplit[0] += 1

            def high_half(i, half):
                n = SPLIT[i]
                size = items[n][2] * items[n][3] // 2
                if half == 0:
                    wait_raw(act, n)
                    if i >= NSPL:
                        act.wait_ge(split_used, i - NSPL + 1)
                ins = act.activation(w_hi[:, i % NSPL, half * size:(half + 1) * size],
                                     raw[:, n % NRAW, half * size:(half + 1) * size], ACT.Copy)
                if half:
                    ins.then_inc(hi_done, 1)
                    nsplit[0] += 1

            for t in range(NT):
                act.dma_start(xt[:, t, :], x[0, t * P:(t + 1) * P, :]).then_inc(x_in[t], 16)
                if t == 0:
                    act.dma_start(gB, bcast(norm_g[0], D)).then_inc(gb_in, 16)
            for i, v in enumerate([a_q_g[0], a_k_g[0], b_q_g[0], b_k_g[0, 0], b_k_g[0, 1], b_k_g[0, 2]]):
                act.dma_start(gains[:, i, :], bcast(v, DK)).then_inc(small_in, 16)
            act.dma_start(subln[:, :], bcast(a_subln_g[0], 2 * DK)).then_inc(small_in, 16)
            act.dma_start(lamv, bass.AP(a_lam.tensor, 0, [[0, P], [DK, 4], [1, DK]])).then_inc(small_in, 16)
            act.dma_start(rows[0:NF, :], c_scale[0].rearrange("(g p) -> g p", p=P)).then_inc(rows_in, 16)
            act.dma_start(rows[NF:NF + 2 * LP, :], b_cmp_pos[0].rearrange("c (l two) d -> (c l) (two d)", two=2)).then_inc(rows_in, 16)
            for c in range(2):
                act.dma_start(w2[:, c, :, :], b_phi_w2[0, c].rearrange("(n p) d -> p n d", p=P)).then_inc(small_in, 16)

            for t in range(NT):
                act.wait_ge(x_in[t], 16)
                if t >= 1:
                    act.wait_ge(ssx_done, t)
                act.activation(sq2, xt[:, t, :], ACT.Square, accum_out=ssx[:, t:t + 1]).then_inc(ssx_done, 1)
            high_parts(1)
            for n in range(2 * NT):
                t, half = n // 2, n % 2
                act.wait_ge(xT_done, n + 1)
                act.activation(h_hi[:, 4 * half:4 * half + 4, t * P:(t + 1) * P],
                               PS[:, n % 8, :].rearrange("p (k s) -> p k s", k=4), ACT.Copy).then_inc(hhi_done, 1)
                if n == 3:
                    high_parts(2)
            act.wait_ge(cols_tr, 1)
            act.activation(cols[:, :], PS[:, 0, 0:NF + 2 * LP], ACT.Copy).then_inc(cols_done, 1)
            act.wait_ge(lam_s, 1)
            act.activation(lame, lam2, ACT.Exp).then_inc(lam_e, 1)

            nsq = 0
            for c in CHUNKS1:
                high_parts(splits_through(c))
                wait_item_used(act, LAST[c])
                b0 = bank0(c)
                for t in range(NT):
                    if c == "av":
                        ins = act.activation(vA[:, t, :], PS[:, b0 + t, :], ACT.Copy)
                        if t == NT - 1:
                            ins.then_inc(drained[PARITY[c]], 1)
                        continue
                    if nsq >= 2:
                        act.wait_ge(ssn_part, nsq - 1)
                    act.activation(gt[:, nsq % 2, :], PS[:, b0 + t, :], ACT.Square).then_inc(sq_done, 1)
                    nsq += 1

            def drain_tr(r):
                n = tr_no(r)
                act.wait_ge(tr_made, n + 1)
                src = PS[:, B_TR, :]
                if r[0] == "kc":
                    act.activation(KC[:, r[1], :], src[:, 0:G * CP], ACT.Copy).then_inc(tr_drained, 1)
                elif r[0] == "ht":
                    hid = src[:, 0:NH2 * P].rearrange("p (n c k) -> p c n k", n=NH2, c=2)
                    act.activation(HTk, hid[:, 0, :, :].unsqueeze(2).broadcast_to([P, NH2, 2, G * CP]), ACT.Copy, scale=0.5)
                    for n in range(NH2):
                        v = hid[:, 1, n, :].rearrange("p (g b) -> p g b", g=G).unsqueeze(2).broadcast_to([P, G, 4, CP])
                        ins = act.activation(HTv[:, n], v, ACT.Copy, scale=0.5)
                    ins.then_inc(tr_drained, 1)
                elif r[0] == "q":
                    _, i, m = hls[r[1]]
                    act.activation(QS[:, 2 * (i % 2) + m, :], src, ACT.Copy).then_inc(tr_drained, 1)
                elif r[0] in ("kh", "kl"):
                    _, i, m = hls[r[1]]
                    par = i % 2 if i < AH else ((i - AH) // HPG) % 2
                    act.activation(KS[:, 4 * par + 2 * m + (r[0] == "kl"), :], src, ACT.Copy).then_inc(tr_drained, 1)
                elif r[0] == "oc":
                    act.activation(OC[:, units[r[1]][1] % 2, :, :].rearrange("p t d -> p (t d)"), src[:, 0:NT * DK],
                                   ACT.Copy).then_inc(tr_drained, 1)
                else:
                    i = r[1]
                    act.activation(U[:, i if i < AH else NF + (i - AH) // 2, :], src, ACT.Copy).then_inc(tr_drained, 1)

            def drain_fill(k):
                kind, name, w = fills[k]
                wait_filled(act, k)
                bank = PS[:, B_F + k % 2, :]
                if kind == "tok":
                    half = int(name[2])
                    b = bank.rearrange("p (t n) -> p t n", t=2)
                    if name[:2] == "bq":
                        act.activation(qB[:, 2 * w:2 * w + 2, half * PC:(half + 1) * PC], b, ACT.Copy).then_inc(act_free, 1)
                    else:
                        act.activation(kB[:, 2 * w:2 * w + 2, half * P:(half + 1) * P], b[:, :, 0:P], ACT.Copy)
                        act.activation(vB[:, 2 * w:2 * w + 2, half * P:(half + 1) * P], b[:, :, P:2 * P],
                                       ACT.Copy).then_inc(act_free, 1)
                elif kind == "cmp":
                    for g in range(G):
                        src = bank[g * DK:(g + 1) * DK, :]
                        act.activation(T2[0:DK, w, g, :], src, ACT.Copy)
                        ins = act.activation(T2[DK:P, w, g, 0:SEQ - 1], src[:, 1:SEQ], ACT.Copy)
                    ins.then_inc(act_free, 1)
                elif kind == "phi":
                    act.wait_ge(x_done, 2)
                    for c in range(2):
                        ins = act.activation(hid_e[c * DK:(c + 1) * DK, :], bank[c * DK:(c + 1) * DK, c * HID:(c + 1) * HID],
                                             ACT.Tanh, scale=0.5)
                    ins.then_inc(e_done, 1)
                elif kind == "bbg":
                    act.activation(gates[:, :, :].rearrange("p t n -> p (t n)"), bank[:, 0:NT * NG], ACT.Tanh,
                                   scale=0.5).then_inc(act_free, 1)
                elif kind in ("ag", "bg"):
                    j = gate_fills.index(k)
                    if j >= 2:
                        act.wait_ge(g_done, j - 1)
                    act.activation(gt[:, j % 2, :], bank, ACT.Tanh, scale=0.5).then_inc(e_done, 1)
                elif kind == "cu":
                    act.activation(U[:, 2 * NF + 2 * int(name[2]) + w, :], bank, ACT.Copy).then_inc(act_free, 1)
                elif kind == "cw":
                    act.activation(U[:, 2 * NF + w, :], bank, ACT.Copy, scale=cols[:, w:w + 1]).then_inc(act_free, 1)

            for s in STEPS:
                if 0 <= s < NU:
                    kind, h, t, m = units[s]
                    if kind == "C":
                        act.wait_ge(csub, h + 1)
                        act.activation(Pr[:, s % 3, 0:P], Pr[:, s % 3, 0:P], ACT.Exp).then_inc(exped, 1)
                    else:
                        wait_place(act, s)
                        W = (t + 1) * P
                        act.wait_ge(maxed, s + 1)
                        o = s % 16 if kind == "A" else m * NT + t + 8 * (h % 2)
                        act.activation(Pr[:, s % 3, 0:W], PS[:, B_S + s % 2, 0:W], ACT.Exp,
                                       bias=negmax[:, s % 8:s % 8 + 1], accum_out=rowsum[:, o:o + 1]).then_inc(exped, 1)
                for what, k in act_at[s]:
                    drain_fill(k)
                for r in trs[s]:
                    drain_tr(r)
                for i, half in highs_at[s]:
                    high_half(i, half)

            k = 0
            for f in range(NF):
                act.wait_ge(u_done, f + 1)
                act.activation(o_hi[NF + f], U[:, NF + f, :], ACT.Copy).then_inc(u_hi, 1)
            for c in CHUNKS2:
                high_parts(splits_through(c))
                if c[0] == "m":
                    wait_item_used(act, "mg" + c[1:])
                elif c == "cg":
                    wait_item_used(act, LAST[c])
                b0 = bank0(c) if c in PARITY else 0
                if c == "cg":
                    for f in range(NF):
                        if f < 2:
                            act.wait_ge(g_done, 2 * NF)
                        else:
                            act.wait_ge(u_done, NF + f - 1)
                        act.activation(gt[:, f % 2, :], PS[:, b0 + f, :], ACT.Silu).then_inc(silu_done, 1)
                        act.wait_ge(u_done, NF + f + 1)
                        act.activation(o_hi[2 * NF + f], U[:, 2 * NF + f, :], ACT.Copy).then_inc(u_hi, 1)
                elif c[0] == "m":
                    k = MI[c]
                    if k >= 2:
                        act.wait_ge(sg_used, k - 1)
                    act.activation(sg[:, k % 2, :], PS[:, b0:b0 + 2, :].rearrange("p a s -> p (a s)"), ACT.Sigmoid).then_inc(sg_done, 1)
                    if c[2] == "2":
                        pr = int(c[1])
                        act.wait_ge(acc_done, k + 1)
                        act.activation(M_hi[:, 2 * pr:2 * pr + 2, :].rearrange("p a s -> p (a s)"), acc, ACT.Copy).then_inc(m_hi, 1)

        @block.vector
        def _(dve):
            link = linker(dve, dve_link)
            nlow = [0]

            def low_parts(upto):
                while nlow[0] < upto:
                    i = nlow[0]
                    n = SPLIT[i]
                    if n in DVE_LO:
                        a, b = items[n][2] * items[n][3] - DVE_LO[n], items[n][2] * items[n][3]
                        dve.wait_ge(hi_done, i + 1)
                        dve.tensor_tensor(w_lo[:, i % NSPL, a:b], raw[:, n % NRAW, a:b],
                                          w_hi[:, i % NSPL, a:b].bitcast(F32), ALU.subtract).then_inc(lo_dve, 1)
                    nlow[0] += 1

            for t in range(NT):
                dve.wait_ge(rsx_done, t + 1)
                if t == 0:
                    dve.wait_ge(gb_in, 16)
                dve.scalar_tensor_tensor(xt[:, t, :], xt[:, t, :], rsx[:, t:t + 1], gB, ALU.mult, ALU.mult).then_inc(xn_done, 1)
            dve.wait_ge(consts, 1)
            dve.tensor_copy(identb[:, :], ident[:, :])
            for n in range(2 * NT):
                t, half = n // 2, n % 2
                dve.wait_ge(hhi_done, n + 1)
                hh = h_hi[:, 4 * half:4 * half + 4, t * P:(t + 1) * P]
                dve.tensor_tensor(h_lo[:, 4 * half:4 * half + 4, t * P:(t + 1) * P],
                                  PS[:, n % 8, :].rearrange("p (k s) -> p k s", k=4), hh.bitcast(F32), ALU.subtract).then_inc(hlo_done, 1)
            dve.wait_ge(maskf, 1)
            dve.tensor_copy(causal[:, :], mtmp).then_inc(maskb, 1)
            dve.wait_ge(maskf, 2)
            dve.tensor_copy(cmask[:, :], mtmp).then_inc(maskb, 1)
            dve.wait_ge(small_in, 16 * 10)
            lv = lamv.rearrange("p (a two) d -> p a two d", two=2)
            link(dve.tensor_tensor(lamt, lv[:, :, 0, :], lv[:, :, 1, :], ALU.mult))
            dve.reduce_sum(lam2, lamt, AX.X).then_inc(lam_s, 1)
            link(dve.tensor_scalar(subln[:, :], subln[:, :], 1.0 - LAM_INIT, None, ALU.mult))
            dve.wait_ge(lam_e, 1)
            link(dve.tensor_scalar(nlam, lame[:, 1:2], lame[:, 0:1], -LAM_INIT, ALU.subtract, ALU.add))

            nsq = 0
            for k, c in enumerate(("aq", "ak")):
                b0 = bank0(c)
                for t in range(NT):
                    dve.wait_ge(sq_done, nsq + 1)
                    dve.reduce_sum(ssn[:, BH * t:BH * (t + 1)], gt[:, nsq % 2, :].rearrange("p (h d) -> p h d", d=DK),
                                   AX.X).then_inc(ssn_part, 1)
                    nsq += 1
                dve.wait_ge(rsn_done, k + 1)
                dst = qkA[:, k]
                for t in range(NT):
                    r = rsn[:, BH * t:BH * (t + 1)].unsqueeze(2).broadcast_to([P, BH, DK])
                    ins = dve.tensor_tensor(dst[:, t, :].rearrange("p (h d) -> p h d", d=DK),
                                            PS[:, b0 + t, :].rearrange("p (h d) -> p h d", d=DK), r, ALU.mult)
                link(ins)
                dve.sem_inc(drained[PARITY[c]], 1)
                v = dst.rearrange("p t (h d) -> p (t h) d", d=DK)
                dve.tensor_tensor(v, v, gains[:, k, :].unsqueeze(1).broadcast_to([P, NT * BH, DK]), ALU.mult).then_inc(tok_done, 1)
            dve.wait_ge(tok_done, 2)

            gates_h = gates[:, :, :].rearrange("p t (h j) -> p t h j", j=3)

            def fill_work(what, a):
                if what == "hl":
                    kind, i, m = hls[a]
                    if i < AH:
                        src = (qA if kind == "q" else kA)[:, :, (2 * i + m) * DK:(2 * i + m + 1) * DK]
                    elif kind == "q":
                        src = qB[:, :, (i - AH) * DK:(i - AH + 1) * DK]
                    else:
                        g = (i - AH) // HPG
                        src = kB[:, :, (m * G + g) * DK:(m * G + g + 1) * DK]
                    before = [k for k in range(a) if hls[k][0] == kind]
                    if before:
                        dve.wait_ge(tr_made, last_tr(before[-1]) + 1)
                    hl = HLq if kind == "q" else HLk
                    link(dve.tensor_copy(hl[:, :, 0, :], src))
                    if kind == "k":
                        dve.tensor_copy(hl[:, :, 2, :], src)
                    dve.tensor_tensor(hl[:, :, 1, :], src, hl[:, :, 0, :].bitcast(F32), ALU.subtract).then_inc(hl_made, 1)
                elif what in ("norm1", "norm2"):
                    k = ("bq0", "bq1", "sw0", "sw1").index(a)
                    v = (qB[:, :, k * PC:(k + 1) * PC] if k < 2 else kB[:, :, (k - 2) * P:(k - 1) * P])
                    ng, n = (16, PC) if k < 2 else (8, P)
                    if what == "norm1":
                        dve.wait_ge(act_free, sum(1 for f in fills[:FILL[("tok", a, 1)] + 1] if f[0] not in DVE_DRAINS))
                        link(dve.tensor_tensor(sq2[:, 0:NT * n].rearrange("p (t n) -> p t n", t=NT), v, v, ALU.mult))
                        link(dve.reduce_sum(ssn[:, 0:ng], sq2[:, 0:NT * n].rearrange("p (h d) -> p h d", d=DK), AX.X))
                        dve.sem_inc(ssn2_done, 1)
                    else:
                        dve.wait_ge(rsn2_done, k + 1)
                        v4 = v.rearrange("p t (h d) -> p t h d", d=DK)
                        sh = [P, NT, n // DK, DK]
                        r = rsn[:, 0:ng].rearrange("p (t h) -> p t h", t=NT).unsqueeze(3).broadcast_to(sh)
                        link(dve.tensor_tensor(v4, v4, r, ALU.mult))
                        gg = gains[:, 2 if k < 2 else 2 + k, :].unsqueeze(1).unsqueeze(1).broadcast_to(sh)
                        link(dve.tensor_tensor(v4, v4, gg, ALU.mult))
                elif what == "x":
                    dve.wait_ge(act_free, sum(1 for f in fills[:FILL[("cmp", "cmp", a)] + 1] if f[0] not in DVE_DRAINS))
                    if a == 0:
                        dve.wait_ge(cols_done, 1)
                        dve.wait_ge(xpad, 1)
                    for g in range(G):
                        base_ = T2[:, a, g, :]
                        src = bass.AP(base_.tensor, base_.offset, [list(base_.ap[0]), [2, LP], [CMP_STRIDE, NCMP]])
                        pos = cols[:, NF + a * LP:NF + (a + 1) * LP].unsqueeze(2).broadcast_to([P, LP, NCMP])
                        ins = dve.tensor_tensor(X[:, :, a, g, 0:NCMP], src, pos, ALU.add)
                    ins.then_inc(x_done, 1)
                elif what == "silu":
                    dve.wait_ge(e_done, 1)
                    for c in range(2):
                        h = hid_e[c * DK:(c + 1) * DK, :]
                        ins = dve.scalar_tensor_tensor(h, h, 1.0, PS[c * DK:(c + 1) * DK, B_F + a % 2, c * HID:(c + 1) * HID],
                                                       ALU.add, ALU.mult)
                    link(ins)
                    dve.sem_inc(dve_free, 1)
                    dve.sem_inc(hid_done, 1)
                elif what == "gates":
                    dve.wait_ge(act_free, sum(1 for f in fills[:a + 1] if f[0] not in DVE_DRAINS))
                    v = gates[:, :, :].rearrange("p t n -> p (t n)")
                    link(dve.tensor_scalar(v, v, 1.0, 0.5, ALU.add, ALU.mult))
                elif what == "kc1":
                    bank = PS[:, B_F + a % 2, :]
                    wait_filled(dve, a)
                    dve.wait_ge(vbd_zero, 1)
                    for g in range(G):
                        for t in range(NT):
                            dve.tensor_copy(Vbd[t * CP:(t + 1) * CP, g, t * DK:(t + 1) * DK],
                                            bank[t * CP:(t + 1) * CP, (1 + g) * DK:(2 + g) * DK])
                    link(dve.tensor_copy(kcn[:, :], bank[:, 0:DK]))
                    dve.sem_inc(dve_free, 1)
                    link(dve.tensor_tensor(kchl[:, 0, :].bitcast(F32), kcn[:, :], kcn[:, :], ALU.mult))
                    link(dve.reduce_sum(sskc, kchl[:, 0, :].bitcast(F32), AX.X))
                    dve.sem_inc(kcs_done, 1)
                elif what == "kc2":
                    dve.wait_ge(kcr_done, 1)
                    link(dve.scalar_tensor_tensor(kcn[:, :], kcn[:, :], rskc, gains[:, 3, :], ALU.mult, ALU.mult))
                    link(dve.tensor_copy(kchl[:, 0, :], kcn[:, :]))
                    dve.tensor_copy(kchl[:, 2, :], kcn[:, :])
                    dve.tensor_tensor(kchl[:, 1, :], kcn[:, :], kchl[:, 0, :].bitcast(F32), ALU.subtract).then_inc(kchl_done, 1)
                elif what == "gate":
                    j = gate_fills.index(a)
                    dve.wait_ge(e_done, 2 + j)
                    v = gt[:, j % 2, :]
                    dst = v if j < NF else gB2[:, j - NF, :]
                    link(dve.scalar_tensor_tensor(dst, v, 1.0, PS[:, B_F + a % 2, :], ALU.add, ALU.mult))
                    dve.sem_inc(dve_free, 1)
                    if j >= NF:
                        dve.sem_inc(g_done, 1)
                elif what == "agate":
                    j = gate_fills.index(a)
                    v = gt[:, j % 2, :]
                    dve.wait_ge(tr_drained, tr_no(("fin", j)) + 1)
                    link(dve.scalar_tensor_tensor(v, v, 0.5, U[:, j, :], ALU.mult, ALU.mult))
                    link(dve.tensor_copy(o_hi[j], v))
                    link(dve.tensor_tensor(o_lo[j], v, o_hi[j].bitcast(F32), ALU.subtract))
                    dve.sem_inc(g_done, 1)
                elif what == "pool":
                    k, g, level = a
                    u = U[:, 2 * NF + g, :]
                    if level == 0:
                        dve.wait_ge(act_free, sum(1 for f in fills[:k + 1] if f[0] not in DVE_DRAINS))
                    if level <= g:
                        width = 1 << level
                        src = u if level == 0 else gB2[:, 2 + (level - 1) % 2, :]
                        dst = gB2[:, 2 + level % 2, :]
                        link(dve.tensor_copy(dst[:, 0:width], src[:, 0:width]))
                        link(dve.tensor_tensor(dst[:, width:SEQ], src[:, width:SEQ], src[:, 0:SEQ - width], ALU.add))
                    else:
                        win = 2 << g
                        src = gB2[:, 2 + g % 2, :]
                        head = gB2[:, 2 + (g + 1) % 2, 0:win - 1]
                        link(dve.tensor_tensor(head, src[:, 0:win - 1], inv_cnt[:, 0:win - 1], ALU.mult))
                        link(dve.tensor_tensor(head, head, u[:, 0:win - 1], ALU.subtract))
                        link(dve.scalar_tensor_tensor(u, src, 1.0 / win, u, ALU.mult, ALU.subtract))
                        link(dve.tensor_copy(u[:, 0:win - 1], head))
                        dve.sem_inc(pooled, 1)

            for s in STEPS:
                if 0 <= s < NU:
                    kind, h, t, m = units[s]
                    dve.wait_ge(scores, s + 1)
                    if kind == "C":
                        wait_place(dve, s)
                        sc = PS[:, B_S + s % 2, 0:P].rearrange("p (t k) -> p t k", t=NT)
                        dve.tensor_reduce(nmc, sc, AX.X, ALU.max, negate=True).then_inc(maxed, 1)
                        dve.wait_ge(maxed, s + 1)
                        dve.tensor_tensor(Pr[:, s % 3, 0:P].rearrange("p (t k) -> p t k", t=NT), sc,
                                          nmc.unsqueeze(2).broadcast_to([P, NT, CP]), ALU.add).then_inc(csub, 1)
                    else:
                        dve.tensor_reduce(negmax[:, s % 8:s % 8 + 1], PS[:, B_S + s % 2, 0:(t + 1) * P], AX.X, ALU.max,
                                          negate=True).then_inc(maxed, 1)
                u = s - 1
                if 0 <= u < NU:
                    kind, h, t, m = units[u]
                    W = (t + 1) * P
                    if kind == "A" and m == 1:
                        a, b = (u - 1) % 16, u % 16
                        dve.wait_ge(exped, u + 1)
                        link(dve.reciprocal(recip[:, a:b + 1], rowsum[:, a:b + 1]))
                        link(dve.tensor_tensor(recip[:, b:b + 1], recip[:, b:b + 1], nlam, ALU.mult))
                        link(dve.tensor_scalar(Pr[:, u % 3, 0:W], Pr[:, u % 3, 0:W], recip[:, b:b + 1], None, ALU.mult))
                        dve.scalar_tensor_tensor(Pr[:, u % 3, 0:W], Pr[:, (u - 1) % 3, 0:W], recip[:, a:a + 1],
                                                 Pr[:, u % 3, 0:W], ALU.mult, ALU.add).then_inc(weighted, 1)
                    elif kind == "C":
                        pc = Pr[:, u % 3, 0:P].rearrange("p (t k) -> p t k", t=NT)
                        dve.wait_ge(exped, u + 1)
                        link(dve.reduce_sum(lc, pc, AX.X))
                        link(dve.reciprocal(fc, lc))
                        link(dve.tensor_tensor(fc, fc, gates_h[:, :, h, 0], ALU.mult))
                        link(dve.tensor_tensor(fc[:, 0:1], fc[:, 0:1], has_cmp[:, :], ALU.mult))
                        dve.tensor_tensor(pc, pc, fc.unsqueeze(2).broadcast_to([P, NT, CP]), ALU.mult).then_inc(weighted, 1)
                u = s - LT
                if u in job_of:
                    j = job_of[u]
                    kind, h, t, m = units[u]
                    W = P if kind == "C" else (t + 1) * P
                    dve.wait_ge(ptd, j + 1)
                    if j >= 2:
                        wait_pv(dve, j - 2)
                    dve.tensor_copy(PTs[:, j % 2, 0:W], PS[:, B_PT + j % 2, 0:W]).then_inc(pt_out, 1)
                ob = PS[:, B_O, :]
                for i in range(NHEAD):
                    if AH <= i and s == last_u[i] + 2:
                        h = i - AH
                        link(dve.reciprocal(fB, rowsum[:, 8 * (h % 2):8 * (h % 2) + 8]))
                        for m in range(2):
                            ins = dve.tensor_tensor(fB[:, m * NT:(m + 1) * NT], fB[:, m * NT:(m + 1) * NT], gates_h[:, :, h, 1 + m], ALU.mult)
                        link(ins)
                    elif AH <= i and s == last_u[i] + LV:
                        wait_pv(dve, job_of[last_u[i] - 1])
                        link(dve.tensor_tensor(wB, ob.rearrange("p (m d) -> p m d", d=DK),
                                               fB.unsqueeze(2).broadcast_to([P, 2 * NT, DK]), ALU.mult))
                        dve.sem_inc(o_free, 1)
                    elif i < AH and s == last_u[i] + LF:
                        wait_pv(dve, job_of[last_u[i]])
                        if i >= 1:
                            dve.wait_ge(tr_made, tr_no(("fin", i - 1)) + 1)
                        link(dve.tensor_copy(OF[:, :, :].rearrange("p t n -> p (t n)"), ob))
                        dve.sem_inc(o_free, 1)
                    elif i < AH and s == last_u[i] + LF + 1:
                        for t in range(NT):
                            link(dve.tensor_tensor_reduce(out=OC[:, 0, 0:2, :].rearrange("p a d -> p (a d)"), in0=OF[:, t, :],
                                                          in1=OF[:, t, :], scale=1.0, scalar=0.0,
                                                          op0=ALU.mult, op1=ALU.add, accum_out=ssf[:, t:t + 1]))
                        dve.sem_inc(ss_f, 1)
                    elif i < AH and s == last_u[i] + LF + 3:
                        dve.wait_ge(rs_f, i + 1)
                        link(dve.tensor_tensor(OF[:, :, :], OF[:, :, :], rsf.unsqueeze(2).broadcast_to([P, NT, P]), ALU.mult))
                        dve.tensor_tensor(OF[:, :, :], OF[:, :, :], subln[:, :].unsqueeze(1).broadcast_to([P, NT, P]),
                                          ALU.mult).then_inc(of_done, 1)
                    elif i >= AH and s == last_u[i] + LF:
                        h = i - AH
                        o = OF[:, :, (h % 2) * DK:(h % 2 + 1) * DK]
                        dve.wait_ge(tr_drained, tr_no(("oc", last_u[i])) + 1)
                        if h % 2 == 0:
                            dve.wait_ge(tr_made, tr_no(("fin", i - 1)) + 1)
                        link(dve.tensor_tensor(o, wB[:, 0:NT, :], wB[:, NT:2 * NT, :], ALU.add))
                        dve.tensor_tensor(o, o, OC[:, h % 2, :, :], ALU.add).then_inc(of_done, 1)
                for what, a in dve_at[s]:
                    fill_work(what, a)

            dve.wait_ge(tr_drained, NTR)
            dve.wait_ge(act_free, sum(1 for f in fills if f[0] not in DVE_DRAINS))
            for f in range(NF):
                link(dve.scalar_tensor_tensor(U[:, NF + f, :], U[:, NF + f, :], 0.5, gB2[:, f, :], ALU.mult, ALU.mult))
                dve.sem_inc(u_done, 1)
                dve.wait_ge(u_hi, f + 1)
                dve.tensor_tensor(o_lo[NF + f], U[:, NF + f, :], o_hi[NF + f].bitcast(F32), ALU.subtract).then_inc(u_lo, 1)
            for c in CHUNKS2:
                low_parts(splits_through(c))
                b0 = bank0(c)
                if c == "cg":
                    for f in range(NF):
                        u = U[:, 2 * NF + f, :]
                        dve.wait_ge(silu_done, f + 1)
                        if f == NF - 1:
                            dve.sem_inc(drained[PARITY[c]], 1)
                        link(dve.tensor_tensor(u, gt[:, f % 2, :], u, ALU.mult))
                        dve.sem_inc(u_done, 1)
                        dve.wait_ge(u_hi, NF + f + 1)
                        dve.tensor_tensor(o_lo[2 * NF + f], u, o_hi[2 * NF + f].bitcast(F32), ALU.subtract).then_inc(u_lo, 1)
                elif c[0] == "m":
                    k = MI[c]
                    dve.wait_ge(sg_done, k + 1)
                    wait_item_used(dve, LAST[c])
                    y = PS[:, b0 + 2:b0 + 4, :].rearrange("p a s -> p (a s)")
                    if c[2] == "0":
                        if k:
                            dve.wait_ge(m_lo, int(c[1]))
                        link(dve.tensor_tensor(acc, sg[:, k % 2, :], y, ALU.mult))
                        dve.sem_inc(drained[PARITY[c]], 1)
                    else:
                        link(dve.tensor_tensor(sg[:, k % 2, :], sg[:, k % 2, :], y, ALU.mult))
                        dve.sem_inc(drained[PARITY[c]], 1)
                        link(dve.tensor_tensor(acc, acc, sg[:, k % 2, :], ALU.add))
                    dve.sem_inc(sg_used, 1)
                    dve.sem_inc(acc_done, 1)
                    if c[2] == "2":
                        pr = int(c[1])
                        dve.wait_ge(m_hi, pr + 1)
                        dve.tensor_tensor(M_lo[:, 2 * pr:2 * pr + 2, :].rearrange("p a s -> p (a s)"), acc,
                                          M_hi[:, 2 * pr:2 * pr + 2, :].rearrange("p a s -> p (a s)").bitcast(F32), ALU.subtract).then_inc(m_lo, 1)
                else:
                    cc = int(c[2])
                    wait_item_used(dve, LAST[c])
                    dve.wait_ge(xres_in[cc], 16)
                    for t in range(NT):
                        dve.tensor_tensor(xres[cc][:, t, :], xres[cc][:, t, :], PS[:, b0 + t, :], ALU.add).then_inc(res_done, 1)

        @block.tensor
        def _(pe):
            pe.wait_ge(consts, 1)
            for n in range(2 * NT):
                t, half = n // 2, n % 2
                if half == 0:
                    pe.wait_ge(xn_done, t + 1)
                for k in range(4):
                    ins = pe.transpose(PS[:, n % 8, k * P:(k + 1) * P], xt[:, t, (4 * half + k) * P:(4 * half + k + 1) * P], ident[:, :])
                ins.then_inc(xT_done, 1)
            pe.wait_ge(rows_in, 32)
            pe.wait_ge(hlo_done, 1)
            NR = NF + 2 * LP
            pe.transpose(PS[:, 0, 0:NR], rows, ident[0:NR, 0:NR]).then_inc(cols_tr, 1)
            pe.wait_ge(hlo_done, 2 * NT)
            pe.wait_ge(cols_done, 1)
            H_hi, H_lo = [h_hi[:, k, :] for k in range(NK)], [h_lo[:, k, :] for k in range(NK)]
            MH, ML = [M_hi[:, k, :] for k in range(NK)], [M_lo[:, k, :] for k in range(NK)]

            def weights(name):
                n = item(name)
                i = SPLIT.index(n)
                wait_low(pe, i)
                _, _, kt, ncol, _ = items[n]
                return [w[:, i % NSPL, 0:kt * ncol].rearrange("p (k n) -> p k n", k=kt) for w in (w_hi, w_lo)]

            def whole(name):
                n = item(name)
                wait_raw(pe, n)
                _, _, kt, ncol, _ = items[n]
                return raw[:, n % NRAW, 0:kt * ncol].rearrange("p (k n) -> p k n", k=kt)

            def three(out_, s_hi, s_lo, m_hi_, m_lo_, start, stop):
                pe.matmul(out_, s_hi, m_hi_, start=start, stop=False)
                pe.matmul(out_, s_hi, m_lo_, start=False, stop=False)
                return pe.matmul(out_, s_lo, m_hi_, start=False, stop=stop)

            def token_major(c, ths, tls, ready):
                pe.wait_ge(drained[PARITY[c]], EARLIER[c])
                b0 = bank0(c)
                for half in range(2):
                    ready(half)
                    wh, wl = weights(f"{c}{half}")
                    for t in range(NT):
                        for k in range(HK):
                            kk = half * HK + k
                            ins = three(PS[:, b0 + t, 0:wh.shape[2]], ths[kk][:, t * P:(t + 1) * P], tls[kk][:, t * P:(t + 1) * P],
                                        wh[:, k, :], wl[:, k, :], kk == 0, kk == NK - 1)
                    ins.then_inc(split_used, 1)

            def feature_major(name, bank, ths, tls):
                wh, wl = weights(name)
                for f in range(2):
                    for k in range(len(ths)):
                        ins = three(PS[:, bank + f, :], wh[:, k, f * P:(f + 1) * P], wl[:, k, f * P:(f + 1) * P],
                                    ths[k], tls[k], k == 0, k == len(ths) - 1)
                ins.then_inc(split_used, 1)

            for c in CHUNKS1:
                token_major(c, H_hi, H_lo, lambda half: None)

            pe.wait_ge(drained[1], 1)
            pe.wait_ge(maskb, 2)

            def fill_piece(k, p):
                kind, name, w = fills[k]
                bank = PS[:, B_F + k % 2, :]
                if p == 0 and k >= 2:
                    wait_bank_read(pe, k - 2)
                used = False
                if kind == "tok":
                    wh, wl = weights(name)
                    t = 2 * w + p // 2
                    for kk in range(HK * (p % 2), HK * (p % 2) + HK):
                        ins = three(bank[:, (p // 2) * PC:(p // 2 + 1) * PC], H_hi[kk][:, t * P:(t + 1) * P],
                                    H_lo[kk][:, t * P:(t + 1) * P], wh[:, kk, :], wl[:, kk, :], kk == 0, kk == NK - 1)
                    used = w == 1 and p == 3
                elif kind in ("cmp", "ag", "cu", "bg"):
                    wh, wl = weights(name)
                    for kk in (2 * p, 2 * p + 1):
                        ins = three(bank, wh[:, kk, w * P:(w + 1) * P], wl[:, kk, w * P:(w + 1) * P], H_hi[kk], H_lo[kk],
                                    kk == 0, kk == NK - 1)
                    used = w == 1 and p == 3
                elif kind == "phi":
                    c, half = p // 4, p // 2 % 2
                    w1 = whole(f"phi{c}{half}")
                    if p == 0:
                        pe.wait_ge(x_done, 2)
                    for l in range(LP // 4 * (p % 4), LP // 4 * (p % 4 + 1)):
                        ins = pe.matmul(bank[:, c * HID:(c + 1) * HID], X[:, l].rearrange("p c g b -> p (c g b)"),
                                        w1[:, l - half * LP // 2, :], start=l == 0, stop=l == LP - 1)
                    if p % 2:
                        ins.then_inc(whole_used, 1)
                elif kind == "bbg":
                    wh, wl = weights(name)
                    for t in (2 * p, 2 * p + 1):
                        for kk in range(NK):
                            ins = three(bank[:, t * NG:(t + 1) * NG], H_hi[kk][:, t * P:(t + 1) * P], H_lo[kk][:, t * P:(t + 1) * P],
                                        wh[:, kk, :], wl[:, kk, :], kk == 0, kk == NK - 1)
                    used = p == 1
                elif kind == "phi2":
                    pe.wait_ge(tr_drained, tr_no(("ht", 0)) + 1)
                    pe.wait_ge(small_in, 16 * 10)
                    for n in range(NH2):
                        pe.matmul(bank[:, 0:DK], HTk[:, n].rearrange("p r c -> p (r c)"), w2[:, 0, n, :], start=n == 0, stop=n == NH2 - 1)
                    for g in range(G):
                        for n in range(NH2):
                            ins = pe.matmul(bank[:, (1 + g) * DK:(2 + g) * DK], HTv[:, n, g].rearrange("p r b -> p (r b)"),
                                            w2[:, 1, n, :], start=n == 0, stop=n == NH2 - 1)
                else:
                    wc = whole("cw")
                    pe.wait_ge(pooled, w + 1)
                    ins = pe.matmul(bank, wc[:, w, :], U[:, 2 * NF + w, :], start=True, stop=True)
                if used:
                    ins.then_inc(split_used, 1)
                elif kind == "cw" and w == NF - 1:
                    ins.then_inc(whole_used, 1)
                elif p == PIECES[kind] - 1 and kind != "phi":
                    ins.then_inc(filled, 1)

            def transpose_tr(r):
                n = tr_no(r)
                if n:
                    pe.wait_ge(tr_drained, n)
                bank = PS[:, B_TR, :]
                if r[0] == "ht":
                    pe.wait_ge(hid_done, 1)
                    for n in range(NH2):
                        ins = pe.transpose(bank[:, n * P:(n + 1) * P], hid_e[:, n * P:(n + 1) * P], ident[:, :])
                    ins.then_inc(tr_made, 1)
                elif r[0] == "kc":
                    pe.wait_ge(kchl_done, 1)
                    src = kchl[:, r[1]:r[1] + 2, :].rearrange("p a d -> p (a d)").bitcast(F32)
                    pe.transpose(bank[:, 0:P], src, ident[:, :]).then_inc(tr_made, 1)
                elif r[0] in ("q", "kh", "kl"):
                    pe.wait_ge(hl_made, r[1] + 1)
                    j = int(r[0] == "kl")
                    for t in range(NT):
                        hl = (HLq if r[0] == "q" else HLk)[:, t, j:j + 2, :].rearrange("p a d -> p (a d)").bitcast(F32)
                        ins = pe.transpose(bank[:, t * P:(t + 1) * P], hl, ident[:, :])
                    ins.then_inc(tr_made, 1)
                elif r[0] == "oc":
                    u = r[1]
                    j = job_of[u]
                    pe.wait_ge(pt_out, j + 1)
                    pe.matmul(bank[:, 0:NT * DK], PTs[:, j % 2, 0:P], Vbd[:, units[u][1] // HPG, :], start=True,
                              stop=True).then_inc(tr_made, 1)
                else:
                    pe.wait_ge(of_done, r[1] + 1)
                    for t in range(NT):
                        ins = pe.transpose(bank[:, t * P:(t + 1) * P], OF[:, t, :], ident[:, :])
                    ins.then_inc(tr_made, 1)

            for s in STEPS:
                pieces = list(fill_at[s])
                if s == 0:
                    pe.wait_ge(drained[0], 2)
                if 0 <= s < NU:
                    kind, h, t, m = units[s]
                    i = head_of[s]
                    if s >= 2:
                        pe.wait_ge(exped, s - 1)
                    if s == first_u[i]:
                        pe.wait_ge(tr_drained, max(tr_no(r) for r in prep(i)) + 1)
                    bank = PS[:, B_S + s % 2, :]
                    if kind == "C":
                        if h == 0:
                            pe.wait_ge(tr_drained, tr_no(("kc", 1)) + 1)
                        q = QS[:, 2 * (i % 2), :]
                        g = h // HPG
                        for tt in range(NT):
                            o = bank[:, tt * CP:(tt + 1) * CP]
                            for a in range(2):
                                pe.matmul(o, q[:, tt * P:(tt + 1) * P], KC[:, a, g * CP:(g + 1) * CP], start=a == 0, stop=False)
                            ins = pe.matmul(o, identb[:, :], cmask[:, tt * CP:(tt + 1) * CP], start=False, stop=True)
                    else:
                        if kind == "A":
                            q, kpos = QS[:, 2 * (i % 2) + m, :], 4 * (i % 2) + 2 * m
                        else:
                            q, kpos = QS[:, 2 * (i % 2), :], 4 * ((h // HPG) % 2) + 2 * m
                        W = (t + 1) * P
                        for a in range(2):
                            pe.matmul(bank[:, 0:W], q[:, t * P:(t + 1) * P], KS[:, kpos + a, 0:W], start=a == 0, stop=False)
                        ins = pe.matmul(bank[:, t * P:W], identb[:, :], causal[:, :], start=False, stop=True)
                    ins.then_inc(scores, 1)
                if pieces:
                    fill_piece(*pieces.pop(0))
                u = s - LT
                if u in job_of:
                    j = job_of[u]
                    kind, h, t, m = units[u]
                    if kind == "B":
                        pe.wait_ge(exped, u + 1)
                    else:
                        pe.wait_ge(weighted, weighted_no(u))
                    if j >= 2:
                        pe.wait_ge(pt_out, j - 1)
                    for kb in range(1 if kind == "C" else t + 1):
                        ins = pe.transpose(PS[:, B_PT + j % 2, kb * P:(kb + 1) * P], Pr[:, u % 3, kb * P:(kb + 1) * P], ident[:, :])
                    ins.then_inc(ptd, 1)
                u = s - LV
                if u in job_of and units[u][0] != "C":
                    j = job_of[u]
                    kind, h, t, m = units[u]
                    i = head_of[u]
                    pe.wait_ge(pt_out, j + 1)
                    if i >= 1 and u == first_pv[i]:
                        pe.wait_ge(o_free, i)
                    for kb in range(t + 1):
                        lhs = PTs[:, j % 2, kb * P:(kb + 1) * P]
                        if kind == "A":
                            ins = pe.matmul(PS[:, B_O, t * P:(t + 1) * P], lhs, vA[:, kb, h * P:(h + 1) * P], start=kb == 0, stop=kb == t)
                        else:
                            g = h // HPG
                            o = (m * NT + t) * DK
                            ins = pe.matmul(PS[:, B_O, o:o + DK], lhs, vB[:, kb, (m * G + g) * DK:(m * G + g + 1) * DK],
                                            start=kb == 0, stop=kb == t)
                    ins.then_inc(pv_done, 1)
                for r in trs[s]:
                    transpose_tr(r)
                for piece in pieces:
                    fill_piece(*piece)

            pe.wait_ge(pt_out, len(jobs))
            for c in CHUNKS2:
                b0 = bank0(c)
                if c == "cg":
                    for half in range(2):
                        feature_major(f"cg{half}", b0 + 2 * half, H_hi, H_lo)
                    pe.wait_ge(tr_drained, NTR)
                    pe.wait_ge(o_free, NHEAD)
                    wait_bank_read(pe, NFILL - 2)
                    wait_bank_read(pe, NFILL - 1)
                elif c[0] == "m":
                    pe.wait_ge(drained[PARITY[c]], EARLIER[c])
                    b = int(c[2])
                    feature_major("mg" + c[1:], b0, H_hi, H_lo)
                    if b:
                        pe.wait_ge(u_lo, b * NF)
                    feature_major("wb" + c[1:], b0 + 2, o_hi[b * NF:(b + 1) * NF], o_lo[b * NF:(b + 1) * NF])
                else:
                    token_major(c, MH, ML, lambda half: pe.wait_ge(m_lo, (half + 1) * NP // 2))


_INS = ['x', 'norm_g', 'w_in', 'a_q_g', 'a_k_g', 'a_lam', 'a_subln_g', 'b_q_g', 'b_k_g', 'b_cmp_pos',
        'b_phi_w1', 'b_phi_w2', 'c_w', 'c_scale', 'w_branch', 'w_out']


def kernel(**inputs):
    import numpy as _np
    import concourse.bacc as _bacc
    from concourse import mybir as _mybir
    from concourse.bass_utils import run_bass_kernel_spmd as _run

    nc = _bacc.Bacc("TRN2", target_bir_lowering=False, num_devices=1)
    arrays, args = {}, []
    for name in _INS:
        a = _np.ascontiguousarray(inputs[name])
        arrays[f"in_{name}_dram"] = a
        args.append(nc.dram_tensor(f"in_{name}_dram", a.shape, _mybir.dt.from_np(a.dtype), kind="ExternalInput").ap())
    shape = arrays["in_x_dram"].shape
    args.append(nc.dram_tensor("out_0_dram", shape, _mybir.dt.float32, kind="ExternalOutput").ap())
    hybrid_trunk_kernel(nc, *args)
    r = _run(nc, [arrays], core_ids=[0])
    return r.results[0]["out_0_dram"]
```

```python
import math
from contextlib import ExitStack

import concourse.bass as bass
from concourse import mybir


def hybrid_trunk_kernel(nc: bass.Bass, x, norm_g, w_in, a_q_g, a_k_g, a_lam, a_subln_g, b_q_g, b_k_g,
                        b_cmp_pos, b_phi_w1, b_phi_w2, c_w, c_scale, w_branch, w_out, out):
    F32, F32R, BF16 = mybir.dt.float32, mybir.dt.float32r, mybir.dt.bfloat16
    ALU, ACT, AX = mybir.AluOpType, mybir.ActivationFunctionType, mybir.AxisListType
    P = 128
    _, SEQ, D = x.shape
    EPS, NEG = 1e-6, -1e30
    NT = SEQ // P
    NK = D // P
    BW = w_branch.shape[2]
    NF = BW // P
    DK = a_q_g.shape[1]
    AH = BW // (2 * DK)
    BH = BW // DK
    G = 2
    HPG = BH // G
    CMP_LEN, CMP_STRIDE = b_cmp_pos.shape[2], 16
    NCMP = (SEQ - CMP_LEN) // CMP_STRIDE + 1
    CP = 32
    LP = CMP_LEN // 2
    HID = b_phi_w1.shape[3]
    NH2 = HID // P
    LAM_INIT = 0.8 - 0.6 * math.exp(-0.3 * 0)

    C_AQ, C_AK, C_AV, C_AG = 0, BW, 2 * BW, 3 * BW
    C_BQ = 4 * BW
    C_KV = 5 * BW
    C_CMP, C_SW = C_KV, C_KV + 4 * DK
    C_BBG = C_KV + 12 * DK
    NG = 3 * BH
    C_BG = C_BBG + NG
    C_CU, C_CG = C_BG + BW, C_BG + 2 * BW
    C_MG = C_BG + 3 * BW

    win_k = w_in[0].rearrange("(k p) n -> p k n", p=P)
    wout_k = w_out[0].rearrange("(k p) n -> p k n", p=P)
    wbr_k = [w_branch[0, b].rearrange("(k p) n -> p k n", p=P) for b in range(3)]
    w1_k = [b_phi_w1[0, c].rearrange("(l p) n -> p l n", p=P) for c in range(2)]
    HK = NK // 2
    SLOT = HK * BW
    PC = 2 * P
    items = []

    def add(name, view, kt, cols, split=True):
        items.append((name, view, kt, cols, split))

    def add_halves(name, view, c0):
        for half in range(2):
            add(f"{name}{half}", view[:, half * HK:(half + 1) * HK, c0:c0 + BW], HK, BW)

    def add_pairs(name, c0):
        for half in range(2):
            add(f"{name}{half}", win_k[:, :, c0 + half * PC:c0 + (half + 1) * PC], NK, PC)

    add_halves("aq", win_k, C_AQ)
    add_halves("ak", win_k, C_AK)
    add_halves("av", win_k, C_AV)
    add_pairs("bq", C_BQ)
    add_pairs("sw", C_SW)
    add("cmp", win_k[:, :, C_CMP:C_CMP + PC], NK, PC)
    for c in range(2):
        for half in range(2):
            add(f"phi{c}{half}", w1_k[c][:, half * LP // 2:(half + 1) * LP // 2, :], LP // 2, HID, False)
    add("bbg", win_k[:, :, C_BBG:C_BBG + NG], NK, NG)
    add_pairs("ag", C_AG)
    add_pairs("cu", C_CU)
    add_pairs("bg", C_BG)
    add("cw", c_w[0].rearrange("g c d -> c g d"), NF, P, False)
    add_pairs("cg", C_CG)
    NP = D // PC
    for pr in range(NP):
        for b in range(3):
            add(f"mg{pr}{b}", win_k[:, :, C_MG + b * D + pr * PC:C_MG + b * D + (pr + 1) * PC], NK, PC)
            add(f"wb{pr}{b}", wbr_k[b][:, :, pr * PC:(pr + 1) * PC], NF, PC)
    for c in range(2):
        add_halves(f"wo{c}", wout_k, c * BW)
    NAMES = [i[0] for i in items]
    SPLIT = [n for n, i in enumerate(items) if i[4]]
    WHOLE = [n for n, i in enumerate(items) if not i[4]]
    NRAW, NSPL = 3, 2

    def item(name):
        return NAMES.index(name)

    units = []
    for h in range(AH):
        units += [("A", h, t, m) for t in range(NT) for m in range(2)]
    for h in range(BH):
        units += [("B", h, t, m) for m in range(2) for t in range(NT)] + [("C", h, 0, 0)]
    NU = len(units)
    jobs = [u for u, (kind, _, _, m) in enumerate(units) if kind != "A" or m == 1]
    job_of = {u: j for j, u in enumerate(jobs)}
    NHEAD = AH + BH
    head_of = [h if kind == "A" else AH + h for kind, h, _, _ in units]
    first_u = [head_of.index(i) for i in range(NHEAD)]
    last_u = [NU - 1 - head_of[::-1].index(i) for i in range(NHEAD)]
    first_pv = [next(u for u in jobs if head_of[u] == i) for i in range(NHEAD)]
    LT, LV, LF = 2, 3, 4
    S0, NSTEP = -8, NU + LF + 4
    STEPS = range(S0, NSTEP)

    hls, head_hl = [], {}
    for i in range(NHEAD):
        if i < AH:
            mine = [("q", i, 0), ("k", i, 0), ("q", i, 1), ("k", i, 1)]
        else:
            mine = [("q", i, 0)]
            if (i - AH) % HPG == 0:
                mine += [("k", i, 0), ("k", i, 1)]
        head_hl[i] = list(range(len(hls), len(hls) + len(mine)))
        hls += mine

    def prep(i):
        return [(hls[k][0], k) for k in head_hl[i]]

    fills = []
    for name in ("bq", "sw"):
        fills += [("tok", f"{name}{half}", tp) for half in range(2) for tp in range(2)]
    fills += [("cmp", "cmp", kv) for kv in range(2)]
    fills += [("phi", "phi", 0), ("bbg", "bbg", 0), ("phi2", "phi2", 0)]
    NEARLY = len(fills)
    for name in ("ag", "cu", "bg"):
        fills += [(name, f"{name}{half}", f) for half in range(2) for f in range(2)]
    fills += [("cw", "cw", g) for g in range(NF)]
    fills += [("cg", f"cg{half}", f) for half in range(2) for f in range(2)]
    NFILL = len(fills)
    FIRST_CW = fills.index(("cw", "cw", 0))
    PIECES = {"tok": 4, "cmp": 4, "phi": 8, "bbg": 2, "phi2": 1, "ag": 4, "cu": 4, "bg": 4, "cw": 1, "cg": 4}
    DVE_DRAINS = ("phi", "phi2", "ag", "bg", "cg")

    def item_of(kind, name, p):
        return None if kind == "phi2" else item(f"phi{p // 4}{p // 2 % 2}" if kind == "phi" else name)

    def drain_step(k):
        return fill_end[k] + (2 if fills[k][0] in DVE_DRAINS else 1)

    fill_at = {s: [] for s in STEPS}
    fill_end = {}
    used_step = {}
    first_split = sum(1 for n in SPLIT if n <= item("av1")) + NSPL

    def split_step(n):
        i = SPLIT.index(n)
        if i < first_split:
            return S0
        return 1 + max(used_step.get(NAMES[w], S0) for w in [SPLIT[i - NSPL]] + [w for w in WHOLE if w <= n - NRAW])

    def high_step(i):
        return max(split_step(SPLIT[i]), high_step(i - 1) + 2 if i > first_split else S0)
    s, room = S0, 0.0
    RATE_A, RATE_B = 1.37, 0.92
    for k, (kind, name, _) in enumerate(fills):
        for p in range(PIECES[kind]):
            while True:
                ok = room >= 1
                if item_of(kind, name, p) in SPLIT:
                    i = SPLIT.index(item_of(kind, name, p))
                    ok = ok and (i < first_split or s > high_step(i) + 2)
                if p == 0 and k >= 2:
                    ok = ok and s > drain_step(k - 2)
                if kind == "phi" and p == 0:
                    ok = ok and s > fill_end[k - 1] + 2
                if kind == "phi2":
                    ok = ok and s > fill_end[k - 2] + 4
                if kind == "ag" and p == 0:
                    ok = ok and s > last_u[AH - 1] - 1
                if kind == "cw":
                    ok = ok and s > fill_end[k - 2 * NF] + 4 + k - FIRST_CW
                if ok:
                    break
                s += 1
                room = min(room, 1.5) + (RATE_A if k < NEARLY else RATE_B)
            fill_at[s].append((k, p))
            if kind != "phi2":
                used_step[NAMES[item_of(kind, name, p)]] = s
            room -= 1
        fill_end[k] = s
    gate_fills = [k for k, f in enumerate(fills) if f[0] in ("ag", "bg", "cg")]
    FILL = {f: k for k, f in enumerate(fills)}

    trs = {s: [] for s in STEPS}
    for i in range(NHEAD):
        s0, apart = (first_u[i - 1] + 3, 1) if i else (S0 + 2, 1)
        for n, r in enumerate(prep(i)):
            trs[s0 + n * apart].append(r)
    trs[fill_end[FILL[("phi", "phi", 0)]] + 3].append(("ht", 0))
    trs[fill_end[FILL[("bbg", "bbg", 0)]] + 2].append(("gates", 0))
    KC_STEP = fill_end[FILL[("phi2", "phi2", 0)]] + 4
    trs[KC_STEP].append(("kc", 0))
    trs[KC_STEP + 1].append(("kc", 1))
    for u, (kind, h, _, _) in enumerate(units):
        if kind == "C":
            trs[u + LV].append(("oc", u))
    for i in range(NHEAD):
        if i < AH or (i - AH) % 2:
            trs[last_u[i] + LF + (4 if i < AH else 1)].append(("fin", i))
    tr_list = [(s, r) for s in STEPS for r in trs[s]]
    tr_step = {r: s for s, r in tr_list}
    NTR = len(tr_list)

    def tr_no(r):
        return next(n for n, (_, q) in enumerate(tr_list) if q == r)

    def last_tr(k):
        return tr_no((hls[k][0], k))

    dve_at = {s: [] for s in STEPS}
    act_at = {s: [] for s in STEPS}
    pool_at = {s: [] for s in STEPS}
    for k in range(len(hls)):
        dve_at[tr_step[(hls[k][0], k)] - 1].append(("hl", k))
    for k, (kind, name, w) in enumerate(fills):
        e = fill_end[k]
        act_at[e + 1].append(("drain", k))
        if kind == "tok" and w == 1:
            dve_at[e + 2].append(("norm1", name))
            pool_at[e + 2].append(("norm", name))
            dve_at[e + 5].append(("norm2", name))
        if kind == "cmp":
            dve_at[e + 2].append(("x", w))
        if kind == "phi":
            dve_at[e + 2].append(("silu", k))
        if kind == "bbg":
            dve_at[e + 4].append(("gates", k))
        if kind == "phi2":
            dve_at[e + 2].append(("kc1", k))
            pool_at[e + 2].append(("kc", k))
            dve_at[e + 3].append(("kc2", k))
        if kind in ("ag", "bg", "cg"):
            dve_at[e + 2].append(("gate", k))
        if kind == "ag":
            dve_at[e + 3].append(("agate", k))
        if kind == "cu":
            g = 2 * int(name[2]) + w
            for level in range(g + 2):
                dve_at[e + 2 + level].append(("pool", (k, g, level)))
    for i in range(AH):
        act_at[last_u[i] + LF + 1].append(("squares", i))
        pool_at[last_u[i] + LF + 1].append(("fin", i))
    in_steps = sum(1 for n in SPLIT if n <= item("cg1")) + NSPL
    splits_at = {s: max([first_split] + [i + 1 for i in range(in_steps) if high_step(i) + 1 <= s]) for s in STEPS}
    highs_at = {s: [] for s in STEPS}
    for i in range(first_split, in_steps):
        for half in range(2):
            highs_at[high_step(i) + half].append((i, half))

    ctx = ExitStack()
    with ctx:
        def sem(name):
            return ctx.enter_context(nc.semaphore(name))

        def sb(name, shape, dt, c=ctx):
            return c.enter_context(nc.sbuf_tensor(name, shape, dt))

        h_hi = sb("h_hi", [P, NK, SEQ], F32R)
        h_lo = sb("h_lo", [P, NK, SEQ], F32R)
        raw = sb("raw", [P, NRAW, SLOT], F32)
        w_hi = sb("w_hi", [P, NSPL, SLOT], F32R)
        w_lo = sb("w_lo", [P, NSPL, SLOT], F32R)
        U = sb("U", [P, 3 * NF, SEQ], F32)
        gt = sb("gt", [P, 2, SEQ], F32)
        ident = sb("ident", [P, P], F32)
        identb = sb("identb", [P, P], BF16)
        causal = sb("causal", [P, P], BF16)
        cmask = sb("cmask", [P, NT * CP], BF16)
        gains = sb("gains", [P, 6, DK], F32)
        subln = sb("subln", [P, 2 * DK], F32)
        cols = sb("cols", [P, NF + 2 * LP], F32)
        Vbd = sb("Vbd", [P, G, NT * DK], F32)
        KC = sb("KC", [P, 2, G * CP], F32R)
        gates = sb("gates", [P, NT, NG], F32)
        st = sb("st", [P, 156], F32)
        half_pow = sb("half_pow", [P, 32], F32)
        inv_cnt = sb("inv_cnt", [P, 16], F32)
        has_cmp = sb("has_cmp", [P, 1], F32)

        early = ExitStack()
        qkA = sb("qkA", [P, 2, NT, BW], F32, early)
        early.close()
        oA_hi = sb("oA_hi", [P, NF, SEQ], F32R)
        oA_lo = sb("oA_lo", [P, NF, SEQ], F32R)

        early = ExitStack()
        tok = sb("tok", [P, 3 * NT * BW], F32, early)
        QS = sb("QS", [P, 4, SEQ], F32R, early)
        KS = sb("KS", [P, 8, SEQ], F32R, early)
        PTs = sb("PTs", [P, 2, SEQ], F32, early)
        HLq = sb("HLq", [P, NT, 2, DK], F32R, early)
        HLk = sb("HLk", [P, NT, 2, DK], F32R, early)
        OF = sb("OF", [P, NT, P], F32, early)
        Pr = sb("Pr", [P, 3, SEQ], F32, early)
        OC = sb("OC", [P, 2, NT, DK], F32, early)
        kchl = sb("kchl", [P, 3, DK], F32R, early)
        kcn = sb("kcn", [P, DK], F32, early)
        early.close()
        M_hi = sb("M_hi", [P, NK, SEQ], F32R)
        M_lo = sb("M_lo", [P, NK, SEQ], F32R)
        oB_hi = sb("oB_hi", [P, 2 * NF, SEQ], F32R)
        oB_lo = sb("oB_lo", [P, 2 * NF, SEQ], F32R)
        o_hi = [oA_hi[:, f, :] for f in range(NF)] + [oB_hi[:, f, :] for f in range(2 * NF)]
        o_lo = [oA_lo[:, f, :] for f in range(NF)] + [oB_lo[:, f, :] for f in range(2 * NF)]
        acc = U[:, 0:2, :].rearrange("p a s -> p (a s)")
        sg = U[:, 2:6, :].rearrange("p (b a) s -> p b (a s)", b=2)
        xres = [U[:, 8:12, :], U[:, 4:8, :]]

        def region(a, n):
            return tok[:, a * NT * BW // 2:(a + n) * NT * BW // 2]
        qA, kA = qkA[:, 0], qkA[:, 1]
        vA = region(0, 2).rearrange("p (t n) -> p t n", t=NT)
        gB2 = vA
        qB = region(2, 2).rearrange("p (t n) -> p t n", t=NT)
        kB = region(4, 1).rearrange("p (t n) -> p t n", t=NT)
        vB = region(5, 1).rearrange("p (t n) -> p t n", t=NT)
        gB = qkA[:, 0, 0:2, :].rearrange("p t n -> p (t n)")
        xt = region(0, 4).rearrange("p (t n) -> p t n", t=NT)
        lamv = PTs[:, 0, 0:4 * DK].rearrange("p (a d) -> p a d", a=4)
        rows = PTs[0:NF + 2 * LP, 0, 2 * P:3 * P]
        mtmp = PTs[:, 0, 3 * P:4 * P]
        lamt = PTs[:, 1, 0:2 * DK].rearrange("p (a d) -> p a d", a=2)
        w2 = U[:, 3, 0:2 * NH2 * DK].rearrange("p (c n d) -> p c n d", c=2, n=NH2)
        T2 = U[:, 4:8, :].rearrange("p (c g) s -> p c g s", c=2)
        X = U[:, 8:12, :].rearrange("p c s -> p (c s)").rearrange("p (l c g b) -> p l c g b", c=2, l=LP, g=G)
        gT = U[0:NG, 6, :]
        T2f = U[:, 4:8, :].rearrange("p c s -> p (c s)")
        NH = HID
        hid_e = T2f[:, 0:NH]
        HTk = T2f[:, NH:NH + NH2 * P].rearrange("p (n r c) -> p n r c", n=NH2, r=2)
        HTv = T2f[:, NH + NH2 * P:NH + 3 * NH2 * P].rearrange("p (n g r b) -> p n g r b", n=NH2, g=G, r=4)
        wB = U[:, 2 * NF - 1, :].rearrange("p (m d) -> p m d", d=DK)
        sq2 = gt[:, :, :].rearrange("p a s -> p (a s)")
        PS = ctx.enter_context(nc.psum_tensor("PS", [P, 8, 512], F32))
        B_S, B_PT, B_TR, B_O, B_F = 0, 2, 4, 5, 6

        ssx, rsx = st[:, 0:4], st[:, 4:8]
        ssn, rsn = st[:, 8:40], st[:, 40:72]
        sskc, rskc = st[:, 72:73], st[:, 73:74]
        lam2, lame, nlam = st[:, 74:76], st[:, 76:78], st[:, 78:79]
        negmax = st[:, 80:88]
        rowsum = st[:, 88:104]
        recip = st[:, 104:120]
        nmc, lc, fc = st[:, 120:124], st[:, 124:128], st[:, 128:132]
        ssf, rsf = st[:, 132:136], st[:, 136:140]
        fB = st[:, 140:148]
        rs0 = st[:, 148:152]

        raw_in = [sem(f"raw_in{i}") for i in range(NRAW)]
        x_in = [sem(f"x_in{i}") for i in range(NT)]
        gb_in, small_in, rows_in = sem("gb_in"), sem("small_in"), sem("rows_in")
        xres_in = [sem("xres_in0"), sem("xres_in1")]
        stored = sem("stored")
        hi_done, lo_done, lo_dve, split_used, whole_used = (sem(n) for n in (
            "hi_done", "lo_done", "lo_dve", "split_used", "whole_used"))
        consts, maskf, maskb, ssx_done, rsx_done, xn_done = (sem(n) for n in (
            "consts", "maskf", "maskb", "ssx_done", "rsx_done", "xn_done"))
        xT_done, hhi_done, hlo_done, cols_tr, cols_done, vbd_zero, xpad = (sem(n) for n in (
            "xT_done", "hhi_done", "hlo_done", "cols_tr", "cols_done", "vbd_zero", "xpad"))
        lam_s, lam_e = sem("lam_s"), sem("lam_e")
        drained = [sem("drained0"), sem("drained1")]
        sq_done, ssn_part, rsn_done = sem("sq_done"), sem("ssn_part"), sem("rsn_done")
        filled, act_free, dve_free = sem("filled"), sem("act_free"), sem("dve_free")
        ssn2_done, rsn2_done, x_done, hid_done, kcs_done, kcr_done, kchl_done = (sem(n) for n in (
            "ssn2_done", "rsn2_done", "x_done", "hid_done", "kcs_done", "kcr_done", "kchl_done"))
        e_done, g_done, pooled = sem("e_done"), sem("g_done"), sem("pooled")
        hl_made, tr_made, tr_drained = sem("hl_made"), sem("tr_made"), sem("tr_drained")
        scores, maxed, exped, weighted = sem("scores"), sem("maxed"), sem("exped"), sem("weighted")
        csub, ptd, pt_out, pv_done = sem("csub"), sem("ptd"), sem("pt_out"), sem("pv_done")
        ss_f, rs_f, of_done, o_free = sem("ss_f"), sem("rs_f"), sem("of_done"), sem("o_free")
        u_done, u_hi, u_lo = sem("u_done"), sem("u_hi"), sem("u_lo")
        wo_tile, passed = sem("wo_tile"), sem("passed")
        sg_done, sg_used, y_done, acc_done, m_hi, m_lo, res_done = (sem(n) for n in (
            "sg_done", "sg_used", "y_done", "acc_done", "m_hi", "m_lo", "res_done"))
        dve_link, act_link, pool_link = sem("dve_link"), sem("act_link"), sem("pool_link")

        CHUNKS1 = ["aq", "ak", "av"]
        PARITY = {c: n % 2 for n, c in enumerate(CHUNKS1)}
        EARLIER = {c: n // 2 for n, c in enumerate(CHUNKS1)}
        LAST = {"aq": "aq1", "ak": "ak1", "av": "av1"}
        MERGE0 = item("mg00")
        SPLIT_M = SPLIT.index(MERGE0)
        PER_PAIR = 6
        WO_BANK = [4, 0]
        assert PER_PAIR % NRAW == 0 and PER_PAIR % NSPL == 0

        def bank0(c):
            return 4 * PARITY[c]

        def bcast(v, n):
            return bass.AP(v.tensor, v.offset, [[0, P], [1, n]])

        def splits_through(c):
            return min(sum(1 for n in SPLIT if n <= item(LAST[c])) + NSPL, len(SPLIT))

        DVE_LO = {n: 1408 for n in SPLIT if NAMES[n][:2] in ("mg", "aq", "wo")}
        LO_M = sum(1 for n in DVE_LO if n < MERGE0)


        def wait_item_used(eng, name):
            n = item(name)
            if n in SPLIT:
                eng.wait_ge(split_used, SPLIT.index(n) + 1)
            else:
                eng.wait_ge(whole_used, WHOLE.index(n) + 1)

        def wait_low(eng, i):
            eng.wait_ge(lo_done, i + 1)
            if SPLIT[i] in DVE_LO:
                eng.wait_ge(lo_dve, sum(1 for n in DVE_LO if n <= SPLIT[i]))

        def wait_at(eng, what, value):
            eng.wait_ge(what, value)
            eng.sem_inc(passed, 1)

        def merge_low(eng, pr, r):
            wait_at(eng, lo_done, pr * PER_PAIR + (SPLIT_M + r + 1))
            if r % 2 == 0:
                wait_at(eng, lo_dve, pr * 3 + (LO_M + r // 2 + 1))

        def merge_used(eng, pr, r):
            wait_at(eng, split_used, pr * PER_PAIR + (SPLIT_M + r + 1))

        def merge_size(r):
            return (NF * PC, 0) if r % 2 else (SLOT, 1408)

        def wait_pv(eng, j):
            if units[jobs[j]][0] == "C":
                eng.wait_ge(tr_made, tr_no(("oc", jobs[j])) + 1)
            else:
                eng.wait_ge(pv_done, sum(1 for v in jobs[:j + 1] if units[v][0] != "C"))

        def wait_bank_read(eng, k):
            mine = fills[k][0] in DVE_DRAINS
            eng.wait_ge(dve_free if mine else act_free, sum(1 for f in fills[:k + 1] if (f[0] in DVE_DRAINS) == mine))

        def ends_item(k):
            kind, _, w = fills[k]
            return kind == "phi" or kind == "bbg" or (kind == "cw" and w == NF - 1) or \
                (kind in ("tok", "cmp", "ag", "cu", "bg", "cg") and w == 1)

        def wait_filled(eng, k):
            kind, name, _ = fills[k]
            if ends_item(k):
                wait_item_used(eng, f"phi1{NH2 - 1}" if kind == "phi" else name)
            else:
                eng.wait_ge(filled, sum(1 for q in range(k + 1) if not ends_item(q)))

        def wait_place(eng, s):
            if s >= 3:
                kind, _, _, m = units[s - 3]
                if kind == "A" and m == 0:
                    eng.wait_ge(weighted, weighted_no(s - 2))
                else:
                    eng.wait_ge(ptd, job_of[s - 3] + 1)

        def weighted_no(u):
            return sum(1 for v in jobs[:job_of[u] + 1] if units[v][0] != "B")

        def linker(eng, s):
            n = [0]

            def link(ins):
                n[0] += 1
                ins.then_inc(s, 1)
                eng.wait_ge(s, n[0])
            return link

        def wait_raw(eng, n):
            eng.wait_ge(raw_in[n % NRAW], 16 * (n // NRAW + 1))

        block = ctx.enter_context(nc.Block())

        @block.sync
        def _(sp):
            def load_x(t):
                sp.dma_start(xt[:, t, :], x[0, t * P:(t + 1) * P, :]).then_inc(x_in[t], 16)

            load_x(0)
            sp.dma_start(gB, bcast(norm_g[0], D)).then_inc(gb_in, 16)
            def load(n):
                name, view, kt, ncol, split = items[n]
                if n == 1:
                    for t in range(1, NT):
                        load_x(t)
                if n == NRAW:
                    for i, v in enumerate([a_q_g[0], a_k_g[0], b_q_g[0], b_k_g[0, 0], b_k_g[0, 1], b_k_g[0, 2]]):
                        sp.dma_start(gains[:, i, :], bcast(v, DK)).then_inc(small_in, 16)
                    sp.dma_start(subln[:, :], bcast(a_subln_g[0], 2 * DK)).then_inc(small_in, 16)
                    sp.dma_start(lamv, bass.AP(a_lam.tensor, 0, [[0, P], [DK, 4], [1, DK]])).then_inc(small_in, 16)
                    sp.dma_start(rows[0:NF, :], c_scale[0].rearrange("(g p) -> g p", p=P)).then_inc(rows_in, 16)
                    sp.dma_start(rows[NF:NF + 2 * LP, :], b_cmp_pos[0].rearrange("c (l two) d -> (c l) (two d)", two=2)).then_inc(rows_in, 16)
                    for c in range(2):
                        sp.dma_start(w2[:, c, :, :], b_phi_w2[0, c].rearrange("(n p) d -> p n d", p=P)).then_inc(small_in, 16)
                if n >= NRAW:
                    if n - NRAW in SPLIT:
                        wait_low(sp, SPLIT.index(n - NRAW))
                    else:
                        sp.wait_ge(whole_used, WHOLE.index(n - NRAW) + 1)
                dst = raw[:, n % NRAW, 0:kt * ncol].rearrange("p (k n) -> p k n", k=kt)
                sp.dma_start(dst, view).then_inc(raw_in[n % NRAW], 16)

            for n in range(MERGE0 + PER_PAIR):
                load(n)
            with sp.Fori(1, NP) as pr:
                lows = [sp.snap(pr * PER_PAIR + (SPLIT_M + r - NRAW + 1)) for r in range(PER_PAIR)]
                low_shares = [sp.snap(pr * 3 + (LO_M + n)) for n in range(3)]
                col = sp.snap(pr * PC)
                for r in range(PER_PAIR):
                    wait_at(sp, lo_done, lows[r])
                    if (r - NRAW) % 2 == 0:
                        wait_at(sp, lo_dve, low_shares[(r - NRAW) // 2 + 1])
                    b = r // 2
                    if r % 2 == 0:
                        first = C_MG + b * D
                        view, kt = win_k[:, :, first:first + D][:, :, bass.ds(col, PC)], NK
                    else:
                        view, kt = wbr_k[b][:, :, bass.ds(col, PC)], NF
                    slot = (MERGE0 + r) % NRAW
                    sp.dma_start(raw[:, slot, 0:kt * PC].rearrange("p (k n) -> p k n", k=kt), view).then_inc(raw_in[slot], 16)
            for n in range(item("wo00"), len(items)):
                load(n)
            for c in range(2):
                if c == 0:
                    sp.wait_ge(u_lo, NF)
                else:
                    sp.wait_ge(m_lo, NP + 1)
                sp.dma_start(xres[c], x[0, :, c * BW:(c + 1) * BW].rearrange("(t p) n -> p t n", p=P))\
                    .then_inc(xres_in[c], 16)
            for c in range(2):
                for t in range(NT):
                    sp.wait_ge(res_done, c * NT + t + 1)
                    sp.dma_start(out[0, t * P:(t + 1) * P, c * BW:(c + 1) * BW], xres[c][:, t, :]).then_inc(stored, 16)
            sp.wait_ge(stored, 16 * 2 * NT)

        @block.gpsimd
        def _(pool):
            link = linker(pool, pool_link)
            nsplit = [0]

            def low_parts(upto):
                while nsplit[0] < upto:
                    i = nsplit[0]
                    n = SPLIT[i]
                    size = items[n][2] * items[n][3] - DVE_LO.get(n, 0)
                    pool.wait_ge(hi_done, i + 1)
                    pool.tensor_tensor(w_lo[:, i % NSPL, 0:size], raw[:, n % NRAW, 0:size],
                                       w_hi[:, i % NSPL, 0:size].bitcast(F32), ALU.subtract).then_inc(lo_done, 1)
                    nsplit[0] += 1

            def rsqrt(dst, src, scale, add):
                link(pool.tensor_scalar(dst, src, scale, add, ALU.mult, ALU.add))
                return pool.tensor_tensor(dst, dst, half_pow[:, 0:dst.shape[1]], ALU.pow)

            link(pool.memset(ident[:, :], 0.0))
            pool.affine_select(out=ident[:, :], in_=ident[:, :], compare_op=ALU.not_equal, fill=1.0, base=0,
                               pattern=[[-1, P]], channel_multiplier=1).then_inc(consts, 1)
            pool.memset(half_pow[:, :], -0.5).then_inc(consts, 1)
            pool.wait_ge(consts, 2)
            for t in range(NT):
                if t == 1:
                    low_parts(1)
                pool.wait_ge(ssx_done, t + 1)
                rsqrt(rsx[:, t:t + 1], ssx[:, t:t + 1], 1.0 / D, EPS).then_inc(rsx_done, 1)
            link(pool.memset(mtmp, 0.0))
            pool.affine_select(out=mtmp, in_=mtmp, compare_op=ALU.is_ge, fill=NEG, base=0,
                               pattern=[[-1, P]], channel_multiplier=1).then_inc(maskf, 1)
            low_parts(2)
            pool.wait_ge(maskb, 1)
            link(pool.memset(mtmp, 0.0))
            pool.affine_select(out=mtmp, in_=mtmp, compare_op=ALU.is_ge, fill=NEG, base=-(CMP_LEN - 1),
                               pattern=[[P, NT], [-CMP_STRIDE, CP]], channel_multiplier=1).then_inc(maskf, 1)
            link(pool.memset(has_cmp[:, :], 1.0))
            link(pool.affine_select(out=has_cmp[:, :], in_=has_cmp[:, :], compare_op=ALU.is_ge, fill=0.0,
                                    base=-(CMP_LEN - 1), pattern=[[0, 1]], channel_multiplier=1))
            for i in range(16):
                pool.memset(inv_cnt[:, i:i + 1], 1.0 / (i + 1))
            pool.memset(Vbd[:, :, :], 0.0).then_inc(vbd_zero, 1)
            pool.memset(X.rearrange("p l c g b -> p (l c g) b")[:, :, NCMP:CP], 0.0).then_inc(xpad, 1)
            for k, c in enumerate(CHUNKS1):
                low_parts(splits_through(c))
                if c != "av":
                    pool.wait_ge(ssn_part, NT * (k + 1))
                    scale, add_ = (1.0, DK * EPS) if c == "aq" else (1.0 / DK, EPS)
                    rsqrt(rsn[:, 0:BH * NT], ssn[:, 0:BH * NT], scale, add_).then_inc(rsn_done, 1)
            for s in STEPS:
                for what, a in pool_at[s]:
                    if what == "norm":
                        k = ("bq0", "bq1", "sw0", "sw1").index(a)
                        ng = 16 if k < 2 else 8
                        pool.wait_ge(ssn2_done, k + 1)
                        scale, add_ = (1.0, DK * EPS) if k < 2 else (1.0 / DK, EPS)
                        rsqrt(rsn[:, 0:ng], ssn[:, 0:ng], scale, add_).then_inc(rsn2_done, 1)
                    elif what == "kc":
                        pool.wait_ge(kcs_done, 1)
                        rsqrt(rskc, sskc, 1.0 / DK, EPS).then_inc(kcr_done, 1)
                    elif what == "fin":
                        pool.wait_ge(ss_f, a + 1)
                        rsqrt(rsf, ssf, 1.0 / P, EPS).then_inc(rs_f, 1)
                low_parts(splits_at[s])
            def merge_ahead(pr, b):
                r = 2 * b + 2
                nxt = pr + 1 if r == PER_PAIR else pr
                for q in (r % PER_PAIR, r % PER_PAIR + 1):
                    wait_at(pool, hi_done, nxt * PER_PAIR + (SPLIT_M + q + 1))
                    slot, place = (SPLIT_M + q) % NSPL, (MERGE0 + q) % NRAW
                    size = merge_size(q)[0] - merge_size(q)[1]
                    pool.tensor_tensor(w_lo[:, slot, 0:size], raw[:, place, 0:size],
                                       w_hi[:, slot, 0:size].bitcast(F32), ALU.subtract).then_inc(lo_done, 1)

            with pool.Fori(0, NP - 1) as pr:
                for b in range(3):
                    merge_ahead(pr, b)
            for b in range(2):
                merge_ahead(NP - 1, b)
            nsplit[0] = SPLIT.index(item("wo00"))
            low_parts(len(SPLIT))

        @block.scalar
        def _(act):
            link = linker(act, act_link)
            nsplit = [0]

            def high_parts(upto):
                while nsplit[0] < upto:
                    i = nsplit[0]
                    n = SPLIT[i]
                    size = items[n][2] * items[n][3]
                    wait_raw(act, n)
                    if i >= NSPL:
                        act.wait_ge(split_used, i - NSPL + 1)
                    act.activation(w_hi[:, i % NSPL, 0:size], raw[:, n % NRAW, 0:size], ACT.Copy).then_inc(hi_done, 1)
                    nsplit[0] += 1

            def high_half(i, half):
                n = SPLIT[i]
                size = items[n][2] * items[n][3] // 2
                if half == 0:
                    wait_raw(act, n)
                    if i >= NSPL:
                        act.wait_ge(split_used, i - NSPL + 1)
                ins = act.activation(w_hi[:, i % NSPL, half * size:(half + 1) * size],
                                     raw[:, n % NRAW, half * size:(half + 1) * size], ACT.Copy)
                if half:
                    ins.then_inc(hi_done, 1)
                    nsplit[0] += 1

            def square_x(t):
                act.wait_ge(x_in[t], 16)
                if t >= 1:
                    act.wait_ge(ssx_done, t)
                act.activation(sq2, xt[:, t, :], ACT.Square, accum_out=ssx[:, t:t + 1]).then_inc(ssx_done, 1)

            def high_h(t):
                for half in range(2):
                    n = 2 * t + half
                    act.wait_ge(xT_done, n + 1)
                    act.activation(h_hi[:, 4 * half:4 * half + 4, t * P:(t + 1) * P],
                                   PS[:, 4 + n % 4, :].rearrange("p (k s) -> p k s", k=4), ACT.Copy).then_inc(hhi_done, 1)

            act.sem_inc(sg_done, 1)
            square_x(0)
            high_parts(1)
            high_h(0)
            for t in range(1, NT):
                square_x(t)
            for t in range(1, NT):
                high_h(t)
            high_parts(2)
            act.wait_ge(cols_tr, 1)
            act.activation(cols[:, :], PS[:, 7, 0:NF + 2 * LP], ACT.Copy).then_inc(cols_done, 1)
            act.wait_ge(lam_s, 1)
            act.activation(lame, lam2, ACT.Exp).then_inc(lam_e, 1)

            nsq = 0
            for c in CHUNKS1:
                high_parts(splits_through(c))
                wait_item_used(act, LAST[c])
                b0 = bank0(c)
                for t in range(NT):
                    if c == "av":
                        ins = act.activation(vA[:, t, :], PS[:, b0 + t, :], ACT.Copy)
                        if t == NT - 1:
                            ins.then_inc(drained[PARITY[c]], 1)
                        continue
                    if nsq >= 2:
                        act.wait_ge(ssn_part, nsq - 1)
                    act.activation(gt[:, nsq % 2, :], PS[:, b0 + t, :], ACT.Square).then_inc(sq_done, 1)
                    nsq += 1

            def drain_tr(r):
                n = tr_no(r)
                act.wait_ge(tr_made, n + 1)
                src = PS[:, B_TR, :]
                if r[0] == "kc":
                    act.activation(KC[:, r[1], :], src[:, 0:G * CP], ACT.Copy).then_inc(tr_drained, 1)
                elif r[0] == "gates":
                    act.activation(gates[:, :, :].rearrange("p t n -> p (t n)"), src[:, 0:NT * NG], ACT.Copy).then_inc(tr_drained, 1)
                elif r[0] == "ht":
                    hid = src[:, 0:NH2 * P].rearrange("p (n c k) -> p c n k", n=NH2, c=2)
                    act.activation(HTk, hid[:, 0, :, :].unsqueeze(2).broadcast_to([P, NH2, 2, G * CP]), ACT.Copy, scale=0.5)
                    for n in range(NH2):
                        v = hid[:, 1, n, :].rearrange("p (g b) -> p g b", g=G).unsqueeze(2).broadcast_to([P, G, 4, CP])
                        ins = act.activation(HTv[:, n], v, ACT.Copy, scale=0.5)
                    ins.then_inc(tr_drained, 1)
                elif r[0] == "q":
                    _, i, m = hls[r[1]]
                    act.activation(QS[:, 2 * (i % 2) + m, :], src, ACT.Copy).then_inc(tr_drained, 1)
                elif r[0] == "k":
                    _, i, m = hls[r[1]]
                    par = i % 2 if i < AH else ((i - AH) // HPG) % 2
                    act.activation(KS[:, 4 * par + 2 * m, :], src, ACT.Copy)
                    act.activation(KS[0:DK, 4 * par + 2 * m + 1, :], src[DK:P, :], ACT.Copy)
                    act.activation(KS[DK:P, 4 * par + 2 * m + 1, :], src[0:DK, :], ACT.Copy).then_inc(tr_drained, 1)
                elif r[0] == "oc":
                    act.activation(OC[:, units[r[1]][1] % 2, :, :].rearrange("p t d -> p (t d)"), src[:, 0:NT * DK],
                                   ACT.Copy).then_inc(tr_drained, 1)
                else:
                    i = r[1]
                    act.activation(U[:, i if i < AH else NF + (i - AH) // 2, :], src, ACT.Copy).then_inc(tr_drained, 1)

            def drain_fill(k):
                kind, name, w = fills[k]
                wait_filled(act, k)
                bank = PS[:, B_F + k % 2, :]
                if kind == "tok":
                    half = int(name[2])
                    b = bank.rearrange("p (t n) -> p t n", t=2)
                    if name[:2] == "bq":
                        act.activation(qB[:, 2 * w:2 * w + 2, half * PC:(half + 1) * PC], b, ACT.Copy).then_inc(act_free, 1)
                    else:
                        act.activation(kB[:, 2 * w:2 * w + 2, half * P:(half + 1) * P], b[:, :, 0:P], ACT.Copy)
                        act.activation(vB[:, 2 * w:2 * w + 2, half * P:(half + 1) * P], b[:, :, P:2 * P],
                                       ACT.Copy).then_inc(act_free, 1)
                elif kind == "cmp":
                    for g in range(G):
                        src = bank[g * DK:(g + 1) * DK, :]
                        act.activation(T2[0:DK, w, g, :], src, ACT.Copy)
                        ins = act.activation(T2[DK:P, w, g, 0:SEQ - 1], src[:, 1:SEQ], ACT.Copy)
                    ins.then_inc(act_free, 1)
                elif kind == "phi":
                    act.wait_ge(x_done, 2)
                    for c in range(2):
                        ins = act.activation(hid_e[c * DK:(c + 1) * DK, :], bank[c * DK:(c + 1) * DK, c * HID:(c + 1) * HID],
                                             ACT.Tanh, scale=0.5)
                    ins.then_inc(e_done, 1)
                elif kind == "bbg":
                    act.activation(gT, bank[0:NG, :], ACT.Tanh, scale=0.5).then_inc(act_free, 1)
                elif kind in ("ag", "bg", "cg"):
                    j = gate_fills.index(k)
                    if j >= 2:
                        act.wait_ge(g_done, j - 1)
                    act.activation(gt[:, j % 2, :], bank, ACT.Tanh, scale=0.5).then_inc(e_done, 1)
                elif kind == "cu":
                    act.activation(U[:, 2 * NF + 2 * int(name[2]) + w, :], bank, ACT.Copy).then_inc(act_free, 1)
                elif kind == "cw":
                    act.activation(U[:, 2 * NF + w, :], bank, ACT.Copy, scale=cols[:, w:w + 1]).then_inc(act_free, 1)

            for s in STEPS:
                if 0 <= s < NU:
                    kind, h, t, m = units[s]
                    if kind == "C":
                        act.wait_ge(csub, h + 1)
                        act.activation(Pr[:, s % 3, 0:P], Pr[:, s % 3, 0:P], ACT.Exp).then_inc(exped, 1)
                    else:
                        wait_place(act, s)
                        W = (t + 1) * P
                        act.wait_ge(maxed, s + 1)
                        o = s % 16 if kind == "A" else m * NT + t + 8 * (h % 2)
                        act.activation(Pr[:, s % 3, 0:W], PS[:, B_S + s % 2, 0:W], ACT.Exp,
                                       bias=negmax[:, s % 8:s % 8 + 1], accum_out=rowsum[:, o:o + 1]).then_inc(exped, 1)
                for what, k in act_at[s]:
                    if what == "drain":
                        drain_fill(k)
                    else:
                        act.wait_ge(o_free, k + 1)
                        if k:
                            act.wait_ge(rs_f, k)
                        for tt in range(NT):
                            ins = act.activation(OC[:, :, :, :].rearrange("p a (t b) d -> p (a t) (b d)", b=2)[:, tt, :], OF[:, tt, :],
                                                 ACT.Square, accum_out=ssf[:, tt:tt + 1])
                        ins.then_inc(ss_f, 1)
                for r in trs[s]:
                    drain_tr(r)
                for i, half in highs_at[s]:
                    high_half(i, half)

            for n in range(2 * NF):
                act.wait_ge(u_done, n + 1)
                f = (n + NF) % (2 * NF)
                act.activation(o_hi[NF + f], U[:, NF + f, :], ACT.Copy).then_inc(u_hi, 1)

            def merge_high(pr, r):
                nxt, q = (pr + 1, r - PER_PAIR) if r >= PER_PAIR else (pr, r)
                slot, place, size = (SPLIT_M + q) % NSPL, (MERGE0 + q) % NRAW, merge_size(q)[0]
                wait_at(act, raw_in[place], nxt * (16 * PER_PAIR // NRAW) + 16 * ((MERGE0 + q) // NRAW + 1))
                wait_at(act, split_used, nxt * PER_PAIR + (SPLIT_M + q + 1 - NSPL))
                act.activation(w_hi[:, slot, 0:size], raw[:, place, 0:size], ACT.Copy).then_inc(hi_done, 1)

            def merge_pair(pr, last):
                for b in range(3):
                    ahead = not (last and b == 2)
                    if ahead:
                        merge_high(pr, 2 * b + 2)
                    else:
                        high_parts(SPLIT.index(item("wo00")) + 1)
                    merge_used(act, pr, 2 * b)
                    if b == 1:
                        act.wait_ge(u_lo, 2 * NF)
                    wait_at(act, sg_used, pr * 3 + (b // 2 + 1))
                    act.activation(sg[:, b % 2, :], PS[:, 4 * (b % 2):4 * (b % 2) + 2, :].rearrange("p a s -> p (a s)"),
                                   ACT.Tanh, scale=0.5).then_inc(sg_done, 1)
                    if ahead:
                        merge_high(pr, 2 * b + 3)
                    else:
                        high_parts(SPLIT.index(item("wo00")) + 2)
                wait_at(act, acc_done, pr + 1)
                act.activation(M_hi[:, bass.ds(2 * pr, 2), :].rearrange("p a s -> p (a s)"), acc, ACT.Copy,
                               scale=0.5).then_inc(m_hi, 1)

            with act.Fori(0, NP - 1) as pr:
                merge_pair(pr, False)
            nsplit[0] = SPLIT.index(item("wo00"))
            merge_pair(NP - 1, True)
            high_parts(len(SPLIT))

        @block.vector
        def _(dve):
            link = linker(dve, dve_link)
            nlow = [0]

            def low_parts(upto):
                while nlow[0] < upto:
                    i = nlow[0]
                    n = SPLIT[i]
                    if n in DVE_LO:
                        a, b = items[n][2] * items[n][3] - DVE_LO[n], items[n][2] * items[n][3]
                        dve.wait_ge(hi_done, i + 1)
                        dve.tensor_tensor(w_lo[:, i % NSPL, a:b], raw[:, n % NRAW, a:b],
                                          w_hi[:, i % NSPL, a:b].bitcast(F32), ALU.subtract).then_inc(lo_dve, 1)
                    nlow[0] += 1

            def norm_x(t):
                dve.wait_ge(rsx_done, t + 1)
                if t == 0:
                    dve.wait_ge(gb_in, 16)
                dve.scalar_tensor_tensor(xt[:, t, :], xt[:, t, :], rsx[:, t:t + 1], gB, ALU.mult, ALU.mult).then_inc(xn_done, 1)

            def low_h(t):
                for half in range(2):
                    n = 2 * t + half
                    dve.wait_ge(hhi_done, n + 1)
                    hh = h_hi[:, 4 * half:4 * half + 4, t * P:(t + 1) * P]
                    dve.tensor_tensor(h_lo[:, 4 * half:4 * half + 4, t * P:(t + 1) * P],
                                      PS[:, 4 + n % 4, :].rearrange("p (k s) -> p k s", k=4), hh.bitcast(F32), ALU.subtract).then_inc(hlo_done, 1)

            dve.sem_inc(sg_used, 1)
            dve.sem_inc(m_lo, 1)
            norm_x(0)
            low_parts(1)
            low_h(0)
            norm_x(1)
            for t in range(1, NT):
                if t + 1 < NT:
                    norm_x(t + 1)
                low_h(t)
            low_parts(2)
            dve.wait_ge(consts, 1)
            dve.tensor_copy(identb[:, :], ident[:, :])
            dve.wait_ge(maskf, 1)
            dve.tensor_copy(causal[:, :], mtmp).then_inc(maskb, 1)
            dve.wait_ge(maskf, 2)
            dve.tensor_copy(cmask[:, :], mtmp).then_inc(maskb, 1)
            dve.wait_ge(small_in, 16 * 10)
            lv = lamv.rearrange("p (a two) d -> p a two d", two=2)
            link(dve.tensor_tensor(lamt, lv[:, :, 0, :], lv[:, :, 1, :], ALU.mult))
            dve.reduce_sum(lam2, lamt, AX.X).then_inc(lam_s, 1)
            dve.tensor_tensor(gains[:, 1, :], gains[:, 1, :], gains[:, 0, :], ALU.mult)
            link(dve.tensor_tensor(gains[:, 3:6, :], gains[:, 3:6, :], gains[:, 2, :].unsqueeze(1).broadcast_to([P, 3, DK]), ALU.mult))
            link(dve.tensor_scalar(subln[:, :], subln[:, :], 1.0 - LAM_INIT, None, ALU.mult))
            dve.wait_ge(lam_e, 1)
            link(dve.tensor_scalar(nlam, lame[:, 1:2], lame[:, 0:1], -LAM_INIT, ALU.subtract, ALU.add))

            nsq = 0
            for k, c in enumerate(("aq", "ak")):
                b0 = bank0(c)
                for t in range(NT):
                    dve.wait_ge(sq_done, nsq + 1)
                    dve.reduce_sum(ssn[:, BH * t:BH * (t + 1)], gt[:, nsq % 2, :].rearrange("p (h d) -> p h d", d=DK),
                                   AX.X).then_inc(ssn_part, 1)
                    nsq += 1
                dve.wait_ge(rsn_done, k + 1)
                dst = qkA[:, k]
                for t in range(NT):
                    r = rsn[:, BH * t:BH * (t + 1)].unsqueeze(2).broadcast_to([P, BH, DK])
                    ins = dve.tensor_tensor(dst[:, t, :].rearrange("p (h d) -> p h d", d=DK),
                                            PS[:, b0 + t, :].rearrange("p (h d) -> p h d", d=DK), r, ALU.mult)
                link(ins)
                dve.sem_inc(drained[PARITY[c]], 1)
                if c == "ak":
                    v = dst.rearrange("p t (h d) -> p (t h) d", d=DK)
                    link(dve.tensor_tensor(v, v, gains[:, 1, :].unsqueeze(1).broadcast_to([P, NT * BH, DK]), ALU.mult))

            gates_h = gates[:, :, :].rearrange("p t (h j) -> p t h j", j=3)

            def fill_work(what, a):
                if what == "hl":
                    kind, i, m = hls[a]
                    if i < AH:
                        src = (qA if kind == "q" else kA)[:, :, (2 * i + m) * DK:(2 * i + m + 1) * DK]
                    elif kind == "q":
                        src = qB[:, :, (i - AH) * DK:(i - AH + 1) * DK]
                    else:
                        g = (i - AH) // HPG
                        src = kB[:, :, (m * G + g) * DK:(m * G + g + 1) * DK]
                    before = [k for k in range(a) if hls[k][0] == kind]
                    if before:
                        dve.wait_ge(tr_made, last_tr(before[-1]) + 1)
                    hl = HLq if kind == "q" else HLk
                    link(dve.tensor_copy(hl[:, :, 0, :], src))
                    dve.tensor_tensor(hl[:, :, 1, :], src, hl[:, :, 0, :].bitcast(F32), ALU.subtract).then_inc(hl_made, 1)
                elif what in ("norm1", "norm2"):
                    k = ("bq0", "bq1", "sw0", "sw1").index(a)
                    v = (qB[:, :, k * PC:(k + 1) * PC] if k < 2 else kB[:, :, (k - 2) * P:(k - 1) * P])
                    ng, n = (16, PC) if k < 2 else (8, P)
                    if what == "norm1":
                        dve.wait_ge(act_free, sum(1 for f in fills[:FILL[("tok", a, 1)] + 1] if f[0] not in DVE_DRAINS))
                        link(dve.tensor_tensor(sq2[:, 0:NT * n].rearrange("p (t n) -> p t n", t=NT), v, v, ALU.mult))
                        link(dve.reduce_sum(ssn[:, 0:ng], sq2[:, 0:NT * n].rearrange("p (h d) -> p h d", d=DK), AX.X))
                        dve.sem_inc(ssn2_done, 1)
                    else:
                        dve.wait_ge(rsn2_done, k + 1)
                        v4 = v.rearrange("p t (h d) -> p t h d", d=DK)
                        sh = [P, NT, n // DK, DK]
                        r = rsn[:, 0:ng].rearrange("p (t h) -> p t h", t=NT).unsqueeze(3).broadcast_to(sh)
                        link(dve.tensor_tensor(v4, v4, r, ALU.mult))
                        if k >= 2:
                            gg = gains[:, 2 + k, :].unsqueeze(1).unsqueeze(1).broadcast_to(sh)
                            link(dve.tensor_tensor(v4, v4, gg, ALU.mult))
                elif what == "x":
                    dve.wait_ge(act_free, sum(1 for f in fills[:FILL[("cmp", "cmp", a)] + 1] if f[0] not in DVE_DRAINS))
                    if a == 0:
                        dve.wait_ge(cols_done, 1)
                        dve.wait_ge(xpad, 1)
                    for g in range(G):
                        base_ = T2[:, a, g, :]
                        src = bass.AP(base_.tensor, base_.offset, [list(base_.ap[0]), [2, LP], [CMP_STRIDE, NCMP]])
                        pos = cols[:, NF + a * LP:NF + (a + 1) * LP].unsqueeze(2).broadcast_to([P, LP, NCMP])
                        ins = dve.tensor_tensor(X[:, :, a, g, 0:NCMP], src, pos, ALU.add)
                    ins.then_inc(x_done, 1)
                elif what == "silu":
                    dve.wait_ge(e_done, 1)
                    for c in range(2):
                        h = hid_e[c * DK:(c + 1) * DK, :]
                        ins = dve.scalar_tensor_tensor(h, h, 1.0, PS[c * DK:(c + 1) * DK, B_F + a % 2, c * HID:(c + 1) * HID],
                                                       ALU.add, ALU.mult)
                    link(ins)
                    dve.sem_inc(dve_free, 1)
                    dve.sem_inc(hid_done, 1)
                elif what == "gates":
                    dve.wait_ge(tr_drained, tr_no(("gates", 0)) + 1)
                    v = gates[:, :, :].rearrange("p t n -> p (t n)")
                    link(dve.tensor_scalar(v, v, 1.0, 0.5, ALU.add, ALU.mult))
                elif what == "kc1":
                    bank = PS[:, B_F + a % 2, :]
                    wait_filled(dve, a)
                    dve.wait_ge(vbd_zero, 1)
                    for g in range(G):
                        for t in range(NT):
                            dve.tensor_copy(Vbd[t * CP:(t + 1) * CP, g, t * DK:(t + 1) * DK],
                                            bank[t * CP:(t + 1) * CP, (1 + g) * DK:(2 + g) * DK])
                    link(dve.tensor_copy(kcn[:, :], bank[:, 0:DK]))
                    dve.sem_inc(dve_free, 1)
                    link(dve.tensor_tensor(kchl[:, 0, :].bitcast(F32), kcn[:, :], kcn[:, :], ALU.mult))
                    link(dve.reduce_sum(sskc, kchl[:, 0, :].bitcast(F32), AX.X))
                    dve.sem_inc(kcs_done, 1)
                elif what == "kc2":
                    dve.wait_ge(kcr_done, 1)
                    link(dve.scalar_tensor_tensor(kcn[:, :], kcn[:, :], rskc, gains[:, 3, :], ALU.mult, ALU.mult))
                    link(dve.tensor_copy(kchl[:, 0, :], kcn[:, :]))
                    dve.tensor_copy(kchl[:, 2, :], kcn[:, :])
                    dve.tensor_tensor(kchl[:, 1, :], kcn[:, :], kchl[:, 0, :].bitcast(F32), ALU.subtract).then_inc(kchl_done, 1)
                elif what == "gate":
                    j = gate_fills.index(a)
                    dve.wait_ge(e_done, 2 + j)
                    v = gt[:, j % 2, :]
                    dst = gB2[:, j - NF, :] if NF <= j < 2 * NF else v
                    link(dve.scalar_tensor_tensor(dst, v, 1.0, PS[:, B_F + a % 2, :], ALU.add, ALU.mult))
                    dve.sem_inc(dve_free, 1)
                    if j >= 2 * NF:
                        f = j - 2 * NF
                        wait_bank_read(dve, FIRST_CW + f)
                        u_ = U[:, 2 * NF + f, :]
                        link(dve.scalar_tensor_tensor(u_, v, 0.5, u_, ALU.mult, ALU.mult))
                    if j >= NF:
                        dve.sem_inc(g_done, 1)
                elif what == "agate":
                    j = gate_fills.index(a)
                    v = gt[:, j % 2, :]
                    dve.wait_ge(tr_drained, tr_no(("fin", j)) + 1)
                    link(dve.scalar_tensor_tensor(v, v, 0.5, U[:, j, :], ALU.mult, ALU.mult))
                    link(dve.tensor_copy(o_hi[j], v))
                    link(dve.tensor_tensor(o_lo[j], v, o_hi[j].bitcast(F32), ALU.subtract))
                    dve.sem_inc(g_done, 1)
                elif what == "pool":
                    k, g, level = a
                    u = U[:, 2 * NF + g, :]
                    if level == 0:
                        dve.wait_ge(act_free, sum(1 for f in fills[:k + 1] if f[0] not in DVE_DRAINS))
                    if level <= g:
                        width = 1 << level
                        src = u if level == 0 else gB2[:, 2 + (level - 1) % 2, :]
                        dst = gB2[:, 2 + level % 2, :]
                        link(dve.tensor_copy(dst[:, 0:width], src[:, 0:width]))
                        link(dve.tensor_tensor(dst[:, width:SEQ], src[:, width:SEQ], src[:, 0:SEQ - width], ALU.add))
                    else:
                        win = 2 << g
                        src = gB2[:, 2 + g % 2, :]
                        head = gB2[:, 2 + (g + 1) % 2, 0:win - 1]
                        link(dve.tensor_tensor(head, src[:, 0:win - 1], inv_cnt[:, 0:win - 1], ALU.mult))
                        link(dve.tensor_tensor(head, head, u[:, 0:win - 1], ALU.subtract))
                        link(dve.scalar_tensor_tensor(u, src, 1.0 / win, u, ALU.mult, ALU.subtract))
                        link(dve.tensor_copy(u[:, 0:win - 1], head))
                        dve.sem_inc(pooled, 1)

            for s in STEPS:
                if 0 <= s < NU:
                    kind, h, t, m = units[s]
                    dve.wait_ge(scores, s + 1)
                    if kind == "C":
                        wait_place(dve, s)
                        sc = PS[:, B_S + s % 2, 0:P].rearrange("p (t k) -> p t k", t=NT)
                        dve.tensor_reduce(nmc, sc, AX.X, ALU.max, negate=True).then_inc(maxed, 1)
                        dve.wait_ge(maxed, s + 1)
                        dve.tensor_tensor(Pr[:, s % 3, 0:P].rearrange("p (t k) -> p t k", t=NT), sc,
                                          nmc.unsqueeze(2).broadcast_to([P, NT, CP]), ALU.add).then_inc(csub, 1)
                    else:
                        dve.tensor_reduce(negmax[:, s % 8:s % 8 + 1], PS[:, B_S + s % 2, 0:(t + 1) * P], AX.X, ALU.max,
                                          negate=True).then_inc(maxed, 1)
                u = s - 1
                if 0 <= u < NU:
                    kind, h, t, m = units[u]
                    W = (t + 1) * P
                    if kind == "A" and m == 1:
                        a, b = (u - 1) % 16, u % 16
                        dve.wait_ge(exped, u + 1)
                        link(dve.reciprocal(recip[:, b:b + 1], rowsum[:, b:b + 1]))
                        link(dve.scalar_tensor_tensor(recip[:, b:b + 1], recip[:, b:b + 1], rowsum[:, a:a + 1], nlam,
                                                      ALU.mult, ALU.mult))
                        dve.scalar_tensor_tensor(Pr[:, u % 3, 0:W], Pr[:, u % 3, 0:W], recip[:, b:b + 1],
                                                 Pr[:, (u - 1) % 3, 0:W], ALU.mult, ALU.add).then_inc(weighted, 1)
                    elif kind == "C":
                        pc = Pr[:, u % 3, 0:P].rearrange("p (t k) -> p t k", t=NT)
                        dve.wait_ge(exped, u + 1)
                        link(dve.reduce_sum(lc, pc, AX.X))
                        link(dve.reciprocal(fc, lc))
                        link(dve.tensor_tensor(fc, fc, gates_h[:, :, h, 0], ALU.mult))
                        link(dve.tensor_tensor(fc[:, 0:1], fc[:, 0:1], has_cmp[:, :], ALU.mult))
                        dve.tensor_tensor(pc, pc, fc.unsqueeze(2).broadcast_to([P, NT, CP]), ALU.mult).then_inc(weighted, 1)
                u = s - LT
                if u in job_of:
                    j = job_of[u]
                    kind, h, t, m = units[u]
                    W = P if kind == "C" else (t + 1) * P
                    dve.wait_ge(ptd, j + 1)
                    if j >= 2:
                        wait_pv(dve, j - 2)
                    dve.tensor_copy(PTs[:, j % 2, 0:W], PS[:, B_PT + j % 2, 0:W]).then_inc(pt_out, 1)
                ob = PS[:, B_O, :]
                for i in range(NHEAD):
                    if AH <= i and s == last_u[i] + 2:
                        h = i - AH
                        link(dve.reciprocal(fB, rowsum[:, 8 * (h % 2):8 * (h % 2) + 8]))
                        for m in range(2):
                            ins = dve.tensor_tensor(fB[:, m * NT:(m + 1) * NT], fB[:, m * NT:(m + 1) * NT], gates_h[:, :, h, 1 + m], ALU.mult)
                        link(ins)
                    elif AH <= i and s == last_u[i] + LV:
                        wait_pv(dve, job_of[last_u[i] - 1])
                        link(dve.tensor_tensor(wB, ob.rearrange("p (m d) -> p m d", d=DK),
                                               fB.unsqueeze(2).broadcast_to([P, 2 * NT, DK]), ALU.mult))
                        dve.sem_inc(o_free, 1)
                    elif i < AH and s == last_u[i] + LF:
                        wait_pv(dve, job_of[last_u[i]])
                        if i >= 1:
                            dve.wait_ge(tr_made, tr_no(("fin", i - 1)) + 1)
                        sum0 = rowsum[:, 8 * (i % 2):8 * (i % 2) + 8].rearrange("p (t m) -> p t m", m=2)[:, :, 0]
                        link(dve.reciprocal(rs0, sum0))
                        link(dve.tensor_tensor(OF[:, :, :], ob.rearrange("p (t n) -> p t n", t=NT),
                                               rs0.unsqueeze(2).broadcast_to([P, NT, P]), ALU.mult))
                        dve.sem_inc(o_free, 1)
                    elif i < AH and s == last_u[i] + LF + 3:
                        dve.wait_ge(rs_f, i + 1)
                        link(dve.tensor_tensor(OF[:, :, :], OF[:, :, :], rsf.unsqueeze(2).broadcast_to([P, NT, P]), ALU.mult))
                        dve.tensor_tensor(OF[:, :, :], OF[:, :, :], subln[:, :].unsqueeze(1).broadcast_to([P, NT, P]),
                                          ALU.mult).then_inc(of_done, 1)
                    elif i >= AH and s == last_u[i] + LF:
                        h = i - AH
                        o = OF[:, :, (h % 2) * DK:(h % 2 + 1) * DK]
                        dve.wait_ge(tr_drained, tr_no(("oc", last_u[i])) + 1)
                        if h % 2 == 0:
                            dve.wait_ge(tr_made, tr_no(("fin", i - 1)) + 1)
                        link(dve.tensor_tensor(o, wB[:, 0:NT, :], wB[:, NT:2 * NT, :], ALU.add))
                        dve.tensor_tensor(o, o, OC[:, h % 2, :, :], ALU.add).then_inc(of_done, 1)
                for what, a in dve_at[s]:
                    fill_work(what, a)
                if s == min(high_step(SPLIT_M) + 2, NSTEP - 1):
                    low_parts(SPLIT_M + 1)

            dve.wait_ge(tr_drained, NTR)
            dve.wait_ge(act_free, sum(1 for f in fills if f[0] not in DVE_DRAINS))
            dve.sem_inc(u_done, NF)
            for n in range(2 * NF):
                f = (n + NF) % (2 * NF)
                if f < NF:
                    link(dve.scalar_tensor_tensor(U[:, NF + f, :], U[:, NF + f, :], 0.5, gB2[:, f, :], ALU.mult, ALU.mult))
                    dve.sem_inc(u_done, 1)
                dve.wait_ge(u_hi, n + 1)
                dve.tensor_tensor(o_lo[NF + f], U[:, NF + f, :], o_hi[NF + f].bitcast(F32), ALU.subtract).then_inc(u_lo, 1)

            def merge_low_part(pr, r):
                nxt, q = (pr + 1, r - PER_PAIR) if r >= PER_PAIR else (pr, r)
                slot, place = (SPLIT_M + q) % NSPL, (MERGE0 + q) % NRAW
                a, b_ = merge_size(q)[0] - merge_size(q)[1], merge_size(q)[0]
                wait_at(dve, hi_done, nxt * PER_PAIR + (SPLIT_M + q + 1))
                dve.tensor_tensor(w_lo[:, slot, a:b_], raw[:, place, a:b_],
                                  w_hi[:, slot, a:b_].bitcast(F32), ALU.subtract).then_inc(lo_dve, 1)

            def merge_pair(pr, last):
                for b in range(3):
                    if not (last and b == 2):
                        merge_low_part(pr, 2 * b + 2)
                    else:
                        nlow[0] = SPLIT.index(item("wo00"))
                        low_parts(nlow[0] + 1)
                    wait_at(dve, sg_done, pr * 3 + (b + 2))
                    merge_used(dve, pr, 2 * b + 1)
                    y = PS[:, 4 * (b % 2) + 2:4 * (b % 2) + 4, :].rearrange("p a s -> p (a s)")
                    if b == 0:
                        wait_at(dve, m_lo, pr + 1)
                        dve.scalar_tensor_tensor(acc, sg[:, 0, :], 1.0, y, ALU.add, ALU.mult).then_inc(sg_used, 1)
                    else:
                        dve.scalar_tensor_tensor(sg[:, b % 2, :], sg[:, b % 2, :], 1.0, y, ALU.add, ALU.mult).then_inc(y_done, 1)
                        wait_at(dve, sg_used, pr * 3 + (b + 1))
                        wait_at(dve, y_done, pr * 2 + b)
                        dve.tensor_tensor(acc, acc, sg[:, b % 2, :], ALU.add).then_inc(sg_used, 1)
                wait_at(dve, sg_used, pr * 3 + 4)
                dve.sem_inc(acc_done, 1)
                wait_at(dve, m_hi, pr + 1)
                m_h, m_l = (m[:, bass.ds(2 * pr, 2), :].rearrange("p a s -> p (a s)") for m in (M_hi, M_lo))
                dve.scalar_tensor_tensor(m_l, acc, 0.5, m_h.bitcast(F32), ALU.mult, ALU.subtract).then_inc(m_lo, 1)

            with dve.Fori(0, NP - 1) as pr:
                merge_pair(pr, False)
            merge_pair(NP - 1, True)
            low_parts(len(SPLIT))

            for cc in range(2):
                dve.wait_ge(xres_in[cc], 16)
                for t in range(NT):
                    if t < NT - 1:
                        dve.wait_ge(wo_tile, cc * (NT - 1) + t + 1)
                    else:
                        wait_item_used(dve, f"wo{cc}1")
                    dve.tensor_tensor(xres[cc][:, t, :], xres[cc][:, t, :], PS[:, WO_BANK[cc] + t, :], ALU.add).then_inc(res_done, 1)

        @block.tensor
        def _(pe):
            pe.wait_ge(consts, 1)
            def transpose_x(t):
                pe.wait_ge(xn_done, t + 1)
                for half in range(2):
                    n = 2 * t + half
                    if n >= 4:
                        pe.wait_ge(hlo_done, n - 3)
                    for k in range(4):
                        ins = pe.transpose(PS[:, 4 + n % 4, k * P:(k + 1) * P], xt[:, t, (4 * half + k) * P:(4 * half + k + 1) * P], ident[:, :])
                    ins.then_inc(xT_done, 1)

            def ready_first(half, t, k):
                if half == 0:
                    if k == 0:
                        pe.wait_ge(hlo_done, 2 * t + 2)
                    elif k == 2 and t + 1 < NT:
                        transpose_x(t + 1)
                elif t == 0 and k == 0:
                    pe.wait_ge(rows_in, 32)
                    NR = NF + 2 * LP
                    pe.transpose(PS[:, 7, 0:NR], rows, ident[0:NR, 0:NR]).then_inc(cols_tr, 1)

            transpose_x(0)
            H_hi, H_lo = [h_hi[:, k, :] for k in range(NK)], [h_lo[:, k, :] for k in range(NK)]
            MH, ML = [M_hi[:, k, :] for k in range(NK)], [M_lo[:, k, :] for k in range(NK)]

            def weights(name):
                n = item(name)
                i = SPLIT.index(n)
                wait_low(pe, i)
                _, _, kt, ncol, _ = items[n]
                return [w[:, i % NSPL, 0:kt * ncol].rearrange("p (k n) -> p k n", k=kt) for w in (w_hi, w_lo)]

            def whole(name):
                n = item(name)
                wait_raw(pe, n)
                _, _, kt, ncol, _ = items[n]
                return raw[:, n % NRAW, 0:kt * ncol].rearrange("p (k n) -> p k n", k=kt)

            def three(out_, s_hi, s_lo, m_hi_, m_lo_, start, stop):
                pe.matmul(out_, s_hi, m_hi_, start=start, stop=False)
                pe.matmul(out_, s_hi, m_lo_, start=False, stop=False)
                return pe.matmul(out_, s_lo, m_hi_, start=False, stop=stop)

            def token_major(c, b0, ths, tls, ready):
                for half in range(2):
                    wh, wl = weights(f"{c}{half}")
                    for t in range(NT):
                        for k in range(HK):
                            ready(half, t, k)
                            kk = half * HK + k
                            ins = three(PS[:, b0 + t, 0:wh.shape[2]], ths[kk][:, t * P:(t + 1) * P], tls[kk][:, t * P:(t + 1) * P],
                                        wh[:, k, :], wl[:, k, :], kk == 0, kk == NK - 1)
                        if c[0] == "w" and half == 1 and t < NT - 1:
                            ins.then_inc(wo_tile, 1)
                    ins.then_inc(split_used, 1)

            def feature_major(ws, bank, ths, tls):
                wh, wl = ws
                for f in range(2):
                    for k in range(len(ths)):
                        ins = three(PS[:, bank + f, :], wh[:, k, f * P:(f + 1) * P], wl[:, k, f * P:(f + 1) * P],
                                    ths[k], tls[k], k == 0, k == len(ths) - 1)
                ins.then_inc(split_used, 1)

            for c in CHUNKS1:
                if c == "ak":
                    pe.wait_ge(cols_done, 1)
                if EARLIER[c]:
                    pe.wait_ge(drained[PARITY[c]], EARLIER[c])
                token_major(c, bank0(c), H_hi, H_lo, ready_first if c == "aq" else lambda half, t, k: None)

            pe.wait_ge(drained[1], 1)
            pe.wait_ge(maskb, 2)

            def fill_piece(k, p):
                kind, name, w = fills[k]
                bank = PS[:, B_F + k % 2, :]
                if p == 0 and k >= 2:
                    wait_bank_read(pe, k - 2)
                used = False
                if kind == "tok":
                    wh, wl = weights(name)
                    t = 2 * w + p // 2
                    for kk in range(HK * (p % 2), HK * (p % 2) + HK):
                        ins = three(bank[:, (p // 2) * PC:(p // 2 + 1) * PC], H_hi[kk][:, t * P:(t + 1) * P],
                                    H_lo[kk][:, t * P:(t + 1) * P], wh[:, kk, :], wl[:, kk, :], kk == 0, kk == NK - 1)
                    used = w == 1 and p == 3
                elif kind in ("cmp", "ag", "cu", "bg", "cg"):
                    wh, wl = weights(name)
                    for kk in (2 * p, 2 * p + 1):
                        ins = three(bank, wh[:, kk, w * P:(w + 1) * P], wl[:, kk, w * P:(w + 1) * P], H_hi[kk], H_lo[kk],
                                    kk == 0, kk == NK - 1)
                    used = w == 1 and p == 3
                elif kind == "phi":
                    c, half = p // 4, p // 2 % 2
                    w1 = whole(f"phi{c}{half}")
                    if p == 0:
                        pe.wait_ge(x_done, 2)
                    for l in range(LP // 4 * (p % 4), LP // 4 * (p % 4 + 1)):
                        ins = pe.matmul(bank[:, c * HID:(c + 1) * HID], X[:, l].rearrange("p c g b -> p (c g b)"),
                                        w1[:, l - half * LP // 2, :], start=l == 0, stop=l == LP - 1)
                    if p % 2:
                        ins.then_inc(whole_used, 1)
                elif kind == "bbg":
                    wh, wl = weights(name)
                    for kk in range(HK * p, HK * p + HK):
                        ins = three(bank[0:NG, :], wh[:, kk, :], wl[:, kk, :], H_hi[kk], H_lo[kk], kk == 0, kk == NK - 1)
                    used = p == 1
                elif kind == "phi2":
                    pe.wait_ge(tr_drained, tr_no(("ht", 0)) + 1)
                    pe.wait_ge(small_in, 16 * 10)
                    for n in range(NH2):
                        pe.matmul(bank[:, 0:DK], HTk[:, n].rearrange("p r c -> p (r c)"), w2[:, 0, n, :], start=n == 0, stop=n == NH2 - 1)
                    for g in range(G):
                        for n in range(NH2):
                            ins = pe.matmul(bank[:, (1 + g) * DK:(2 + g) * DK], HTv[:, n, g].rearrange("p r b -> p (r b)"),
                                            w2[:, 1, n, :], start=n == 0, stop=n == NH2 - 1)
                else:
                    wc = whole("cw")
                    pe.wait_ge(pooled, w + 1)
                    ins = pe.matmul(bank, wc[:, w, :], U[:, 2 * NF + w, :], start=True, stop=True)
                if used:
                    ins.then_inc(split_used, 1)
                elif kind == "cw" and w == NF - 1:
                    ins.then_inc(whole_used, 1)
                elif p == PIECES[kind] - 1 and kind != "phi":
                    ins.then_inc(filled, 1)

            def transpose_tr(r):
                n = tr_no(r)
                if n:
                    pe.wait_ge(tr_drained, n)
                bank = PS[:, B_TR, :]
                if r[0] == "gates":
                    k = FILL[("bbg", "bbg", 0)]
                    wait_bank_read(pe, k)
                    for t in range(NT):
                        ins = pe.transpose(bank[:, t * NG:(t + 1) * NG], gT[:, t * P:(t + 1) * P], ident[0:NG, 0:NG])
                    ins.then_inc(tr_made, 1)
                elif r[0] == "ht":
                    pe.wait_ge(hid_done, 1)
                    for n in range(NH2):
                        ins = pe.transpose(bank[:, n * P:(n + 1) * P], hid_e[:, n * P:(n + 1) * P], ident[:, :])
                    ins.then_inc(tr_made, 1)
                elif r[0] == "kc":
                    pe.wait_ge(kchl_done, 1)
                    src = kchl[:, r[1]:r[1] + 2, :].rearrange("p a d -> p (a d)").bitcast(F32)
                    pe.transpose(bank[:, 0:P], src, ident[:, :]).then_inc(tr_made, 1)
                elif r[0] in ("q", "k"):
                    pe.wait_ge(hl_made, r[1] + 1)
                    for t in range(NT):
                        hl = (HLq if r[0] == "q" else HLk)[:, t, :, :].rearrange("p a d -> p (a d)").bitcast(F32)
                        ins = pe.transpose(bank[:, t * P:(t + 1) * P], hl, ident[:, :])
                    ins.then_inc(tr_made, 1)
                elif r[0] == "oc":
                    u = r[1]
                    j = job_of[u]
                    pe.wait_ge(pt_out, j + 1)
                    pe.matmul(bank[:, 0:NT * DK], PTs[:, j % 2, 0:P], Vbd[:, units[u][1] // HPG, :], start=True,
                              stop=True).then_inc(tr_made, 1)
                else:
                    pe.wait_ge(of_done, r[1] + 1)
                    for t in range(NT):
                        ins = pe.transpose(bank[:, t * P:(t + 1) * P], OF[:, t, :], ident[:, :])
                    ins.then_inc(tr_made, 1)

            for s in STEPS:
                pieces = list(fill_at[s])
                if s == 0:
                    pe.wait_ge(drained[0], 2)
                if 0 <= s < NU:
                    kind, h, t, m = units[s]
                    i = head_of[s]
                    if s >= 2:
                        pe.wait_ge(exped, s - 1)
                    if s == first_u[i]:
                        pe.wait_ge(tr_drained, max(tr_no(r) for r in prep(i)) + 1)
                    bank = PS[:, B_S + s % 2, :]
                    if kind == "C":
                        if h == 0:
                            pe.wait_ge(tr_drained, tr_no(("kc", 1)) + 1)
                        q = QS[:, 2 * (i % 2), :]
                        g = h // HPG
                        for tt in range(NT):
                            o = bank[:, tt * CP:(tt + 1) * CP]
                            for a in range(2):
                                pe.matmul(o, q[:, tt * P:(tt + 1) * P], KC[:, a, g * CP:(g + 1) * CP], start=a == 0, stop=False)
                            ins = pe.matmul(o, identb[:, :], cmask[:, tt * CP:(tt + 1) * CP], start=False, stop=True)
                    else:
                        if kind == "A":
                            q, kpos = QS[:, 2 * (i % 2) + m, :], 4 * (i % 2) + 2 * m
                        else:
                            q, kpos = QS[:, 2 * (i % 2), :], 4 * ((h // HPG) % 2) + 2 * m
                        W = (t + 1) * P
                        for a in range(2):
                            pe.matmul(bank[:, 0:W], q[:, t * P:(t + 1) * P], KS[:, kpos + a, 0:W], start=a == 0, stop=False)
                        ins = pe.matmul(bank[:, t * P:W], identb[:, :], causal[:, :], start=False, stop=True)
                    ins.then_inc(scores, 1)
                if pieces:
                    fill_piece(*pieces.pop(0))
                u = s - LT
                if u in job_of:
                    j = job_of[u]
                    kind, h, t, m = units[u]
                    if kind == "B":
                        pe.wait_ge(exped, u + 1)
                    else:
                        pe.wait_ge(weighted, weighted_no(u))
                    if j >= 2:
                        pe.wait_ge(pt_out, j - 1)
                    for kb in range(1 if kind == "C" else t + 1):
                        ins = pe.transpose(PS[:, B_PT + j % 2, kb * P:(kb + 1) * P], Pr[:, u % 3, kb * P:(kb + 1) * P], ident[:, :])
                    ins.then_inc(ptd, 1)
                u = s - LV
                if u in job_of and units[u][0] != "C":
                    j = job_of[u]
                    kind, h, t, m = units[u]
                    i = head_of[u]
                    pe.wait_ge(pt_out, j + 1)
                    if i >= 1 and u == first_pv[i]:
                        pe.wait_ge(o_free, i)
                    for kb in range(t + 1):
                        lhs = PTs[:, j % 2, kb * P:(kb + 1) * P]
                        if kind == "A":
                            ins = pe.matmul(PS[:, B_O, t * P:(t + 1) * P], lhs, vA[:, kb, h * P:(h + 1) * P], start=kb == 0, stop=kb == t)
                        else:
                            g = h // HPG
                            o = (m * NT + t) * DK
                            ins = pe.matmul(PS[:, B_O, o:o + DK], lhs, vB[:, kb, (m * G + g) * DK:(m * G + g + 1) * DK],
                                            start=kb == 0, stop=kb == t)
                    ins.then_inc(pv_done, 1)
                for r in trs[s]:
                    transpose_tr(r)
                for piece in pieces:
                    fill_piece(*piece)

            pe.wait_ge(pt_out, len(jobs))

            def merge_weights(pr, r):
                merge_low(pe, pr, r)
                n, kt = (SPLIT_M + r) % NSPL, NF if r % 2 else NK
                return [w[:, n, 0:kt * PC].rearrange("p (k n) -> p k n", k=kt) for w in (w_hi, w_lo)]

            def merge_pair(pr):
                for b in range(3):
                    bank = 4 * (b % 2)
                    if b == 1:
                        pe.wait_ge(tr_drained, NTR)
                        pe.wait_ge(o_free, NHEAD)
                        wait_bank_read(pe, NFILL - 2)
                        wait_bank_read(pe, NFILL - 1)
                    wait_at(pe, sg_done, pr * 3 + (b // 2 + 1))
                    feature_major(merge_weights(pr, 2 * b), bank, H_hi, H_lo)
                    if b:
                        pe.wait_ge(u_lo, 2 * NF)
                    wait_at(pe, sg_used, pr * 3 + (b // 2 + 1))
                    feature_major(merge_weights(pr, 2 * b + 1), bank + 2, o_hi[b * NF:(b + 1) * NF], o_lo[b * NF:(b + 1) * NF])

            with pe.Fori(0, NP) as pr:
                merge_pair(pr)
            for cc in range(2):
                pe.wait_ge(sg_used, 3 * NP + cc)
                token_major(f"wo{cc}", WO_BANK[cc], MH, ML, lambda half, t, k: pe.wait_ge(m_lo, (half + 1) * NP // 2 + 1))


_INS = ['x', 'norm_g', 'w_in', 'a_q_g', 'a_k_g', 'a_lam', 'a_subln_g', 'b_q_g', 'b_k_g', 'b_cmp_pos',
        'b_phi_w1', 'b_phi_w2', 'c_w', 'c_scale', 'w_branch', 'w_out']


def kernel(**inputs):
    import numpy as _np
    import concourse.bacc as _bacc
    from concourse import mybir as _mybir
    from concourse.bass_utils import run_bass_kernel_spmd as _run

    nc = _bacc.Bacc("TRN2", target_bir_lowering=False, num_devices=1)
    arrays, args = {}, []
    for name in _INS:
        a = _np.ascontiguousarray(inputs[name])
        arrays[f"in_{name}_dram"] = a
        args.append(nc.dram_tensor(f"in_{name}_dram", a.shape, _mybir.dt.from_np(a.dtype), kind="ExternalInput").ap())
    shape = arrays["in_x_dram"].shape
    args.append(nc.dram_tensor("out_0_dram", shape, _mybir.dt.float32, kind="ExternalOutput").ap())
    hybrid_trunk_kernel(nc, *args)
    r = _run(nc, [arrays], core_ids=[0])
    return r.results[0]["out_0_dram"]
```
